# Optimizing a Trainium2 kernel written in Bass

```python
import math
import jax, jax.numpy as jnp
from jax import lax
import numpy as np

D_MODEL = 1024
BATCH = 1
SEQ = 512
DEPTH = 2

RET_HEADS = 4
RET_DK = D_MODEL // RET_HEADS
RET_DV = 2 * RET_DK
RET_CHUNK = 128
RET_THETA = 10000.0
ATT_GROUPS = ((128, 1), (512, 4), (2048, 16))
ATT_HEADS_PER_GROUP = 4
ATT_HEADS = ATT_HEADS_PER_GROUP * len(ATT_GROUPS)
ATT_DH = 128
ATT_ROT_DIM = ATT_DH // 4
ATT_THETA = 500000.0
D_FF = ((8 * D_MODEL // 3 + 255) // 256) * 256
NORM_EPS = 1e-6

SPLIT_SIZES = (
    RET_HEADS * RET_DK,
    RET_HEADS * RET_DK,
    RET_HEADS * RET_DV,
    RET_HEADS * RET_DV,
    ATT_HEADS * ATT_DH,
    ATT_HEADS * ATT_DH,
    ATT_HEADS * ATT_DH,
    D_MODEL,
    D_MODEL,
)
D_IN = sum(SPLIT_SIZES)

kernel_name = "hybrid_retention_dilated_attn_block"

def rmsnorm(x, g):
    xf = x.astype(jnp.float32)
    y = xf * lax.rsqrt(jnp.mean(xf * xf, axis=-1, keepdims=True) + NORM_EPS)
    return (y * g.astype(jnp.float32)).astype(x.dtype)

def rotary(x, rot_dim, theta):
    s = x.shape[1]
    half = rot_dim // 2
    inv = theta ** (-jnp.arange(half, dtype=jnp.float32) / half)
    ang = jnp.arange(s, dtype=jnp.float32)[:, None] * inv[None, :]
    cos = jnp.cos(ang)[None, :, None, :]
    sin = jnp.sin(ang)[None, :, None, :]
    xr = x[..., :rot_dim].astype(jnp.float32)
    x1, x2 = xr[..., :half], xr[..., half:]
    rot = jnp.concatenate([x1 * cos - x2 * sin, x1 * sin + x2 * cos], axis=-1)
    return jnp.concatenate([rot.astype(x.dtype), x[..., rot_dim:]], axis=-1)

def retention_chunkwise(q, k, v):
    b, s, h, dk = q.shape
    dv = v.shape[-1]
    c = RET_CHUNK
    n = s // c
    lg = jnp.log(1.0 - 2.0 ** (-5.0 - jnp.arange(h, dtype=jnp.float32)))
    pos = jnp.arange(c, dtype=jnp.float32)
    rel = pos[:, None] - pos[None, :]
    dmask = jnp.where(rel[None] >= 0,
                      jnp.exp(jnp.maximum(rel, 0.0)[None] * lg[:, None, None]), 0.0)
    xi = jnp.exp((pos + 1.0)[None, :] * lg[:, None])
    zeta = jnp.exp((c - 1.0 - pos)[None, :] * lg[:, None])
    chunk_decay = jnp.exp(c * lg)[None, :, None, None]

    def chunks(t):
        return t.astype(jnp.float32).reshape(b, n, c, h, t.shape[-1]).transpose(0, 1, 3, 2, 4)

    qc, kc, vc = chunks(q), chunks(k), chunks(v)
    scores = jnp.einsum('bnhcd,bnhmd->bnhcm', qc, kc) * dmask[None, None]
    intra = jnp.einsum('bnhcm,bnhme->bnhce', scores, vc)

    def step(r, xs):
        qn, kn, vn = xs
        out = jnp.einsum('bhcd,bhde->bhce', qn * xi[None, :, :, None], r)
        r = chunk_decay * r + jnp.einsum('bhcd,bhce->bhde', kn * zeta[None, :, :, None], vn)
        return r, out

    r0 = jnp.zeros((b, h, dk, dv), jnp.float32)
    _, cross = lax.scan(step, r0, (qc.transpose(1, 0, 2, 3, 4),
                                   kc.transpose(1, 0, 2, 3, 4),
                                   vc.transpose(1, 0, 2, 3, 4)))
    y = intra + cross.transpose(1, 0, 2, 3, 4)
    return y.transpose(0, 1, 3, 2, 4).reshape(b, s, h, dv)

def dilated_window_attention(q, k, v, window, dilation):
    b, s, h, dh = q.shape
    r = dilation
    nblk = window // dilation
    unit = r * nblk
    s_pad = -(-s // unit) * unit
    pad = ((0, 0), (0, s_pad - s), (0, 0), (0, 0))
    L = s_pad // r
    nb = L // nblk

    def to_blocks(t):
        t = jnp.pad(t, pad).reshape(b, L, r, h, dh).transpose(0, 2, 3, 1, 4)
        return t.reshape(b, r, h, nb, nblk, dh)

    qb, kb, vb = to_blocks(q), to_blocks(k), to_blocks(v)
    prev = lambda t: jnp.pad(t, ((0, 0), (0, 0), (0, 0), (1, 0), (0, 0), (0, 0)))[:, :, :, :-1]
    kcat = jnp.concatenate([prev(kb), kb], axis=4)
    vcat = jnp.concatenate([prev(vb), vb], axis=4)
    scale = 1.0 / math.sqrt(dh)
    scores = jnp.einsum('brhncd,brhnmd->brhncm', qb, kcat).astype(jnp.float32) * scale
    ci = jnp.arange(nblk)[:, None]
    mi = jnp.arange(2 * nblk)[None, :]
    dist = ci + nblk - mi
    valid = (dist >= 0) & (dist <= nblk)
    first = (jnp.arange(nb) == 0)[:, None, None] & (mi < nblk)[None]
    valid = valid[None] & ~first
    scores = jnp.where(valid, scores, -1e30)
    lse = jax.nn.logsumexp(scores, axis=-1)
    p = jnp.exp(scores - lse[..., None])
    out = jnp.einsum('brhncm,brhnmd->brhncd', p, vcat.astype(jnp.float32))
    out = out.reshape(b, r, h, L, dh).transpose(0, 3, 1, 2, 4).reshape(b, s_pad, h, dh)[:, :s]
    lse = lse.reshape(b, r, h, L).transpose(0, 3, 1, 2).reshape(b, s_pad, h)[:, :s]
    return out, lse

def hybrid_mixer(h, w_in, w_ret_out, w_att_out, w_o):
    b, s, _ = h.shape
    proj = h @ w_in
    idx = list(np.cumsum(SPLIT_SIZES)[:-1])
    rq, rk, rv, rg, aq, ak, av, gr, ga = jnp.split(proj, idx, axis=-1)

    rq = rotary(rq.reshape(b, s, RET_HEADS, RET_DK), RET_DK, RET_THETA)
    rk = rotary(rk.reshape(b, s, RET_HEADS, RET_DK), RET_DK, RET_THETA) * (RET_DK ** -0.5)
    rv = rv.reshape(b, s, RET_HEADS, RET_DV)
    yr = retention_chunkwise(rq, rk, rv)
    mu = jnp.mean(yr, axis=-1, keepdims=True)
    var = jnp.mean(jnp.square(yr - mu), axis=-1, keepdims=True)
    yr = ((yr - mu) * lax.rsqrt(var + NORM_EPS)).reshape(b, s, RET_HEADS * RET_DV)
    y_ret = (jax.nn.silu(rg.astype(jnp.float32)) * yr).astype(h.dtype) @ w_ret_out

    aq = rotary(aq.reshape(b, s, ATT_HEADS, ATT_DH), ATT_ROT_DIM, ATT_THETA)
    ak = rotary(ak.reshape(b, s, ATT_HEADS, ATT_DH), ATT_ROT_DIM, ATT_THETA)
    av = av.reshape(b, s, ATT_HEADS, ATT_DH)
    outs, lses = [], []
    for gi, (window, dilation) in enumerate(ATT_GROUPS):
        sl = slice(gi * ATT_HEADS_PER_GROUP, (gi + 1) * ATT_HEADS_PER_GROUP)
        o, l = dilated_window_attention(aq[:, :, sl], ak[:, :, sl], av[:, :, sl], window, dilation)
        outs.append(o)
        lses.append(l)
    wts = jax.nn.softmax(jnp.stack(lses, axis=0), axis=0)
    ya = jnp.sum(wts[..., None] * jnp.stack(outs, axis=0), axis=0)
    y_att = ya.reshape(b, s, ATT_HEADS_PER_GROUP * ATT_DH).astype(h.dtype) @ w_att_out

    merged = jax.nn.sigmoid(gr) * y_ret + jax.nn.sigmoid(ga) * y_att
    return merged @ w_o

def swiglu(h, w_gate, w_up, w_down):
    return (jax.nn.silu(h @ w_gate) * (h @ w_up)) @ w_down

def setup_inputs(seed: int = 0) -> dict:
    key = jax.random.key(seed)
    ks = jax.random.split(key, 12)
    f32 = jnp.float32

    def w(k, fan_in, fan_out):
        return jax.random.normal(k, (DEPTH, fan_in, fan_out), f32) * (fan_in ** -0.5)

    def gain(k):
        return 1.0 + 0.05 * jax.random.normal(k, (DEPTH, D_MODEL), f32)

    return {
        "x": jax.random.normal(ks[0], (BATCH, SEQ, D_MODEL), f32),
        "w_in": w(ks[1], D_MODEL, D_IN),
        "w_ret_out": w(ks[2], RET_HEADS * RET_DV, D_MODEL),
        "w_att_out": w(ks[3], ATT_HEADS_PER_GROUP * ATT_DH, D_MODEL),
        "w_o": w(ks[4], D_MODEL, D_MODEL),
        "w_ffn_gate": w(ks[5], D_MODEL, D_FF),
        "w_ffn_up": w(ks[6], D_MODEL, D_FF),
        "w_ffn_down": w(ks[7], D_FF, D_MODEL),
        "g_pre_mix": gain(ks[8]),
        "g_post_mix": gain(ks[9]),
        "g_pre_ffn": gain(ks[10]),
        "g_post_ffn": gain(ks[11]),
    }

def reference(x, w_in, w_ret_out, w_att_out, w_o, w_ffn_gate, w_ffn_up, w_ffn_down,
              g_pre_mix, g_post_mix, g_pre_ffn, g_post_ffn):
    for l in range(DEPTH):
        h = rmsnorm(x, g_pre_mix[l])
        m = hybrid_mixer(h, w_in[l], w_ret_out[l], w_att_out[l], w_o[l])
        x = x + rmsnorm(m, g_post_mix[l])
        h = rmsnorm(x, g_pre_ffn[l])
        f = swiglu(h, w_ffn_gate[l], w_ffn_up[l], w_ffn_down[l])
        x = x + rmsnorm(f, g_post_ffn[l])
    return x


_drawn_inputs = setup_inputs


def setup_inputs(seed=0):
    import zlib

    import numpy as np

    out = dict(_drawn_inputs(seed))
    spreads = {}
    factors = {}
    for name, (base, spread) in spreads.items():
        noise = np.random.default_rng([zlib.crc32(name.encode()), seed]).standard_normal(out[name].shape)
        drawn = base * np.exp(spread * noise) if base else spread * noise
        out[name] = __import__('jax').numpy.asarray(drawn.astype(out[name].dtype))
    for name, factor in factors.items():
        out[name] = (out[name] * factor).astype(out[name].dtype)
    return out
```

```python
from contextlib import ExitStack

import numpy as np

import concourse.bass as bass
from concourse import mybir

F32 = mybir.dt.float32
F32R = mybir.dt.float32r
ALU = mybir.AluOpType
ACT = mybir.ActivationFunctionType
AX_X = mybir.AxisListType.X

P = 128
D = 1024
SEQ = 512
DEPTH = 2
KT = D // P
TT = SEQ // P
RH = 4
AG = 3
AI = 4
DFF = 2816
PAIRS = DFF // (2 * P)
EPS = 1e-6
NEG = -1e30
ATT_SCALE = 1.0 / float(np.sqrt(128.0))
RQ, RK, RV, RG, AQ, AK, AV, GR, GA = 0, 1024, 2048, 4096, 6144, 7680, 9216, 10752, 11776
D_IN = 12800
SLOTS = 2
SLOT = 2048


class Steps:

    def __init__(self, plan):
        self.base, self.per, self.index, at = {}, {}, {}, 1
        for phase, times, labels in plan:
            self.base[phase], self.per[phase] = at, len(labels)
            self.index[phase] = {name: n for n, name in enumerate(labels)}
            assert len(self.index[phase]) == len(labels)
            at += times * len(labels)
        self.layer = at - 1

    def start(self, phase, l, i=0):
        return l * self.layer + (self.base[phase] + i * self.per[phase])

    def of(self, phase, name, l, i=0):
        return l * self.layer + (i * self.per[phase] + (self.base[phase] + self.index[phase][name] + 1))


PHASES = [("pre_mix", 1), ("ret_first", 1), ("ret", RH - 1), ("ret_last", 1), ("att", AI),
          ("merge", 2), ("w_o", 1), ("post_mix", 1), ("pre_ffn", 1), ("ffn_first", 1),
          ("ffn", PAIRS // 2 - 1), ("ffn_end", 1), ("ffn_last", 1), ("post_ffn", 1)]
TIMES = dict(PHASES)

FULL, HALF = (2048, 2), (1024, 1)
UNITS = {
    "pre_mix": [],
    "ret_first": [FULL] * 6,
    "ret": [FULL] * 8,
    "ret_last": [FULL] * 2,
    "att": [FULL] * 3 + [(1152, 3), (1152, 3), (768, 3)] + [HALF] * 2,
    "merge": [FULL, HALF] * 2,
    "w_o": [FULL] * 4,
    "post_mix": [], "pre_ffn": [],
    "ffn_first": [FULL] * 2,
    "ffn": ([FULL] * 2 + [HALF] * 2) * 2,
    "ffn_end": ([FULL] * 2 + [HALF] * 2) * 2,
    "ffn_last": [HALF] * 2,
    "post_ffn": [],
}
AHEAD = {"pre_mix": 2048, "ret_first": 2048, "ret": 2048, "ret_last": 2048, "att": 2048, "merge": 2048,
         "post_mix": 0, "w_o": 2048, "pre_ffn": 0, "ffn_first": 2048, "ffn": 2048, "ffn_end": 1024,
         "ffn_last": 0, "post_ffn": 0}


class Units:

    def __init__(self):
        self.base, self.dmas, at, dmas = {}, {}, 0, [0, 0]
        for phase, times in PHASES:
            assert len(UNITS[phase]) % SLOTS == 0
            self.base[phase] = at
            self.dmas[phase] = list(dmas)
            at += times * len(UNITS[phase])
            for s in range(SLOTS):
                dmas[s] += times * sum(n for _, n in UNITS[phase][s::SLOTS])
        self.layer, self.layer_dmas = at, dmas

    def number(self, phase, c, l, i=0):
        return l * self.layer + (i * len(UNITS[phase]) + (self.base[phase] + c))

    def landed(self, phase, c, l, i=0):
        s = c % SLOTS
        per = sum(n for _, n in UNITS[phase][s::SLOTS])
        upto = sum(n for _, n in UNITS[phase][s:c + 1:SLOTS])
        return l * (16 * self.layer_dmas[s]) + (i * (16 * per) + 16 * (self.dmas[phase][s] + upto))


def plans():
    r4, r8 = range(4), range(8)
    rstd = ["v", "rc", "n0", "n1", "n2"]

    def head(prev, cur):
        pe = [("q", 0), ("q", 1)] * cur + [("t", e) for e in r4] * prev + [("k", 0), ("k", 1)] * cur
        pe += [("w", f) for f in r8] * prev
        pe += ([("v", t) for t in r4] + [("s", j) for j in r4] + [("g", e) for e in r4]
               + [("y", t) for t in r4]) * cur
        act = ["rt"] * prev + [("qh", 0), ("qh", 1)] * cur + [("zh", e) for e in r4] * prev
        act += ([("kh", 0), ("kh", 1)] + [("vh", t) for t in r4] + [("ph", j) for j in r4]
                + [("sg", e) for e in r4]) * cur
        rot = lambda x: [(x, n) for n in range(6)] + [(x + "l", 0), (x + "l", 1)]
        dve = (rstd + [("yn", t) for t in r4]) * prev + rot("q") * cur
        dve += [(z, e) for e in r4 for z in ("zm", "zl")] * prev
        dve += rot("k") * cur + [("wa", f) for f in r8] * prev
        dve += ([("vl", t) for t in r4] + [(z, j) for j in r4 for z in ("pm", "pl")]
                + [(z, t) for t in r4 for z in ("st", "ag")]) * cur
        return pe, act, dve

    att_pe = [("x", n) for n in range(6)] + [("v", t) for t in r4]
    att_pe += [("s", 0), ("g", 0), ("t", 0)]
    for c in range(1, 4):
        att_pe += [("s", c), ("p", c - 1), ("t", c)]
    att_pe += [("g", 1), ("p", 3)]
    att_act = [(z, n) for n in range(6) for z in ("xc", "xh")] + [("vh", t) for t in r4]
    att_act += [("ex", 0), ("sg", 0)]
    att_act += [(z, b) for z, b in [(("th", 0), 0)]]
    for c in range(1, 4):
        att_act += [("ex", c)] + [(("th", c), b) for b in range(banks_of(c))]
    att_act += [("sg", 1), "yh"]
    att_dve = [(z, n) for n in range(6) for z in ("xm", "xs", "xp", "xa", "xl")] + [("vl", t) for t in r4]
    soft = lambda c: [(("m", c), g) for g in range(3)] + [("mx", c), ]
    norm = lambda c: [("rc", c), ("pn", c)]
    att_dve += soft(0) + norm(0) + [("gm", 0)]
    att_dve += [(("tl", 0), 0)]
    for c in range(1, 4):
        att_dve += soft(c) + norm(c) + [(("tl", c), b) for b in range(banks_of(c))]
    att_dve += [("gm", 1), "yl"]

    mrg_pe = [(z, p, k) for p in range(2) for z in ("a", "w") for k in range(2)]
    mrg_act = [(z, p, k) for p in range(2) for z in ("sg", "mh") for k in range(2)]
    mrg_dve = [(z, p, k) for p in range(2) for k in range(2) for z in ("yg", "ym", "ml")]

    pre = ([("x", k) for k in r8], [("sq", t) for t in r4] + ["rt"] + [("hh", k) for k in r8],
           rstd + [("h", t) for t in r4] + [("hl", k) for k in r8] + ["clear"])
    post = ([], [("sq", t) for t in r4] + ["rt"], rstd + [(z, t) for t in r4 for z in ("pg", "xa")])
    down = [("d", n, t) for n in range(2) for t in r4]

    def ffn(bodies, up=True):
        pe, act, dve = [], [], []
        for b in range(bodies):
            if up:
                pe += [(z, k, b) for z in ("g", "u") for k in range(2)]
                act += [(z, k, b) for k in range(2) for z in ("si", "ah")]
                dve += [(z, k, b) for k in range(2) for z in ("am", "al")]
            pe += [d + (b,) for d in down]
            dve += [d + (b,) for d in down]
        return pe, act, dve

    one = ffn(1)
    first = ([x for x in one[0] if x[0] != "d"], one[1], [x for x in one[2] if x[0] != "d"])
    lists = {
        "pre_mix": (pre[0], pre[1], ["gains"] + pre[2]),
        "ret_first": head(0, 1), "ret": head(1, 1), "ret_last": head(1, 0),
        "att": (att_pe, att_act, att_dve), "merge": (mrg_pe, mrg_act, mrg_dve),
        "w_o": ([("o", n, t) for n in range(2) for t in r4], [("o", n, t) for n in range(2) for t in r4], []),
        "post_mix": post, "pre_ffn": pre,
        "ffn_first": first, "ffn": ffn(2), "ffn_end": ffn(2), "ffn_last": ffn(1, up=False),
        "post_ffn": post,
    }
    lists["ret_first"] = (with_ends(lists["ret_first"][0]),) + lists["ret_first"][1:]
    lists["ret"] = (with_ends(lists["ret"][0]),) + lists["ret"][1:]
    pe = list(lists["att"][0])
    at = pe.index(("v", 0))
    pe[at:at] = [("end", 3), ("end", 4)]
    lists["att"] = (pe,) + lists["att"][1:]
    pe = list(lists["w_o"][0])
    pe.insert(pe.index(("o", 0, 0)), ("end", 0))
    pe.insert(pe.index(("o", 1, 0)), ("end", 2))
    lists["w_o"] = (pe,) + lists["w_o"][1:]
    return [[(p, n, lists[p][e]) for p, n in PHASES] for e in range(3)]


def with_ends(labels):
    labels = list(labels)
    labels.insert(labels.index(("v", 0)), ("end", "v"))
    return labels


def blocks_of(c):
    return ([(0, m) for m in range(max(0, c - 1), c + 1)] + [(1, m) for m in range(c + 1)]
            + [(2, m) for m in range(c + 1)])


def banks_of(c):
    return -(-len(blocks_of(c)) // 4)


UNIT_END = {
    "ret_first": [("q", 1), ("k", 1), ("end", "v"), ("v", 3), ("g", 1), ("g", 3)],
    "ret": [("q", 1), ("k", 1), ("w", 3), ("w", 7), ("end", "v"), ("v", 3), ("g", 1), ("g", 3)],
    "ret_last": [("w", 3), ("w", 7)],
    "att": [("x", 1), ("x", 3), ("x", 5), ("end", 3), ("end", 4), ("v", 3), ("g", 0), ("g", 1)],
    "merge": [("a", 0, 1), ("w", 0, 1), ("a", 1, 1), ("w", 1, 1)],
    "w_o": [("end", 0), ("o", 0, 3), ("end", 2), ("o", 1, 3)],
    "ffn_first": [("g", 1, 0), ("u", 1, 0)],
    "ffn": [x for b in range(2) for x in (("g", 1, b), ("u", 1, b), ("d", 0, 3, b), ("d", 1, 3, b))],
    "ffn_last": [("d", 0, 3, 0), ("d", 1, 3, 0)],
}
UNIT_END["ffn_end"] = UNIT_END["ffn"]


def build(nc, x, w_in, w_ret, w_att, w_o, w_gate, w_up, w_down, gains, g_post_mix, g_post_ffn,
          ident_in, ret_trig, att_cos, att_sin, att_masks, decays, out):
    plan_pe, plan_act, plan_dve = plans()
    PE, AC, DV, UN = Steps(plan_pe), Steps(plan_act), Steps(plan_dve), Units()

    with ExitStack() as ctx:
        def sb(name, shape, dt=F32):
            return ctx.enter_context(nc.sbuf_tensor(name, shape, dt))

        def sem(name):
            return ctx.enter_context(nc.semaphore(name))

        raw = [sb(f"raw{s}", [P, SLOT]) for s in range(SLOTS)]
        whi = [sb(f"whi{s}", [P, SLOT], F32R) for s in range(SLOTS)]
        wlo = [sb(f"wlo{s}", [P, SLOT], F32R) for s in range(SLOTS)]
        hhi = sb("hhi", [P, KT, SEQ], F32R)
        hlo = sb("hlo", [P, KT, SEQ], F32R)
        acc = sb("acc", [P, TT * D])
        acc_t = acc[:, :].rearrange("p (t n) -> p t n", t=TT)
        acc_f = acc[:, :].rearrange("p (f n) -> p f n", f=8)
        R = sb("split_operands", [P, 15872], F32R)
        F = sb("scratch", [P, 6144])

        def region(buf, at, *shape):
            n = int(np.prod(shape))
            v = buf[:, at:at + n]
            return v.rearrange("p (a b) -> p a b", a=shape[0]) if len(shape) == 2 else v

        rqh, rql, rkh, rkl = (region(R, n * 1024, 2, SEQ) for n in range(4))
        rvh, rvl = region(R, 4096, 4, SEQ), region(R, 6144, 4, SEQ)
        rph, rpl = region(R, 8192, 1280), region(R, 9472, 1280)
        aqh, aql, akh, akl = (region(R, n * 1536, 3, SEQ) for n in range(4))
        avh, avl = region(R, 6144, 4, 384), region(R, 7680, 4, 384)
        pth, ptl = region(R, 9216, 1280), region(R, 10496, 1280)
        yah, yal = region(R, 11776, 4, SEQ), region(R, 13824, 4, SEQ)
        mgh, mgl = region(R, 0, 8, SEQ), region(R, 4096, 8, SEQ)
        ffh, ffl = region(R, 0, 4, SEQ), region(R, 2048, 4, SEQ)

        rows = region(F, 0, 4, D)
        junk = region(F, 4096, 2, D)
        yn = region(F, 0, 4, SEQ)
        sgr = region(F, 2048, 4, SEQ)
        scr = region(F, 4096, 4, SEQ)
        prob = region(F, 0, 2, 1280)
        shuf = region(F, 2560, 2, SEQ)
        sga = region(F, 3584, 1, SEQ)

        ident = sb("ident", [P, P])
        trig = sb("trig", [P, 2, SEQ])
        acos = sb("acos", [P, SEQ])
        asin = sb("asin", [32, SEQ])
        masks = sb("masks", [P, 1280])
        decay = sb("decay", [P, SEQ])
        gall = sb("gall", [P, DEPTH * 16])
        gcur = sb("gcur", [P, 16])
        gpost = sb("gpost", [P, D])
        ss, vv, sq, rs, aa = (sb(n, [P, 4]) for n in ("sum_sq", "var", "root", "rstd", "newton"))
        bst = sb("bst", [P, 4, 6])
        bag = sb("bag", [P, 4, 2])
        rmax = sb("rmax", [P, 2, 3])
        nmax = sb("nmax", [P, 2])
        den = sb("den", [P, 2])
        rden = sb("rden", [P, 2])

        banks = [ctx.enter_context(nc.psum_tensor(f"bank{b}", [P, 512], F32)) for b in range(8)]
        lo4, hi4 = banks[:4], banks[4:]
        xs = nc.dram_tensor("x_between", (SEQ, D), F32, kind="Internal").ap()

        landed = [sem(f"unit_landed{s}") for s in range(SLOTS)]
        hi_ready = sem("unit_hi_ready")
        lo_ready = sem("unit_lo_ready")
        mm_done = sem("mm_done")
        act_done = sem("act_done")
        dve_done = sem("dve_done")
        const_landed = sem("const_landed")
        decay_landed = sem("decay_landed")
        gpost_landed = sem("gpost_landed")
        ve_waited = sem("ve_waited")
        x_landed = sem("x_landed")
        rows_landed = sem("rows_landed")
        x_saved = sem("x_saved")
        out_saved = sem("out_saved")

        x_rows = lambda a: a.rearrange("(t p) n -> p t n", p=P)
        win = w_in.rearrange("l (k p) n -> p (l k) n", p=P)
        wret = w_ret.rearrange("l (k p) n -> p (l k) n", p=P)
        watt = w_att.rearrange("l (k p) n -> p (l k) n", p=P)
        wout = w_o.rearrange("l (k p) n -> p (l k) n", p=P)
        wgate = w_gate.rearrange("l (k p) n -> p (l k) n", p=P)
        wup = w_up.rearrange("l (k p) n -> p (l k) n", p=P)
        wdown = w_down.rearrange("l (k p) n -> p (l k) n", p=P)

        block = ctx.enter_context(nc.Block())

        def bodies(eng, l, body):
            for phase, times in PHASES:
                if times == 1:
                    body(phase, l, 0)
                else:
                    with eng.Fori(0, times) as i:
                        body(phase, l, i)

        @block.sync
        def _(sp):
            sp.dma_start(acc_t, x_rows(x)).then_inc(x_landed, 16)
            sp.dma_start(xs, x).then_inc(x_saved, 16)
            for dst, src in ((ident[:, :], ident_in), (trig[:, :, :], ret_trig), (acos[:, :], att_cos),
                             (asin[:, :], att_sin), (masks[:, :], att_masks), (gall[:, :], gains)):
                sp.dma_start(dst, src).then_inc(const_landed, 16)
            sp.dma_start(decay[:, :], decays[0]).then_inc(decay_landed, 16)

            def unit(phase, c, l, i, parts):
                assert len(parts) == UNITS[phase][c][1]
                sp.wait_ge(lo_ready, UN.number(phase, c, l, i) + 1)
                for at, k, n, src in parts:
                    dst = raw[c % SLOTS][:, at:at + k * n].rearrange("p (k n) -> p k n", k=k)
                    sp.dma_start(dst, src).then_inc(landed[c % SLOTS], 16)

            def cols(w, l, col, n=256):
                if n == 128:
                    return [(0, 8, n, w[:, bass.ds(l * 8, 8), bass.ds(col, n)])]
                return [(h * 4 * n, 4, n, w[:, bass.ds(l * 8 + h * 4, 4), bass.ds(col, n)]) for h in range(2)]

            def rows4(w, k0, col):
                return [(h * 1024, 2, 512, w[:, bass.ds(k0 + 2 * h, 2), col:col + 512]) for h in range(2)]

            def v_rows(l, k0, col):
                return [(h * 1024, 2, 512, win[:, bass.ds(l * 8 + k0 + 2 * h, 2), bass.ds(col, 512)])
                        for h in range(2)]

            def body(phase, l, i):
                if phase in ("ret_first", "ret", "ret_last"):
                    h = {"ret_first": 0, "ret": i + 1, "ret_last": RH}[phase]
                    c = 0
                    if phase != "ret_last":
                        unit(phase, 0, l, i, cols(win, l, h * 256 + RQ))
                        unit(phase, 1, l, i, cols(win, l, h * 256 + RK))
                        c = 2
                    if phase != "ret_first":
                        for n in range(2):
                            unit(phase, c + n, l, i, rows4(wret, l * 16 + (h * 4 - 4), 512 * n))
                        c += 2
                    if phase != "ret_last":
                        for n in range(2):
                            unit(phase, c + n, l, i, v_rows(l, 4 * n, h * 512 + RV))
                        for n in range(2):
                            unit(phase, c + 2 + n, l, i, cols(win, l, h * 512 + (RG + 256 * n)))
                elif phase == "att":
                    tiles = [AQ + g * 512 for g in range(AG)] + [AK + g * 512 for g in range(AG)]
                    for u in range(3):
                        unit(phase, u, l, i, [(n * 1024, 8, 128, win[:, bass.ds(l * 8, 8),
                                               bass.ds(i * 128 + tiles[2 * u + n], 128)]) for n in range(2)])
                    for u, (k0, k) in enumerate(((0, 3), (3, 3), (6, 2))):
                        unit(phase, 3 + u, l, i, [(g * k * 128, k, 128, win[:, bass.ds(l * 8 + k0, k),
                             bass.ds(i * 128 + (AV + g * 512), 128)]) for g in range(AG)])
                    for n in range(2):
                        unit(phase, 6 + n, l, i, cols(win, l, i * 256 + (GR + 128 * n), 128))
                elif phase == "merge":
                    for p in range(2):
                        unit(phase, 2 * p, l, i, cols(win, l, i * 512 + (GA + 256 * p)))
                        unit(phase, 2 * p + 1, l, i,
                             [(0, 4, 256, watt[:, bass.ds(l * 4, 4), bass.ds(i * 512 + 256 * p, 256)])])
                elif phase == "w_o":
                    for n in range(2):
                        for k in range(2):
                            unit(phase, 2 * n + k, l, i, rows4(wout, l * 8 + 4 * k, 512 * n))
                elif phase.startswith("ffn"):
                    pairs = {"ffn_first": [0], "ffn": [i * 2 + 1, i * 2 + 2], "ffn_end": [PAIRS - 2, PAIRS - 1],
                             "ffn_last": [PAIRS]}[phase]
                    c = 0
                    for j in pairs:
                        if phase != "ffn_last":
                            unit(phase, c, l, i, cols(wgate, l, j * 256))
                            unit(phase, c + 1, l, i, cols(wup, l, j * 256))
                            c += 2
                        if phase != "ffn_first":
                            for n in range(2):
                                unit(phase, c + n, l, i, [(0, 2, 512, wdown[:, bass.ds(l * (DFF // P) + (j * 2 - 2), 2),
                                                                          512 * n:512 * n + 512])])
                            c += 2

            with sp.Fori(0, DEPTH) as l:
                bodies(sp, l, body)
            sp.wait_ge(dve_done, DV.start("pre_mix", DEPTH))
            sp.dma_start(x_rows(out), acc_t).then_inc(out_saved, 16)
            sp.wait_ge(out_saved, 16)
            sp.wait_ge(x_saved, 16 * (1 + 2 * DEPTH))
            sp.wait_ge(rows_landed, 16 * 2 * DEPTH)
            sp.wait_ge(gpost_landed, 16 * 2 * DEPTH)
            sp.wait_ge(decay_landed, 16 * (1 + RH * DEPTH))

        @block.gpsimd
        def _(pool):
            pool.sem_inc(lo_ready, 2)

            def body(phase, l, i):
                for c, (size, _) in enumerate(UNITS[phase]):
                    s = c % SLOTS
                    pool.wait_ge(hi_ready, UN.number(phase, c, l, i) + 1)
                    pool.tensor_tensor(wlo[s][:, 0:size], raw[s][:, 0:size], whi[s][:, 0:size].bitcast(F32),
                                       ALU.subtract).then_inc(lo_ready, 1)

            with pool.Fori(0, DEPTH) as l:
                bodies(pool, l, body)

        @block.tensor
        def _(pe):
            def mm3(o, lh, ll, rh, rl, start, stop):
                pe.matmul(o, lh, rh, start=start, stop=False)
                pe.matmul(o, lh, rl, start=False, stop=False)
                return pe.matmul(o, ll, rh, start=False, stop=stop)

            def use(phase, c, l, i):
                pe.wait_ge(lo_ready, UN.number(phase, c, l, i) + 3)

            def dve(phase, name, l, i=0):
                pe.wait_ge(dve_done, DV.of(phase, name, l, i))

            def act(phase, name, l, i=0):
                pe.wait_ge(act_done, AC.of(phase, name, l, i))

            def features(o, c, tile, width=256):
                h = whi[c % SLOTS][:, 0:8 * width].rearrange("p (k n) -> p k n", k=8)
                w = wlo[c % SLOTS][:, 0:8 * width].rearrange("p (k n) -> p k n", k=8)
                at = slice(tile * 128, tile * 128 + 128)
                for k in range(KT):
                    mm = mm3(o, h[:, k, at], w[:, k, at], hhi[:, k, :], hlo[:, k, :], k == 0, k == KT - 1)
                return mm

            def rows_of(o, c, k0, kn, width, t, lh, ll, ktotal):
                h = whi[c % SLOTS][:, 0:kn * width].rearrange("p (k n) -> p k n", k=kn)
                w = wlo[c % SLOTS][:, 0:kn * width].rearrange("p (k n) -> p k n", k=kn)
                at = slice(t * 128, t * 128 + 128)
                for k in range(kn):
                    kk = k0 + k
                    mm = mm3(o, lh[:, kk, at], ll[:, kk, at], h[:, k, :], w[:, k, :], kk == 0, kk == ktotal - 1)
                return mm

            def pre(phase, l, i):
                if phase == "pre_ffn":
                    act("w_o", ("o", 1, 3), l)
                for t in range(TT):
                    dve(phase, ("h", t), l)
                    for k in range(KT):
                        mm = pe.transpose(banks[k][:, t * 128:(t + 1) * 128], rows[:, t, k * 128:(k + 1) * 128],
                                          ident[:, :])
                        if t == TT - 1:
                            mm.then_inc(mm_done, 1)

            def ret(phase, l, i):
                cur, prev = phase != "ret_last", phase != "ret_first"
                back = (lambda e, name: e.of("ret", name, l, i - 1)) if phase == "ret" else \
                       (lambda e, name: e.of("ret", name, l, RH - 2))
                c = 0
                if cur:
                    use(phase, c, l, i)
                    if phase == "ret_first":
                        dve("pre_mix", ("hl", 7), l)
                    else:
                        pe.wait_ge(act_done, back(AC, ("sg", 3)))
                    for n in range(2):
                        features(hi4[n][:, :], c, n).then_inc(mm_done, 1)
                    c += 1
                if prev:
                    dve(phase, ("yn", 3), l, i)
                    for e in range(4):
                        for t in range(TT):
                            mm = pe.transpose(lo4[e][:, t * 128:(t + 1) * 128], yn[:, t, e * 128:(e + 1) * 128],
                                              ident[:, :])
                        mm.then_inc(mm_done, 1)
                if cur:
                    use(phase, c, l, i)
                    for n in range(2):
                        features(hi4[2 + n][:, :], c, n).then_inc(mm_done, 1)
                    c += 1
                if prev:
                    dve(phase, ("zl", 3), l, i)
                    for half in range(2):
                        use(phase, c, l, i)
                        h = whi[c % SLOTS][:, :].rearrange("p (k n) -> p k n", k=4)
                        w = wlo[c % SLOTS][:, :].rearrange("p (k n) -> p k n", k=4)
                        for f in range(4):
                            if half:
                                dve(phase, ("wa", f), l, i)
                            at = slice(f * 128, f * 128 + 128)
                            for k in range(4):
                                mm = mm3(lo4[f][:, :], h[:, k, at], w[:, k, at], rvh[:, k, :], rvl[:, k, :],
                                         k == 0, k == 3)
                            mm.then_inc(mm_done, 1)
                        c += 1
                if not cur:
                    return
                dve(phase, ("kl", 1), l, i)
                for half in range(2):
                    use(phase, c, l, i)
                    for t in range(TT):
                        mm = rows_of(hi4[t][:, :], c, 4 * half, 4, 512, t, hhi, hlo, KT)
                        if half or t == TT - 1:
                            mm.then_inc(mm_done, 1)
                    c += 1
                if prev:
                    dve(phase, ("wa", 7), l, i)
                for j in range(TT):
                    n = SEQ - j * 128
                    for d in range(2):
                        mm = mm3(lo4[j][:, 0:n], rkh[:, d, j * 128:(j + 1) * 128], rkl[:, d, j * 128:(j + 1) * 128],
                                 rqh[:, d, j * 128:SEQ], rql[:, d, j * 128:SEQ], d == 0, d == 1)
                    mm.then_inc(mm_done, 1)
                for half in range(2):
                    use(phase, c, l, i)
                    for n in range(2):
                        dve(phase, ("vl", 2 * half + n), l, i)
                        features(hi4[2 * half + n][:, :], c, n).then_inc(mm_done, 1)
                    c += 1
                dve(phase, ("pl", 3), l, i)
                for t in range(TT):
                    for j in range(t + 1):
                        at = sum(SEQ - 128 * a for a in range(j)) + (t - j) * 128
                        mm = mm3(lo4[t][:, :], rph[:, at:at + 128], rpl[:, at:at + 128], rvh[:, j, :], rvl[:, j, :],
                                 j == 0, j == t)
                    mm.then_inc(mm_done, 1)

            def att(phase, l, i):
                xbank = [lo4[0], lo4[1], lo4[2], lo4[3], hi4[0], hi4[1]]
                for u in range(3):
                    use(phase, u, l, i)
                    for n in range(2):
                        b = 2 * u + n
                        if b == 0:
                            dve("ret_last", ("wa", 7), l)
                        if b == 3:
                            pe.wait_ge(dve_done, DV.start(phase, l, i))
                        tile_features(xbank[b], u, n).then_inc(mm_done, 1)
                for u, (k0, k) in enumerate(((0, 3), (3, 3), (6, 2))):
                    use(phase, 3 + u, l, i)
                    s = (3 + u) % SLOTS
                    h = whi[s][:, 0:k * 384].rearrange("p (g k n) -> p k g n", g=3, k=k)
                    w = wlo[s][:, 0:k * 384].rearrange("p (g k n) -> p k g n", g=3, k=k)
                    for t in range(TT):
                        if u == 0:
                            dve(phase, ("xl", t), l, i)
                        at = slice(t * 128, t * 128 + 128)
                        for kk in range(k):
                            mm = mm3(lo4[t][:, 0:384].rearrange("p (g n) -> p g n", g=3),
                                     hhi[:, k0 + kk, at], hlo[:, k0 + kk, at], h[:, kk], w[:, kk],
                                     k0 + kk == 0, k0 + kk == KT - 1)
                        if u == 2 or t == TT - 1:
                            mm.then_inc(mm_done, 1)

                def scores(c):
                    dve(phase, ("xl", 5) if c == 0 else (("m", c - 1), 2), l, i)
                    at = slice(c * 128, c * 128 + 128)
                    for g in range(AG):
                        m0 = max(0, c - 1) if g == 0 else 0
                        keys = slice(m0 * 128, c * 128 + 128)
                        mm = mm3(hi4[g][:, 0:(c + 1 - m0) * 128], aqh[:, g, at], aql[:, g, at],
                                 akh[:, g, keys], akl[:, g, keys], True, True)
                    mm.then_inc(mm_done, 1)

                def gate(n):
                    use(phase, 6 + n, l, i)
                    if n:
                        act(phase, ("sg", 0), l, i)
                    else:
                        pe.wait_ge(act_done, AC.start(phase, l, i))
                    features(hi4[3][:, :], 6 + n, 0, 128).then_inc(mm_done, 1)

                def transposes(c):
                    dve(phase, ("pn", c), l, i)
                    if c == 0:
                        dve(phase, ("vl", 3), l, i)
                    else:
                        dve(phase, (("tl", c - 1), banks_of(c - 1) - 1), l, i)
                    for n in range(len(blocks_of(c))):
                        mm = pe.transpose(lo4[n // 4][:, (n % 4) * 128:(n % 4) * 128 + 128],
                                          prob[:, c % 2, n * 128:n * 128 + 128], ident[:, :])
                    mm.then_inc(mm_done, 1)

                def products(c):
                    dve(phase, (("tl", c), banks_of(c) - 1), l, i)
                    blocks = blocks_of(c)
                    for n, (g, m) in enumerate(blocks):
                        mm = mm3(lo4[3][:, c * 128:(c + 1) * 128], avh[:, m, g * 128:(g + 1) * 128],
                                 avl[:, m, g * 128:(g + 1) * 128], pth[:, n * 128:(n + 1) * 128],
                                 ptl[:, n * 128:(n + 1) * 128], n == 0, n == len(blocks) - 1)
                    mm.then_inc(mm_done, 1)

                scores(0)
                gate(0)
                transposes(0)
                for c in range(1, TT):
                    scores(c)
                    products(c - 1)
                    transposes(c)
                gate(1)
                products(3)

            def tile_features(o, u, n):
                h = whi[u % SLOTS][:, n * 1024:(n + 1) * 1024].rearrange("p (k n) -> p k n", k=8)
                w = wlo[u % SLOTS][:, n * 1024:(n + 1) * 1024].rearrange("p (k n) -> p k n", k=8)
                for k in range(KT):
                    mm = mm3(o[:, :], h[:, k, :], w[:, k, :], hhi[:, k, :], hlo[:, k, :], k == 0, k == KT - 1)
                return mm

            def merge(phase, l, i):
                for p in range(2):
                    side = (lo4, hi4)[p]
                    use(phase, 2 * p, l, i)
                    dve(phase, ("ml", p, 1), l, i - 1)
                    for k in range(2):
                        features(side[k][:, :], 2 * p, k).then_inc(mm_done, 1)
                    use(phase, 2 * p + 1, l, i)
                    s = (2 * p + 1) % SLOTS
                    h = whi[s][:, 0:1024].rearrange("p (k n) -> p k n", k=4)
                    w = wlo[s][:, 0:1024].rearrange("p (k n) -> p k n", k=4)
                    dve("att", "yl", l, AI - 1)
                    for k in range(2):
                        at = slice(k * 128, k * 128 + 128)
                        for kk in range(4):
                            mm = mm3(side[2 + k][:, :], h[:, kk, at], w[:, kk, at], yah[:, kk, :], yal[:, kk, :],
                                     kk == 0, kk == 3)
                        mm.then_inc(mm_done, 1)

            def project(phase, l, i):
                for n in range(2):
                    for half in range(2):
                        c = 2 * n + half
                        use(phase, c, l, i)
                        if half == 0:
                            dve("merge", ("ml", 1, 1), l, 1)
                        for t in range(TT):
                            mm = rows_of((lo4, hi4)[n][t][:, :], c, 4 * half, 4, 512, t, mgh, mgl, KT)
                            if half or t == TT - 1:
                                mm.then_inc(mm_done, 1)

            def ffn(phase, l, i):
                c = 0
                for b in range({"ffn_first": 1, "ffn": 2, "ffn_end": 2, "ffn_last": 1}[phase]):
                    if phase != "ffn_last":
                        for z in range(2):
                            use(phase, c, l, i)
                            for k in range(2):
                                if z == 0 and k == 0:
                                    if phase == "ffn_first":
                                        dve("pre_ffn", ("hl", 7), l)
                                    elif b == 0:
                                        pe.wait_ge(dve_done, DV.start(phase, l, i))
                                    else:
                                        dve(phase, ("al", 1, 0), l, i)
                                features(hi4[2 * z + k][:, :], c, k).then_inc(mm_done, 1)
                            c += 1
                    if phase != "ffn_first":
                        par = {"ffn": b, "ffn_end": b, "ffn_last": 0}[phase]
                        for n in range(2):
                            use(phase, c, l, i)
                            if n == 0:
                                wait_pair(phase, b, l, i)
                            for t in range(TT):
                                if n:
                                    dve(phase, ("d", 0, t, b), l, i)
                                h = whi[c % SLOTS][:, 0:1024].rearrange("p (k n) -> p k n", k=2)
                                w = wlo[c % SLOTS][:, 0:1024].rearrange("p (k n) -> p k n", k=2)
                                at = slice(t * 128, t * 128 + 128)
                                for k in range(2):
                                    mm = mm3(lo4[t][:, :], ffh[:, 2 * par + k, at], ffl[:, 2 * par + k, at],
                                             h[:, k, :], w[:, k, :], k == 0, k == 1)
                                mm.then_inc(mm_done, 1)
                            c += 1

            def wait_pair(phase, b, l, i):
                if b == 1:
                    dve(phase, ("d", 1, 3, 0), l, i)
                else:
                    pe.wait_ge(dve_done, DV.start(phase, l, i))

            def body(phase, l, i):
                if phase in ("pre_mix", "pre_ffn"):
                    pre(phase, l, i)
                elif phase.startswith("ret"):
                    ret(phase, l, i)
                elif phase == "att":
                    att(phase, l, i)
                elif phase == "merge":
                    merge(phase, l, i)
                elif phase == "w_o":
                    project(phase, l, i)
                elif phase.startswith("ffn"):
                    ffn(phase, l, i)

            pe.sem_inc(mm_done, 1)
            pe.wait_ge(const_landed, 16 * 6)
            with pe.Fori(0, DEPTH) as l:
                bodies(pe, l, body)

        @block.scalar
        def _(sc):
            def round_unit(phase, c, l, i, size=None):
                s = c % SLOTS
                size = size or UNITS[phase][c][0]
                sc.activation(whi[s][:, 0:size], raw[s][:, 0:size], ACT.Copy).then_inc(hi_ready, 1)

            def ready(phase, c, l, i):
                sc.wait_ge(landed[c % SLOTS], UN.landed(phase, c, l, i))
                if c == 1:
                    sc.wait_ge(mm_done, PE.start(phase, l, i))
                else:
                    sc.wait_ge(mm_done, PE.of(phase, UNIT_END[phase][c - 2], l, i))
                round_unit(phase, c, l, i)

            def ahead(phase, l, i):
                size = AHEAD[phase]
                units = UNITS[phase]
                dmas = sum(n for _, n in units[0::2])
                first = {2048: 2, 1024: 1}[size]
                base = UN.landed(phase, len(units) - 2, l, i)
                sc.wait_ge(landed[0], base + 16 * first)
                sc.wait_ge(mm_done, PE.of(phase, UNIT_END[phase][len(units) - 2], l, i))
                round_unit(phase, 0, l, i, size)

            def step(ins):
                ins.then_inc(act_done, 1)

            def pe(phase, name, l, i=0):
                sc.wait_ge(mm_done, PE.of(phase, name, l, i))

            def dve(phase, name, l, i=0):
                sc.wait_ge(dve_done, DV.of(phase, name, l, i))

            def own(phase, name, l, i=0):
                sc.wait_ge(act_done, AC.of(phase, name, l, i))

            def squares(phase, l, scale, before):
                for t in range(TT):
                    before(t)
                    if t >= 2:
                        own(phase, ("sq", t - 2), l)
                    step(sc.activation(junk[:, t % 2, :], acc_t[:, t, :], ACT.Square, scale=scale,
                                       accum_out=ss[:, t:t + 1]))

            def root(phase, l, i=0):
                dve(phase, "v", l, i)
                step(sc.activation(sq[:, :], vv[:, :], ACT.Sqrt))

            def pre(phase, l, i):
                if phase == "pre_mix":
                    sc.wait_ge(landed[0], UN.landed("ret_first", 0, l))
                    sc.wait_ge(mm_done, PE.start("pre_mix", l))
                    round_unit("ret_first", 0, l, 0)
                    sc.wait_ge(x_landed, 16)
                    sc.wait_ge(dve_done, DV.start("pre_mix", l))
                    sc.dma_start(gpost[:, :], g_post_mix[bass.ds(l, 1), :].partition_broadcast(P)).then_inc(gpost_landed, 16)
                    squares(phase, l, 1.0 / 32.0, lambda t: sc.wait_ge(act_done, AC.start("pre_mix", l)) if t == 0 else None)
                else:
                    sc.wait_ge(landed[0], UN.landed("ffn_first", 0, l))
                    sc.wait_ge(mm_done, PE.start("post_mix", l))
                    round_unit("ffn_first", 0, l, 0)

                    def before(t):
                        dve("post_mix", ("xa", t), l)
                        if t < 2:
                            own("post_mix", ("sq", 2 + t), l)
                    squares(phase, l, 1.0 / 32.0, before)
                    dve("post_mix", ("xa", 3), l)
                    sc.dma_start(x_rows(xs), acc_t).then_inc(x_saved, 16)
                    sc.dma_start(gpost[:, :], g_post_ffn[bass.ds(l, 1), :].partition_broadcast(P)).then_inc(gpost_landed, 16)
                root(phase, l)
                g0 = 0 if phase == "pre_mix" else 8
                for k in range(KT):
                    pe(phase, ("x", k), l)
                    step(sc.activation(hhi[:, k, :], banks[k][:, :], ACT.Copy, scale=gcur[:, g0 + k:g0 + k + 1]))

            def post(phase, l, i):
                if phase == "post_mix":
                    own("w_o", ("o", 1, 3), l)
                    before = lambda t: None
                else:
                    before = lambda t: dve("ffn_last", ("d", 1, t, 0), l)
                squares(phase, l, 1.0 / 32.0, before)
                root(phase, l)
                if phase == "post_ffn":
                    dve(phase, ("xa", 3), l)
                    sc.dma_start(x_rows(xs), acc_t).then_inc(x_saved, 16)

            def ret(phase, l, i):
                cur, prev = phase != "ret_last", phase != "ret_first"
                c = 1
                ready(phase, c, l, i)
                if prev:
                    root(phase, l, i)
                if cur:
                    c += 1
                    ready(phase, c, l, i)
                    for n in range(2):
                        dve(phase, ("q", 2 + 3 * n), l, i)
                        step(sc.activation(rqh[:, n, :], scr[:, 2 * n, :], ACT.Copy))
                if prev:
                    for e in range(4):
                        dve(phase, ("zm", e), l, i)
                        step(sc.activation(rvh[:, e, :], scr[:, e, :], ACT.Copy))
                if cur:
                    c += 1
                    ready(phase, c, l, i)
                    for n in range(2):
                        dve(phase, ("k", 2 + 3 * n), l, i)
                        step(sc.activation(rkh[:, n, :], scr[:, 2 * n, :], ACT.Copy))
                if cur and prev:
                    c += 1
                    ready(phase, c, l, i)
                    c += 1
                    ready(phase, c, l, i)
                if not cur:
                    ahead(phase, l, i)
                    return
                n_units = len(UNITS[phase])
                c += 1
                ready(phase, c, l, i)
                assert c == n_units - 2
                for t in range(TT):
                    pe(phase, ("v", t), l, i)
                    step(sc.activation(rvh[:, t, :], hi4[t][:, :], ACT.Copy))
                ready(phase, n_units - 1, l, i)
                at = 0
                for j in range(TT):
                    n = SEQ - j * 128
                    dve(phase, ("pm", j), l, i)
                    step(sc.activation(rph[:, at:at + n], scr[:, j, 0:n], ACT.Copy))
                    at += n
                h = 0 if phase == "ret_first" else i + 1
                sc.dma_start(decay[:, :], decays[bass.ds(h + 1, 1)].rearrange("o p n -> p (o n)")
                             if not isinstance(h, int) else decays[h + 1]).then_inc(decay_landed, 16)
                ahead(phase, l, i)
                for e in range(4):
                    pe(phase, ("g", e), l, i)
                    if e == 0 and prev:
                        dve(phase, ("zl", 3), l, i)
                    step(sc.activation(sgr[:, e, :], hi4[e][:, :], ACT.Silu))

            def att(phase, l, i):
                xbank = [lo4[0], lo4[1], lo4[2], lo4[3], hi4[0], hi4[1]]
                ready(phase, 1, l, i)
                sc.wait_ge(dve_done, DV.start(phase, l, i))
                for n in range(6):
                    if n in (2, 4):
                        ready(phase, 1 + n // 2, l, i)
                    pe(phase, ("x", n), l, i)
                    if n >= 2:
                        dve(phase, ("xs", n - 2), l, i)
                    step(sc.activation(scr[0:32, 2 + n % 2, :], xbank[n][0:32, :], ACT.Copy))
                    dve(phase, ("xa", n), l, i)
                    dst = (aqh if n < 3 else akh)[:, n % 3, :]
                    step(sc.activation(dst, scr[:, n % 2, :], ACT.Copy))
                for c in (4, 5, 6):
                    ready(phase, c, l, i)
                for t in range(TT):
                    pe(phase, ("v", t), l, i)
                    step(sc.activation(avh[:, t, :], lo4[t][:, 0:384], ACT.Copy))
                ready(phase, 7, l, i)

                def exps(c):
                    w = len(blocks_of(c)) * 128
                    dve(phase, ("mx", c), l, i)
                    step(sc.activation(prob[:, c % 2, 0:w], prob[:, c % 2, 0:w], ACT.Exp,
                                       bias=nmax[:, c % 2:c % 2 + 1], accum_out=den[:, c % 2:c % 2 + 1]))

                def key_major(c):
                    w = len(blocks_of(c)) * 128
                    pe(phase, ("t", c), l, i)
                    if c:
                        pe(phase, ("p", c - 1), l, i)
                    for b in range(banks_of(c)):
                        n = min(512, w - 512 * b)
                        step(sc.activation(pth[:, 512 * b:512 * b + n], lo4[b][:, 0:n], ACT.Copy))

                def gate(n):
                    pe(phase, ("g", n), l, i)
                    if n:
                        dve(phase, ("gm", 0), l, i)
                    else:
                        sc.wait_ge(dve_done, DV.start(phase, l, i))
                    step(sc.activation(sga[:, 0, :], hi4[3][:, :], ACT.Sigmoid))

                exps(0)
                gate(0)
                key_major(0)
                for c in range(1, TT):
                    exps(c)
                    key_major(c)
                ahead(phase, l, i)
                gate(1)
                pe(phase, ("p", 3), l, i)
                step(sc.activation(yah[:, bass.ds(i, 1), :].rearrange("p o n -> p (o n)"), lo4[3][:, :], ACT.Copy))

            def merge(phase, l, i):
                for p in range(2):
                    side = (lo4, hi4)[p]
                    for k in range(2):
                        if k == 0:
                            ready(phase, 2 * p + 1, l, i)
                        pe(phase, ("a", p, k), l, i)
                        sc.wait_ge(dve_done, DV.start(phase, l, i))
                        step(sc.activation(scr[:, 2 * p + k, :], side[k][:, :], ACT.Sigmoid))
                    if p == 0:
                        ready(phase, 2, l, i)
                    else:
                        ahead(phase, l, i)
                    for k in range(2):
                        dve(phase, ("ym", p, k), l, i)
                        f = i * 4 + (2 * p + k)
                        tile = acc_f[:, bass.ds(f, 1), :].rearrange("p o n -> p (o n)")
                        step(sc.activation(mgh[:, bass.ds(f, 1), :].rearrange("p o n -> p (o n)"), tile, ACT.Copy))

            def project(phase, l, i):
                sc.wait_ge(x_saved, 16 + l * 32)
                dve("att", "yl", l, AI - 1)
                sc.dma_start(rows, x_rows(xs)).then_inc(rows_landed, 16)
                ready(phase, 1, l, i)
                ready(phase, 2, l, i)
                for t in range(TT):
                    pe(phase, ("o", 0, t), l, i)
                    dve("merge", ("ml", 1, 1), l, 1)
                    step(sc.activation(acc_t[:, t, 0:512], lo4[t][:, :], ACT.Copy))
                ready(phase, 3, l, i)
                for t in range(TT):
                    pe(phase, ("o", 1, t), l, i)
                    step(sc.activation(acc_t[:, t, 512:1024], hi4[t][:, :], ACT.Copy))

            def ffn(phase, l, i):
                c = 1
                if phase == "ffn_last":
                    sc.wait_ge(x_saved, 32 + l * 32)
                    pe("pre_ffn", ("x", 7), l)
                    sc.dma_start(rows, x_rows(xs)).then_inc(rows_landed, 16)
                    ready(phase, 1, l, i)
                    return
                n_units = len(UNITS[phase])
                for b in range({"ffn_first": 1}.get(phase, 2)):
                    ready(phase, c, l, i)
                    c += 1
                    if c < n_units:
                        ready(phase, c, l, i)
                        c += 1
                    else:
                        ahead(phase, l, i)
                    for k in range(2):
                        pe(phase, ("g", k, b), l, i)
                        if b:
                            dve(phase, ("am", k, 0), l, i)
                        else:
                            sc.wait_ge(dve_done, DV.start(phase, l, i))
                        step(sc.activation(scr[:, k, :], hi4[k][:, :], ACT.Silu))
                        dve(phase, ("am", k, b), l, i)
                        par = pair_slot(phase, b)
                        step(sc.activation(ffh[:, 2 * par + k, :], scr[:, 2 + k, :], ACT.Copy))
                    if phase == "ffn_first":
                        break
                    ready(phase, c, l, i)
                    c += 1
                    if b == 0:
                        ready(phase, c, l, i)
                        c += 1
                    else:
                        ahead(phase, l, i)

            def body(phase, l, i):
                if phase in ("pre_mix", "pre_ffn"):
                    pre(phase, l, i)
                elif phase in ("post_mix", "post_ffn"):
                    post(phase, l, i)
                elif phase.startswith("ret"):
                    ret(phase, l, i)
                elif phase == "att":
                    att(phase, l, i)
                elif phase == "merge":
                    merge(phase, l, i)
                elif phase == "w_o":
                    project(phase, l, i)
                else:
                    ffn(phase, l, i)

            sc.sem_inc(act_done, 1)
            sc.wait_ge(const_landed, 16 * 6)
            with sc.Fori(0, DEPTH) as l:
                bodies(sc, l, body)

        @block.vector
        def _(ve):
            def step(ins):
                ins.then_inc(dve_done, 1)

            def pe(phase, name, l, i=0):
                ve.wait_ge(mm_done, PE.of(phase, name, l, i))

            def act(phase, name, l, i=0):
                ve.wait_ge(act_done, AC.of(phase, name, l, i))

            def own(phase, name, l, i=0):
                ve.wait_ge(dve_done, DV.of(phase, name, l, i))

            def rstd(phase, l, i, mean):
                step(ve.tensor_scalar(vv[:, :], mean, EPS, None, ALU.add))
                act(phase, "rt", l, i)
                step(ve.reciprocal(rs[:, :], sq[:, :]))
                own(phase, "rc", l, i)
                step(ve.tensor_tensor(aa[:, :], rs[:, :], rs[:, :], ALU.mult))
                own(phase, "n0", l, i)
                step(ve.scalar_tensor_tensor(out=aa[:, :], in0=aa[:, :], scalar=-0.5, in1=vv[:, :],
                                             op0=ALU.mult, op1=ALU.mult))
                own(phase, "n1", l, i)
                step(ve.scalar_tensor_tensor(out=rs[:, :], in0=aa[:, :], scalar=1.5, in1=rs[:, :],
                                             op0=ALU.add, op1=ALU.mult))
                own(phase, "n2", l, i)

            def pre(phase, l, i):
                if phase == "pre_mix":
                    step(ve.tensor_copy(gcur[:, :], gall[:, bass.ds(l * 16, 16)]))
                act(phase, ("sq", 3), l)
                rstd(phase, l, i, ss[:, :])
                for t in range(TT):
                    step(ve.tensor_scalar(rows[:, t, :], acc_t[:, t, :], rs[:, t:t + 1], None, ALU.mult))
                g0 = 0 if phase == "pre_mix" else 8
                for k in range(KT):
                    act(phase, ("hh", k), l)
                    step(ve.scalar_tensor_tensor(out=hlo[:, k, :], in0=banks[k][:, :], scalar=gcur[:, g0 + k:g0 + k + 1],
                                                 in1=hhi[:, k, :].bitcast(F32), op0=ALU.mult, op1=ALU.subtract))
                ve.wait_ge(x_saved, (16 if phase == "pre_mix" else 32) + l * 32)
                own(phase, ("h", 3), l)
                step(ve.memset(acc[:, :], 0.0))

            def post(phase, l, i):
                act(phase, ("sq", 3), l)
                rstd(phase, l, i, ss[:, :])
                ve.wait_ge(gpost_landed, (16 if phase == "post_mix" else 32) + l * 32)
                ve.wait_ge(rows_landed, (16 if phase == "post_mix" else 32) + l * 32)
                for t in range(TT):
                    step(ve.scalar_tensor_tensor(out=acc_t[:, t, :], in0=acc_t[:, t, :], scalar=rs[:, t:t + 1],
                                                 in1=gpost[:, :], op0=ALU.mult, op1=ALU.mult))
                    own(phase, ("pg", t), l)
                    step(ve.tensor_tensor(acc_t[:, t, :], acc_t[:, t, :], rows[:, t, :], ALU.add))

            def ret(phase, l, i):
                cur, prev = phase != "ret_last", phase != "ret_first"
                back = (lambda e, name: e.of("ret", name, l, i - 1)) if phase == "ret" else \
                       (lambda e, name: e.of("ret", name, l, RH - 2))

                def rotate(x, ba, bb, dh, dl):
                    cos, sin = trig[:, 0, :], trig[:, 1, :]
                    ve.wait_ge(dve_done, DV.start(phase, l, i) if x == "q" else DV.of(phase, ("ql", 1), l, i))
                    if x == "q" and prev:
                        own(phase, ("yn", 3), l, i)
                    if x == "k" and prev:
                        own(phase, ("zl", 3), l, i)
                    pe(phase, (x, 1), l, i)
                    step(ve.tensor_tensor(scr[:, 0, :], ba[:, :], cos, ALU.mult))
                    step(ve.tensor_tensor(scr[:, 1, :], bb[:, :], sin, ALU.mult))
                    own(phase, (x, 1), l, i)
                    step(ve.tensor_tensor(scr[:, 0, :], scr[:, 0, :], scr[:, 1, :], ALU.subtract))
                    step(ve.tensor_tensor(scr[:, 2, :], ba[:, :], sin, ALU.mult))
                    step(ve.tensor_tensor(scr[:, 3, :], bb[:, :], cos, ALU.mult))
                    own(phase, (x, 4), l, i)
                    step(ve.tensor_tensor(scr[:, 2, :], scr[:, 2, :], scr[:, 3, :], ALU.add))
                    for n in range(2):
                        act(phase, (x + "h", n), l, i)
                        own(phase, (x, 2 + 3 * n), l, i)
                        step(ve.tensor_tensor(dl[:, n, :], scr[:, 2 * n, :], dh[:, n, :].bitcast(F32), ALU.subtract))

                if prev:
                    ve.wait_ge(dve_done, DV.start(phase, l, i))
                    rstd(phase, l, i, bag[:, :, 1])
                    for t in range(TT):
                        step(ve.tensor_scalar(yn[:, t, :], lo4[t][:, :], bag[:, t, 0:1], rs[:, t:t + 1],
                                              ALU.subtract, ALU.mult))
                if cur:
                    rotate("q", hi4[0], hi4[1], rqh, rql)
                if prev:
                    own(phase, ("ql", 1) if cur else ("yn", 3), l, i)
                    for e in range(4):
                        pe(phase, ("t", e), l, i)
                        ve.wait_ge(act_done, back(AC, ("sg", e)))
                        step(ve.tensor_tensor(scr[:, e, :], lo4[e][:, :], sgr[:, e, :], ALU.mult))
                        act(phase, ("zh", e), l, i)
                        own(phase, ("zm", e), l, i)
                        step(ve.tensor_tensor(rvl[:, e, :], scr[:, e, :], rvh[:, e, :].bitcast(F32), ALU.subtract))
                if cur:
                    rotate("k", hi4[2], hi4[3], rkh, rkl)
                if prev:
                    ve.wait_ge(dve_done, DV.start(phase, l, i))
                    for f in range(8):
                        pe(phase, ("w", f), l, i)
                        step(ve.tensor_tensor(acc_f[:, f, :], acc_f[:, f, :], lo4[f % 4][:, :], ALU.add))
                if not cur:
                    return
                for t in range(TT):
                    act(phase, ("vh", t), l, i)
                    step(ve.tensor_tensor(rvl[:, t, :], hi4[t][:, :], rvh[:, t, :].bitcast(F32), ALU.subtract))
                at = 0
                h = 0 if phase == "ret_first" else i + 1
                ve.wait_ge(decay_landed, l * (16 * RH) + (h * 16 + 16))
                own(phase, ("kl", 1), l, i)
                for j in range(TT):
                    n = SEQ - j * 128
                    pe(phase, ("s", j), l, i)
                    step(ve.tensor_tensor(scr[:, j, 0:n], lo4[j][:, 0:n], decay[:, 0:n], ALU.mult))
                    act(phase, ("ph", j), l, i)
                    own(phase, ("pm", j), l, i)
                    step(ve.tensor_tensor(rpl[:, at:at + n], scr[:, j, 0:n], rph[:, at:at + n].bitcast(F32), ALU.subtract))
                    at += n
                for t in range(TT):
                    pe(phase, ("y", t), l, i)
                    step(ve.bn_stats(bst[:, t, :], lo4[t][:, :]))
                    own(phase, ("st", t), l, i)
                    ve.sem_inc(ve_waited, 1)
                    step(ve.bn_aggr(bag[:, t, :], bst[:, t, :]))

            def att(phase, l, i):
                xbank = [lo4[0], lo4[1], lo4[2], lo4[3], hi4[0], hi4[1]]
                ve.wait_ge(dve_done, DV.start(phase, l, i))
                for n in range(6):
                    s = n % 2
                    act(phase, ("xc", n), l, i)
                    if n >= 2:
                        own(phase, ("xl", n - 2), l, i)
                    step(ve.tensor_tensor(scr[:, s, :], xbank[n][:, :], acos[:, :], ALU.mult))
                    step(ve.stream_shuffle(shuf[0:32, s, :], scr[0:32, 2 + s, :], [(m + 16) % 32 for m in range(32)]))
                    own(phase, ("xs", n), l, i)
                    step(ve.tensor_tensor(shuf[0:32, s, :], shuf[0:32, s, :], asin[:, :], ALU.mult))
                    own(phase, ("xp", n), l, i)
                    step(ve.tensor_tensor(scr[0:32, s, :], scr[0:32, s, :], shuf[0:32, s, :], ALU.add))
                    act(phase, ("xh", n), l, i)
                    own(phase, ("xa", n), l, i)
                    dh, dl = ((aqh, aql) if n < 3 else (akh, akl))
                    step(ve.tensor_tensor(dl[:, n % 3, :], scr[:, s, :], dh[:, n % 3, :].bitcast(F32), ALU.subtract))
                for t in range(TT):
                    act(phase, ("vh", t), l, i)
                    step(ve.tensor_tensor(avl[:, t, :], lo4[t][:, 0:384], avh[:, t, :].bitcast(F32), ALU.subtract))

                def soft(c):
                    q = c % 2
                    pe(phase, ("s", c), l, i)
                    if c >= 2:
                        pe(phase, ("t", c - 2), l, i)
                    ve.sem_inc(ve_waited, 1)
                    at = 0
                    for g in range(AG):
                        w = (min(c, 1) + 1 if g == 0 else c + 1) * 128
                        off = 256 - w if g == 0 else 256 + 512 * g - w
                        step(ve.tensor_tensor_reduce(prob[:, q, at:at + w], hi4[g][:, 0:w], masks[:, off:off + w],
                                                     ATT_SCALE, -3.0e38, ALU.add, ALU.max, rmax[:, q, g:g + 1]))
                        at += w
                    own(phase, (("m", c), 2), l, i)
                    step(ve.tensor_reduce(nmax[:, q:q + 1], rmax[:, q, :], AX_X, ALU.max, negate=True))
                    act(phase, ("ex", c), l, i)
                    step(ve.reciprocal(rden[:, q:q + 1], den[:, q:q + 1]))
                    own(phase, ("rc", c), l, i)
                    step(ve.tensor_scalar(prob[:, q, 0:at], prob[:, q, 0:at], rden[:, q:q + 1], None, ALU.mult))

                def key_major(c):
                    w = len(blocks_of(c)) * 128
                    for b in range(banks_of(c)):
                        n = min(512, w - 512 * b)
                        act(phase, (("th", c), b), l, i)
                        step(ve.tensor_tensor(ptl[:, 512 * b:512 * b + n], lo4[b][:, 0:n],
                                              pth[:, 512 * b:512 * b + n].bitcast(F32), ALU.subtract))

                def gated(n):
                    act(phase, ("sg", n), l, i)
                    tile = acc_f[:, bass.ds(i * 2 + n, 1), :].rearrange("p o n -> p (o n)")
                    step(ve.tensor_tensor(tile, tile, sga[:, 0, :], ALU.mult))

                soft(0)
                gated(0)
                key_major(0)
                for c in range(1, TT):
                    soft(c)
                    key_major(c)
                gated(1)
                act(phase, "yh", l, i)
                step(ve.tensor_tensor(yal[:, bass.ds(i, 1), :].rearrange("p o n -> p (o n)"), lo4[3][:, :],
                                      yah[:, bass.ds(i, 1), :].rearrange("p o n -> p (o n)").bitcast(F32), ALU.subtract))

            def merge(phase, l, i):
                ve.wait_ge(dve_done, DV.start(phase, l, i))
                for p in range(2):
                    side = (lo4, hi4)[p]
                    for k in range(2):
                        f = i * 4 + (2 * p + k)
                        tile = acc_f[:, bass.ds(f, 1), :].rearrange("p o n -> p (o n)")
                        act(phase, ("sg", p, k), l, i)
                        pe(phase, ("w", p, k), l, i)
                        step(ve.tensor_tensor(scr[:, 2 * p + k, :], scr[:, 2 * p + k, :], side[2 + k][:, :], ALU.mult))
                        own(phase, ("yg", p, k), l, i)
                        step(ve.tensor_tensor(tile, tile, scr[:, 2 * p + k, :], ALU.add))
                        act(phase, ("mh", p, k), l, i)
                        own(phase, ("ym", p, k), l, i)
                        step(ve.tensor_tensor(mgl[:, bass.ds(f, 1), :].rearrange("p o n -> p (o n)"), tile,
                                              mgh[:, bass.ds(f, 1), :].rearrange("p o n -> p (o n)").bitcast(F32),
                                              ALU.subtract))

            def ffn(phase, l, i):
                for b in range({"ffn": 2, "ffn_end": 2}.get(phase, 1)):
                    if phase != "ffn_last":
                        par = pair_slot(phase, b)
                        for k in range(2):
                            act(phase, ("si", k, b), l, i)
                            pe(phase, ("u", k, b), l, i)
                            step(ve.tensor_tensor(scr[:, 2 + k, :], scr[:, k, :], hi4[2 + k][:, :], ALU.mult))
                            act(phase, ("ah", k, b), l, i)
                            own(phase, ("am", k, b), l, i)
                            step(ve.tensor_tensor(ffl[:, 2 * par + k, :], scr[:, 2 + k, :],
                                                  ffh[:, 2 * par + k, :].bitcast(F32), ALU.subtract))
                    if phase != "ffn_first":
                        for n in range(2):
                            for t in range(TT):
                                pe(phase, ("d", n, t, b), l, i)
                                rows_n = acc_t[:, t, n * 512:n * 512 + 512]
                                step(ve.tensor_tensor(rows_n, rows_n, lo4[t][:, :], ALU.add))

            def body(phase, l, i):
                if phase in ("pre_mix", "pre_ffn"):
                    pre(phase, l, i)
                elif phase in ("post_mix", "post_ffn"):
                    post(phase, l, i)
                elif phase.startswith("ret"):
                    ret(phase, l, i)
                elif phase == "att":
                    att(phase, l, i)
                elif phase == "merge":
                    merge(phase, l, i)
                elif phase.startswith("ffn"):
                    ffn(phase, l, i)

            ve.sem_inc(dve_done, 1)
            ve.wait_ge(const_landed, 16 * 6)
            with ve.Fori(0, DEPTH) as l:
                bodies(ve, l, body)


def pair_slot(phase, b):
    return 0 if phase == "ffn_first" else 1 - b


def tables():
    f32 = np.float32
    pos = np.arange(SEQ, dtype=f32)
    half = 128
    inv = (f32(10000.0) ** (-np.arange(half, dtype=f32) / f32(half))).astype(f32)
    ang = (pos[None, :] * inv[:, None]).astype(f32)
    trig = np.stack([np.cos(ang), np.sin(ang)], axis=1).astype(f32)
    half = 16
    inv = (f32(500000.0) ** (-np.arange(half, dtype=f32) / f32(half))).astype(f32)
    ang = (pos[None, :] * inv[:, None]).astype(f32)
    acos = np.ones((P, SEQ), f32)
    acos[0:16] = acos[16:32] = np.cos(ang)
    asin = np.concatenate([-np.sin(ang), np.sin(ang)]).astype(f32)
    q, k = np.arange(P)[:, None], np.arange(P)[None, :]
    parts = [k >= q, k <= q]
    for r in (4, 16):
        same = (q - k) % r == 0
        parts += [same, same, same, same & (k <= q)]
    masks = np.where(np.concatenate(parts, axis=1), 0.0, NEG).astype(f32)
    n, p = np.arange(SEQ)[None, :], np.arange(P)[:, None]
    decays = []
    for h in range(RH):
        lg = np.log(1.0 - 2.0 ** (-5.0 - h))
        decays.append(np.where(n >= p, np.exp(np.maximum(n - p, 0) * lg), 0.0) / 16.0)
    decays.append(decays[0])
    return {"ident": np.eye(P, dtype=f32), "ret_trig": trig, "att_cos": acos, "att_sin": asin,
            "att_masks": masks, "decays": np.stack(decays).astype(f32)}


def kernel(x, w_in, w_ret_out, w_att_out, w_o, w_ffn_gate, w_ffn_up, w_ffn_down,
           g_pre_mix, g_post_mix, g_pre_ffn, g_post_ffn):
    import concourse.bacc as bacc
    from concourse.bass_utils import run_bass_kernel_spmd

    nc = bacc.Bacc("TRN2", target_bir_lowering=False, num_devices=1)
    gains = np.stack([np.asarray(g_pre_mix), np.asarray(g_pre_ffn)], axis=1).reshape(DEPTH, 2, KT, P)
    gains = np.ascontiguousarray(gains.transpose(3, 0, 1, 2).reshape(P, DEPTH * 2 * KT))
    arrays = {"x": np.asarray(x).reshape(SEQ, D), "w_in": w_in, "w_ret": w_ret_out, "w_att": w_att_out, "w_o": w_o,
              "w_gate": w_ffn_gate, "w_up": w_ffn_up, "w_down": w_ffn_down, "gains": gains,
              "g_post_mix": g_post_mix, "g_post_ffn": g_post_ffn}
    t = tables()
    arrays |= {"ident_in": t["ident"], "ret_trig": t["ret_trig"], "att_cos": t["att_cos"], "att_sin": t["att_sin"],
               "att_masks": t["att_masks"], "decays": t["decays"]}
    arrays = {k: np.ascontiguousarray(v) for k, v in arrays.items()}
    args = [nc.dram_tensor(k, v.shape, F32, kind="ExternalInput").ap() for k, v in arrays.items()]
    out = nc.dram_tensor("out", (SEQ, D), F32, kind="ExternalOutput").ap()
    build(nc, *args, out)
    r = run_bass_kernel_spmd(nc, [arrays], core_ids=[0])
    return r.results[0]["out"].reshape(1, SEQ, D)
```

```python
from contextlib import ExitStack

import numpy as np

import concourse.bass as bass
from concourse import mybir

F32 = mybir.dt.float32
F32R = mybir.dt.float32r
ALU = mybir.AluOpType
ACT = mybir.ActivationFunctionType
AX_X = mybir.AxisListType.X

P = 128
D = 1024
SEQ = 512
DEPTH = 2
KT = D // P
TT = SEQ // P
RH = 4
AG = 3
AI = 4
DFF = 2816
PAIRS = DFF // (2 * P)
EPS = 1e-6
NEG = -1e30
ATT_SCALE = 1.0 / float(np.sqrt(128.0))
RQ, RK, RV, RG, AQ, AK, AV, GR, GA = 0, 1024, 2048, 4096, 6144, 7680, 9216, 10752, 11776
D_IN = 12800
SLOTS = 2
SLOT = 2048


class Steps:

    def __init__(self, plan):
        self.base, self.per, self.index, at = {}, {}, {}, 1
        for phase, times, labels in plan:
            self.base[phase], self.per[phase] = at, len(labels)
            self.index[phase] = {name: n for n, name in enumerate(labels)}
            assert len(self.index[phase]) == len(labels)
            at += times * len(labels)
        self.layer = at - 1

    def start(self, phase, l, i=0):
        return l * self.layer + (self.base[phase] + i * self.per[phase])

    def of(self, phase, name, l, i=0):
        return l * self.layer + (i * self.per[phase] + (self.base[phase] + self.index[phase][name] + 1))


PHASES = [("pre_mix", 1), ("ret_first", 1), ("ret", RH - 1), ("ret_last", 1), ("att_first", 1),
          ("att", AI - 1), ("merge", 1), ("w_o", 1), ("post_mix", 1), ("pre_ffn", 1), ("ffn_first", 1),
          ("ffn", PAIRS // 2 - 1), ("ffn_end", 1), ("ffn_last", 1), ("post_ffn", 1)]

FULL, HALF = (2048, 2), (1024, 1)
VALUES = [(1152, 3), (1152, 3), (768, 3)]
UNITS = {
    "pre_mix": [],
    "ret_first": [FULL] * 6,
    "ret": [FULL] * 8,
    "ret_last": [FULL] * 4,
    "att_first": [FULL] + VALUES + [HALF] * 2,
    "att": [FULL] * 3 + VALUES + [HALF] * 2,
    "merge": [FULL] * 6,
    "w_o": [FULL] * 4,
    "post_mix": [], "pre_ffn": [],
    "ffn_first": [FULL] * 2,
    "ffn": [FULL] * 6,
    "ffn_end": [FULL] * 6,
    "ffn_last": [HALF] * 2,
    "post_ffn": [],
}
AHEAD = {"ret_first": FULL, "ret": FULL, "ret_last": FULL, "att_first": FULL, "att": FULL, "merge": FULL,
         "w_o": FULL, "ffn_first": FULL, "ffn": FULL, "ffn_end": HALF}


class Units:

    def __init__(self):
        self.base, self.dmas, at, dmas = {}, {}, 0, [0, 0]
        for phase, times in PHASES:
            assert len(UNITS[phase]) % SLOTS == 0
            self.base[phase] = at
            self.dmas[phase] = list(dmas)
            at += times * len(UNITS[phase])
            for s in range(SLOTS):
                dmas[s] += times * sum(n for _, n in UNITS[phase][s::SLOTS])
        self.layer, self.layer_dmas = at, dmas

    def number(self, phase, c, l, i=0):
        return l * self.layer + (i * len(UNITS[phase]) + (self.base[phase] + c))

    def landed(self, phase, c, l, i=0):
        s = c % SLOTS
        per = sum(n for _, n in UNITS[phase][s::SLOTS])
        upto = sum(n for _, n in UNITS[phase][s:c + 1:SLOTS])
        return l * (16 * self.layer_dmas[s]) + (i * (16 * per) + 16 * (self.dmas[phase][s] + upto))


R4, R8 = range(4), range(8)
RSTD = ("v", "rc", "n0", "n1", "n2")


def rotated(x):
    return [(x, n) for n in range(6)] + [(x + "l", 0), (x + "l", 1)]


def retention_plan(phase):
    out_pe = [("w", f) for f in R8]
    gated_dve = [(z, e) for e in R4 for z in ("zm", "zl")]
    norm_dve = list(RSTD) + [("yn", t) for t in R4]
    scores_dve = [(z, j) for j in R4 for z in ("pm", "pl")] + [(z, t) for t in R4 for z in ("st", "ag")]
    vals = [("end", "v")] + [("v", t) for t in R4] + [("s", j) for j in R4]
    if phase == "ret_first":
        pe = [("q", 0), ("q", 1), ("k", 0), ("k", 1), ("g", 0), ("g", 1)] + vals + [("g", 2), ("g", 3)]
        act = [("qh", 0), ("qh", 1), ("kh", 0), ("kh", 1), ("sg", 0), ("sg", 1)] + [("vh", t) for t in R4]
        act += [("ph", j) for j in R4] + [("sg", 2), ("sg", 3)]
        dve = rotated("q") + rotated("k") + [("vl", t) for t in R4] + scores_dve
        return pe + [("y", t) for t in R4], act, dve
    if phase == "ret":
        pe = [("q", 0), ("q", 1)] + [("t", e) for e in R4] + [("k", 0), ("k", 1)] + out_pe + vals
        pe += [("g", e) for e in R4] + [("y", t) for t in R4]
        act = ["rt"] + [("zh", e) for e in R4] + [("qh", 0), ("qh", 1), ("kh", 0), ("kh", 1)]
        act += [("vh", t) for t in R4] + [("ph", j) for j in R4] + [("sg", e) for e in R4]
        dve = norm_dve + gated_dve + rotated("q") + rotated("k") + [("wa", f) for f in R8]
        return pe, act, dve + [("vl", t) for t in R4] + scores_dve
    pe = [("x", 0), ("x", 1)] + [("t", e) for e in R4] + [("x", 2), ("x", 3)] + out_pe
    act = ["rt"] + [("zh", e) for e in R4] + [(z, n) for n in R4 for z in ("xc", "xh")]
    dve = norm_dve + gated_dve + [(z, n) for n in R4 for z in XSTEPS] + [("wa", f) for f in R8]
    return pe, act, dve


XSTEPS = ("xm", "xs", "xp", "xa", "xl")


def attention_plan(phase):
    ends = [("end", 0), ("end", 1)] + [("v", t) for t in R4]
    pe = [("s", 0), ("t", 0)]
    act = [("ex", 0), (("th", 0), 0)]
    dve = soft_plan(0) + [(("tl", 0), 0)]
    for c in range(1, TT):
        gate = {1: [("g", 0)], 3: [("g", 1)]}.get(c, [])
        pe += [("s", c)] + gate + [("p", c - 1), ("t", c)]
        act += [("ex", c)] + [("sg", n) for _, n in gate] + [(("th", c), b) for b in range(banks_of(c))]
        dve += soft_plan(c) + [("gm", n) for _, n in gate] + [(("tl", c), b) for b in range(banks_of(c))]
    first = 4 if phase == "att_first" else 0
    xs = range(first, 6)
    x_pe, x_act, x_dve = [], [], []
    for n in xs:
        x_pe += [("x", n)]
        x_act += [("xc", n), ("xh", n)]
        x_dve += [(z, n) for z in XSTEPS]
        if n == 1:
            x_pe, x_act, x_dve = x_pe + ["pp"], x_act + ["yh"], x_dve + ["yl"]
    return (x_pe + ends + pe, x_act + [("vh", t) for t in R4] + act, x_dve + [("vl", t) for t in R4] + dve)


def soft_plan(c):
    return [(("m", c), g) for g in range(AG)] + [("mx", c), ("rc", c), ("pn", c)]


def ffn_plan(phase):
    pe, act, dve = [], [], []
    for b in range(2 if phase in ("ffn", "ffn_end") else 1):
        if phase != "ffn_last":
            pe += [(z, k, b) for z in ("g", "u") for k in range(2)]
            act += [(z, k, b) for z in ("si", "ah") for k in range(2)]
            dve += [(z, k, b) for k in range(2) for z in ("am", "al")]
        if phase != "ffn_first":
            pe += [("d", g, b) for g in R8]
            dve += [("d", g, b) for g in R8]
    return pe, act, dve


def plans():
    per_tile = [(z, t) for t in R4 for z in RSTD + ("h",)]
    pre = ([("x", k) for k in R8], [(z, t) for t in R4 for z in ("sq", "rt")] + [("hh", k) for k in R8],
           per_tile + [("hl", k) for k in R8] + ["clear"])
    post_dve = []
    for t in range(TT + 1):
        post_dve += [("v", t)] * (t < TT) + [("pg", t - 1), ("xa", t - 1)] * (t > 0)
        post_dve += [(z, t) for z in RSTD[1:]] * (t < TT)
    sums = [(z, t) for t in R4 for z in ("sq", "rt")]
    merge_pe = [("a", 0), ("a", 1), "pp", ("a", 2), ("a", 3)] + [("w", f) for f in R4]
    merge_pe += [("a", f) for f in range(4, 8)] + [("w", f) for f in range(4, 8)]
    merge_act = [("sg", 0), ("sg", 1), "yh", ("sg", 2), ("sg", 3)] + [("mh", f) for f in R4]
    merge_act += [("sg", f) for f in range(4, 8)] + [("mh", f) for f in range(4, 8)]
    lists = {
        "pre_mix": (pre[0], pre[1], ["gains"] + pre[2]),
        "ret_first": retention_plan("ret_first"), "ret": retention_plan("ret"),
        "ret_last": retention_plan("ret_last"),
        "att_first": attention_plan("att_first"), "att": attention_plan("att"),
        "merge": (merge_pe, merge_act, ["yl"] + [(z, f) for f in R8 for z in ("yg", "ym", "ml")]),
        "w_o": ([("end", 0)] + [("o", 0, t) for t in R4] + [("end", 2)] + [("o", 1, t) for t in R4],
                [("o", 0, t) for t in R4], []),
        "post_mix": ([], [(z, t) for t in R4 for z in ("o", "sq", "rt")], post_dve),
        "pre_ffn": pre,
        "ffn_first": ffn_plan("ffn_first"), "ffn": ffn_plan("ffn"), "ffn_end": ffn_plan("ffn_end"),
        "ffn_last": ffn_plan("ffn_last"),
        "post_ffn": ([], sums, post_dve),
    }
    return [[(p, n, lists[p][e]) for p, n in PHASES] for e in range(3)]


def blocks_of(c):
    return ([(0, m) for m in range(max(0, c - 1), c + 1)] + [(1, m) for m in range(c + 1)]
            + [(2, m) for m in range(c + 1)])


def banks_of(c):
    return -(-len(blocks_of(c)) // 4)


UNIT_END = {
    "ret_first": [("q", 1), ("k", 1), ("g", 1), ("end", "v"), ("v", 3), ("g", 3)],
    "ret": [("q", 1), ("k", 1), ("w", 3), ("w", 7), ("end", "v"), ("v", 3), ("g", 1), ("g", 3)],
    "ret_last": [("x", 1), ("x", 3), ("w", 3), ("w", 7)],
    "att_first": [("x", 5), ("end", 0), ("end", 1), ("v", 3), ("g", 0), ("g", 1)],
    "att": [("x", 1), ("x", 3), ("x", 5), ("end", 0), ("end", 1), ("v", 3), ("g", 0), ("g", 1)],
    "merge": [("a", 1), ("a", 3), ("w", 3), ("a", 5), ("a", 7), ("w", 7)],
    "w_o": [("end", 0), ("o", 0, 3), ("end", 2), ("o", 1, 3)],
    "ffn_first": [("g", 1, 0), ("u", 1, 0)],
    "ffn": [x for b in range(2) for x in (("g", 1, b), ("u", 1, b), ("d", 7, b))],
}
UNIT_END["ffn_end"] = UNIT_END["ffn"]


def build(nc, x, w_in, w_ret, w_att, w_o, w_gate, w_up, w_down, gains, g_post_mix, g_post_ffn,
          ident_in, ret_trig, att_cos, att_sin, att_masks, decays, out):
    plan_pe, plan_act, plan_dve = plans()
    PE, AC, DV, UN = Steps(plan_pe), Steps(plan_act), Steps(plan_dve), Units()

    with ExitStack() as ctx:
        def sb(name, shape, dt=F32):
            return ctx.enter_context(nc.sbuf_tensor(name, shape, dt))

        def sem(name):
            return ctx.enter_context(nc.semaphore(name))

        raw = [sb(f"raw{s}", [P, SLOT]) for s in range(SLOTS)]
        whi = [sb(f"whi{s}", [P, SLOT], F32R) for s in range(SLOTS)]
        wlo = [sb(f"wlo{s}", [P, SLOT], F32R) for s in range(SLOTS)]
        hhi = sb("hhi", [P, KT, SEQ], F32R)
        hlo = sb("hlo", [P, KT, SEQ], F32R)
        acc = sb("acc", [P, TT * D])
        acc_t = acc[:, :].rearrange("p (t n) -> p t n", t=TT)
        acc_f = acc[:, :].rearrange("p (f n) -> p f n", f=8)
        R = sb("split_operands", [P, 15872], F32R)
        F = sb("scratch", [P, 6144])

        def region(buf, at, *shape):
            n = int(np.prod(shape))
            v = buf[:, at:at + n]
            return v.rearrange("p (a b) -> p a b", a=shape[0]) if len(shape) == 2 else v

        rqh, rql, rkh, rkl = (region(R, n * 1024, 2, SEQ) for n in range(4))
        rvh, rvl = region(R, 4096, 4, SEQ), region(R, 6144, 4, SEQ)
        rph, rpl = region(R, 11776, 1280), region(R, 13056, 1280)
        aqh, aql = region(R, 0, 3, SEQ), region(R, 1536, 3, SEQ)
        avh, avl = region(R, 3072, 4, 384), region(R, 4608, 4, 384)
        pth, ptl = region(R, 6144, 1280), region(R, 7424, 1280)
        akh, akl = region(R, 8704, 3, SEQ), region(R, 10240, 3, SEQ)
        yah, yal = region(R, 11776, 4, SEQ), region(R, 13824, 4, SEQ)
        mgh, mgl = region(R, 0, 8, SEQ), region(R, 4096, 8, SEQ)
        ffh, ffl = region(R, 0, 4, SEQ), region(R, 2048, 4, SEQ)

        rows = region(F, 0, 4, D)
        junk = region(F, 4096, 2, D)
        yn = region(F, 0, 4, SEQ)
        sgr = region(F, 2048, 4, SEQ)
        scr = region(F, 4096, 4, SEQ)
        prob = region(F, 0, 2, 1280)
        sga = region(F, 3584, 1, SEQ)

        shuf = sb("shuffled", [32, 2, SEQ])
        ident = sb("ident", [P, P])
        trig = sb("trig", [P, 2, SEQ])
        acos = sb("acos", [P, SEQ])
        asin = sb("asin", [32, SEQ])
        masks = sb("masks", [P, 1280])
        decay = sb("decay", [P, SEQ])
        gall = sb("gall", [P, DEPTH * 16])
        gcur = sb("gcur", [P, 16])
        gpost = sb("gpost", [P, D])
        ss, vv, sq, rs, aa = (sb(n, [P, 4]) for n in ("sum_sq", "var", "root", "rstd", "newton"))
        bst = sb("bst", [P, 4, 6])
        bag = sb("bag", [P, 4, 2])
        rmax = sb("rmax", [P, 2, 3])
        nmax = sb("nmax", [P, 2])
        den = sb("den", [P, 2])
        rden = sb("rden", [P, 2])

        banks = [ctx.enter_context(nc.psum_tensor(f"bank{b}", [P, 512], F32)) for b in range(8)]
        lo4, hi4 = banks[:4], banks[4:]
        xbank = [hi4[0], hi4[1], hi4[2], hi4[3], hi4[0], hi4[1]]
        ffn_banks = lambda phase: lo4[:2] + hi4[2:] if phase == "ffn_first" else hi4
        xs = nc.dram_tensor("x_between", (SEQ, D), F32, kind="Internal").ap()

        landed = [sem(f"unit_landed{s}") for s in range(SLOTS)]
        hi_ready = sem("unit_hi_ready")
        lo_ready = sem("unit_lo_ready")
        mm_done = sem("mm_done")
        act_done = sem("act_done")
        dve_done = sem("dve_done")
        early_landed = sem("early_landed")
        const_landed = sem("const_landed")
        decay_landed = sem("decay_landed")
        gpost_landed = sem("gpost_landed")
        ve_waited = sem("ve_waited")
        x_landed = [sem(f"x_landed{t}") for t in range(TT)]
        rows_landed = sem("rows_landed")
        x_saved = sem("x_saved")
        out_saved = sem("out_saved")

        x_rows = lambda a: a.rearrange("(t p) n -> p t n", p=P)
        win = w_in.rearrange("l (k p) n -> p (l k) n", p=P)
        wret = w_ret.rearrange("l (k p) n -> p (l k) n", p=P)
        watt = w_att.rearrange("l (k p) n -> p (l k) n", p=P)
        wout = w_o.rearrange("l (k p) n -> p (l k) n", p=P)
        wgate = w_gate.rearrange("l (k p) n -> p (l k) n", p=P)
        wup = w_up.rearrange("l (k p) n -> p (l k) n", p=P)
        wdown = w_down.rearrange("l (k p) n -> p (l k) n", p=P)

        block = ctx.enter_context(nc.Block())

        def bodies(eng, l, body):
            for phase, times in PHASES:
                if times == 1:
                    body(phase, l, 0)
                else:
                    with eng.Fori(0, times) as i:
                        body(phase, l, i)

        @block.sync
        def _(sp):
            for t in range(TT):
                sp.dma_start(acc_t[:, t, :], x[t * P:(t + 1) * P, :]).then_inc(x_landed[t], 16)
            for dst, src in ((ident[:, :], ident_in), (gall[:, :], gains)):
                sp.dma_start(dst, src).then_inc(early_landed, 16)

            def unit(phase, c, l, i, parts):
                assert len(parts) == UNITS[phase][c][1]
                sp.wait_ge(lo_ready, UN.number(phase, c, l, i) + 1)
                for at, k, n, src in parts:
                    dst = raw[c % SLOTS][:, at:at + k * n].rearrange("p (k n) -> p k n", k=k)
                    sp.dma_start(dst, src).then_inc(landed[c % SLOTS], 16)

            def cols(w, l, col, n=256):
                if n == 128:
                    return [(0, 8, n, w[:, bass.ds(l * 8, 8), bass.ds(col, n)])]
                return [(h * 4 * n, 4, n, w[:, bass.ds(l * 8 + h * 4, 4), bass.ds(col, n)]) for h in range(2)]

            def rows4(w, k0, col):
                return [(h * 1024, 2, 512, w[:, bass.ds(k0 + 2 * h, 2), bass.ds(col, 512)]) for h in range(2)]

            def two_tiles(l, i, u):
                tiles = [AQ + g * 512 for g in range(AG)] + [AK + g * 512 for g in range(AG)]
                return [(n * 1024, 8, 128, win[:, bass.ds(l * 8, 8), bass.ds(i * 128 + tiles[2 * u + n], 128)])
                        for n in range(2)]

            def body(phase, l, i):
                put = lambda c, parts: unit(phase, c, l, i, parts)
                if phase in ("ret_first", "ret"):
                    h = 0 if phase == "ret_first" else i + 1
                    q, k = cols(win, l, h * 256 + RQ), cols(win, l, h * 256 + RK)
                    v = [rows4(win, l * 8 + 4 * n, h * 512 + RV) for n in range(2)]
                    gate = [cols(win, l, h * 512 + (RG + 256 * n)) for n in range(2)]
                    if phase == "ret_first":
                        order = [q, k, gate[0], v[0], v[1], gate[1]]
                    else:
                        order = [q, k] + [rows4(wret, l * 16 + (h * 4 - 4), 512 * n) for n in range(2)] + v + gate
                    for c, parts in enumerate(order):
                        put(c, parts)
                elif phase == "ret_last":
                    for u in range(2):
                        put(u, two_tiles(l, 0, u))
                    for n in range(2):
                        put(2 + n, rows4(wret, l * 16 + (RH * 4 - 4), 512 * n))
                elif phase in ("att_first", "att"):
                    a = 0 if phase == "att_first" else i + 1
                    c = 0
                    for u in range(2 if phase == "att_first" else 0, 3):
                        put(c, two_tiles(l, a, u))
                        c += 1
                    for k0, k in ((0, 3), (3, 3), (6, 2)):
                        put(c, [(g * k * 128, k, 128, win[:, bass.ds(l * 8 + k0, k), bass.ds(a * 128 + (AV + g * 512), 128)])
                                for g in range(AG)])
                        c += 1
                    for n in range(2):
                        put(c + n, cols(win, l, a * 256 + (GR + 128 * n), 128))
                elif phase == "merge":
                    for n in range(2):
                        put(3 * n, cols(win, l, GA + 512 * n))
                        put(3 * n + 1, cols(win, l, GA + 512 * n + 256))
                        put(3 * n + 2, rows4(watt, l * 4, 512 * n))
                elif phase == "w_o":
                    for n in range(2):
                        for k in range(2):
                            put(2 * n + k, rows4(wout, l * 8 + 4 * k, 512 * n))
                elif phase.startswith("ffn"):
                    pairs = {"ffn_first": [0], "ffn": [i * 2 + 1, i * 2 + 2], "ffn_end": [PAIRS - 2, PAIRS - 1],
                             "ffn_last": []}[phase]
                    c = 0
                    for j in pairs:
                        put(c, cols(wgate, l, j * 256))
                        put(c + 1, cols(wup, l, j * 256))
                        c += 2
                        if phase != "ffn_first":
                            k0 = l * (DFF // P) + (j * 2 - 2)
                            put(c, [(k * 1024, 1, 1024, wdown[:, bass.ds(k0 + k, 1), :]) for k in range(2)])
                            c += 1
                    if phase == "ffn_last":
                        for k in range(2):
                            put(k, [(0, 1, 1024, wdown[:, bass.ds(l * (DFF // P) + (2 * PAIRS - 2 + k), 1), :])])

            for dst, src in ((trig[:, :, :], ret_trig), (acos[:, :], att_cos),
                             (asin[:, :], att_sin), (masks[:, :], att_masks)):
                sp.dma_start(dst, src).then_inc(const_landed, 16)
            sp.dma_start(decay[:, :], decays[0]).then_inc(decay_landed, 16)
            sp.dma_start(xs, x).then_inc(x_saved, 16)
            with sp.Fori(0, DEPTH) as l:
                bodies(sp, l, body)
            sp.wait_ge(dve_done, DV.start("pre_mix", DEPTH))
            sp.dma_start(x_rows(out), acc_t).then_inc(out_saved, 16)
            sp.wait_ge(out_saved, 16)
            sp.wait_ge(x_saved, 16 * (1 + 2 * DEPTH))
            sp.wait_ge(rows_landed, 16 * 2 * DEPTH)
            sp.wait_ge(gpost_landed, 16 * 2 * DEPTH)
            sp.wait_ge(decay_landed, 16 * (1 + RH * DEPTH))

        @block.gpsimd
        def _(pool):
            pool.sem_inc(lo_ready, 2)

            def body(phase, l, i):
                for c, (size, _) in enumerate(UNITS[phase]):
                    s = c % SLOTS
                    pool.wait_ge(hi_ready, UN.number(phase, c, l, i) + 1)
                    pool.tensor_tensor(wlo[s][:, 0:size], raw[s][:, 0:size], whi[s][:, 0:size].bitcast(F32),
                                       ALU.subtract).then_inc(lo_ready, 1)

            with pool.Fori(0, DEPTH) as l:
                bodies(pool, l, body)


        @block.tensor
        def _(pe):
            def mm3(o, lh, ll, rh, rl, start, stop):
                pe.matmul(o, lh, rh, start=start, stop=False)
                pe.matmul(o, lh, rl, start=False, stop=False)
                return pe.matmul(o, ll, rh, start=False, stop=stop)

            def use(phase, c, l, i):
                pe.wait_ge(lo_ready, UN.number(phase, c, l, i) + 3)

            def dve(phase, name, l, i=0):
                pe.wait_ge(dve_done, DV.of(phase, name, l, i))

            def act(phase, name, l, i=0):
                pe.wait_ge(act_done, AC.of(phase, name, l, i))

            def parts_of(c, at, k, n):
                return [w[c % SLOTS][:, at:at + k * n].rearrange("p (k n) -> p k n", k=k) for w in (whi, wlo)]

            def features(o, weights, tile, h_steps=None, ks=range(KT)):
                h, w = weights
                at = slice(tile * 128, tile * 128 + 128)
                for k in ks:
                    if h_steps:
                        dve(h_steps[0], ("hl", k), h_steps[1])
                    mm = mm3(o[:, :], h[:, k, at], w[:, k, at], hhi[:, k, :], hlo[:, k, :], k == 0, k == KT - 1)
                return mm

            def token_rows(o, weights, t, lh, ll, k0, ktotal, cols=slice(0, 512)):
                h, w = weights
                at = slice(t * 128, t * 128 + 128)
                for k in range(h.shape[1]):
                    kk = k0 + k
                    mm = mm3(o[:, :], lh[:, kk, at], ll[:, kk, at], h[:, k, cols], w[:, k, cols],
                             kk == 0, kk == ktotal - 1)
                return mm

            def pre(phase, l, i):
                if phase == "pre_ffn":
                    act("post_mix", ("o", 3), l)
                for t in range(TT):
                    dve(phase, ("h", t), l)
                    for k in range(KT):
                        mm = pe.transpose(banks[k][:, t * 128:(t + 1) * 128], rows[:, t, k * 128:(k + 1) * 128],
                                          ident[:, :])
                        if t == TT - 1:
                            mm.then_inc(mm_done, 1)

            def back_transposes(phase, l, i):
                dve(phase, ("yn", 3), l, i)
                for e in range(4):
                    for t in range(TT):
                        mm = pe.transpose(lo4[e][:, t * 128:(t + 1) * 128], yn[:, t, e * 128:(e + 1) * 128],
                                          ident[:, :])
                    mm.then_inc(mm_done, 1)

            def ret_out(phase, c0, l, i):
                dve(phase, ("zl", 3), l, i)
                for half in range(2):
                    use(phase, c0 + half, l, i)
                    h, w = parts_of(c0 + half, 0, 4, 512)
                    for f in range(4):
                        if half:
                            dve(phase, ("wa", f), l, i)
                        at = slice(f * 128, f * 128 + 128)
                        for k in range(4):
                            mm = mm3(lo4[f][:, :], h[:, k, at], w[:, k, at], rvh[:, k, :], rvl[:, k, :],
                                     k == 0, k == 3)
                        mm.then_inc(mm_done, 1)

            def ret_values(phase, c0, l, i):
                dve(phase, ("kl", 1), l, i)
                for half in range(2):
                    use(phase, c0 + half, l, i)
                    for t in range(TT):
                        mm = token_rows(hi4[t], parts_of(c0 + half, 0, 4, 512), t, hhi, hlo, 4 * half, KT)
                        if half or t == TT - 1:
                            mm.then_inc(mm_done, 1)

            def ret_scores():
                for j in range(TT):
                    n = SEQ - j * 128
                    for d in range(2):
                        mm = mm3(lo4[j][:, 0:n], rkh[:, d, j * 128:(j + 1) * 128], rkl[:, d, j * 128:(j + 1) * 128],
                                 rqh[:, d, j * 128:SEQ], rql[:, d, j * 128:SEQ], d == 0, d == 1)
                    mm.then_inc(mm_done, 1)

            def ret_output(phase, l, i):
                dve(phase, ("pl", 3), l, i)
                for t in range(TT):
                    for j in range(t + 1):
                        at = sum(SEQ - 128 * a for a in range(j)) + (t - j) * 128
                        mm = mm3(lo4[t][:, :], rph[:, at:at + 128], rpl[:, at:at + 128], rvh[:, j, :], rvl[:, j, :],
                                 j == 0, j == t)
                    mm.then_inc(mm_done, 1)

            def ret_first(phase, l, i):
                use(phase, 0, l, i)
                features(lo4[0], parts_of(0, 0, 8, 256), 0, ("pre_mix", l)).then_inc(mm_done, 1)
                features(lo4[1], parts_of(0, 0, 8, 256), 1).then_inc(mm_done, 1)
                use(phase, 1, l, i)
                for n in range(2):
                    features(hi4[2 + n], parts_of(1, 0, 8, 256), n).then_inc(mm_done, 1)
                use(phase, 2, l, i)
                for n in range(2):
                    features(hi4[n], parts_of(2, 0, 8, 256), n).then_inc(mm_done, 1)
                act(phase, ("sg", 1), l)
                ret_values(phase, 3, l, i)
                ret_scores()
                use(phase, 5, l, i)
                dve(phase, ("vl", 3), l)
                for n in range(2):
                    features(hi4[2 + n], parts_of(5, 0, 8, 256), n).then_inc(mm_done, 1)
                ret_output(phase, l, i)

            def ret(phase, l, i):
                use(phase, 0, l, i)
                pe.wait_ge(act_done, AC.start(phase, l, i))
                for n in range(2):
                    features(hi4[n], parts_of(0, 0, 8, 256), n).then_inc(mm_done, 1)
                back_transposes(phase, l, i)
                use(phase, 1, l, i)
                for n in range(2):
                    features(hi4[2 + n], parts_of(1, 0, 8, 256), n).then_inc(mm_done, 1)
                ret_out(phase, 2, l, i)
                ret_values(phase, 4, l, i)
                dve(phase, ("wa", 7), l, i)
                ret_scores()
                for half in range(2):
                    use(phase, 6 + half, l, i)
                    for n in range(2):
                        e = 2 * half + n
                        dve(phase, ("vl", e), l, i)
                        features(hi4[e], parts_of(6 + half, 0, 8, 256), n).then_inc(mm_done, 1)
                ret_output(phase, l, i)

            def qk_tile(c, n):
                return features(xbank[n], parts_of(c, (n % 2) * 1024, 8, 128), 0).then_inc(mm_done, 1)

            def ret_last(phase, l, i):
                use(phase, 0, l, i)
                pe.wait_ge(act_done, AC.start(phase, l))
                for n in range(2):
                    qk_tile(0, n)
                back_transposes(phase, l, i)
                use(phase, 1, l, i)
                for n in range(2, 4):
                    qk_tile(1, n)
                ret_out(phase, 2, l, i)

            def att(phase, l, i):
                first = phase == "att_first"
                for c, u in enumerate(range(2 if first else 0, 3)):
                    use(phase, c, l, i)
                    for n in (2 * u, 2 * u + 1):
                        if n == 0:
                            pe.wait_ge(dve_done, before_start(DV, phase, l, i, (("m", 3), 2)))
                        if n == 3:
                            pe.wait_ge(act_done, before_start(AC, phase, l, i, ("sg", 1)))
                        if n >= 4:
                            dve("ret_last" if first else phase, ("xl", n - 4), l, i)
                        qk_tile(c, n)
                    if u == 0:
                        pe.wait_ge(dve_done, DV.start(phase, l, i))
                        products(3)
                v0 = 1 if first else 3
                if first:
                    dve("ret_last", ("wa", 7), l)
                else:
                    dve(phase, "yl", l, i)
                for u, (k0, k) in enumerate(((0, 3), (3, 3), (6, 2))):
                    use(phase, v0 + u, l, i)
                    s = (v0 + u) % SLOTS
                    h = whi[s][:, 0:k * 384].rearrange("p (g k n) -> p k g n", g=3, k=k)
                    w = wlo[s][:, 0:k * 384].rearrange("p (g k n) -> p k g n", g=3, k=k)
                    for t in range(TT):
                        at = slice(t * 128, t * 128 + 128)
                        for kk in range(k):
                            mm = mm3(lo4[t][:, 0:384].rearrange("p (g n) -> p g n", g=3),
                                     hhi[:, k0 + kk, at], hlo[:, k0 + kk, at], h[:, kk], w[:, kk],
                                     k0 + kk == 0, k0 + kk == KT - 1)
                        if u == 2 or t == TT - 1:
                            mm.then_inc(mm_done, 1)

                def scores(c):
                    dve(phase, ("xl", 5) if c == 0 else (("m", c - 1), 2), l, i)
                    at = slice(c * 128, c * 128 + 128)
                    for g in range(AG):
                        m0 = max(0, c - 1) if g == 0 else 0
                        keys = slice(m0 * 128, c * 128 + 128)
                        mm = mm3(hi4[g][:, 0:(c + 1 - m0) * 128], aqh[:, g, at], aql[:, g, at],
                                 akh[:, g, keys], akl[:, g, keys], True, True)
                    mm.then_inc(mm_done, 1)

                def gate(n, half):
                    unit = v0 + 3 + n
                    if half == 0:
                        use(phase, unit, l, i)
                        if n:
                            act(phase, ("sg", 0), l, i)
                    mm = features(hi4[3], parts_of(unit, 0, 8, 128), 0, ks=range(4 * half, 4 * half + 4))
                    if half:
                        mm.then_inc(mm_done, 1)

                def transposes(c):
                    dve(phase, ("pn", c), l, i)
                    if c == 0:
                        dve(phase, ("vl", 3), l, i)
                    else:
                        dve(phase, (("tl", c - 1), banks_of(c - 1) - 1), l, i)
                    for n in range(len(blocks_of(c))):
                        mm = pe.transpose(lo4[n // 4][:, (n % 4) * 128:(n % 4) * 128 + 128],
                                          prob[:, c % 2, n * 128:n * 128 + 128], ident[:, :])
                    mm.then_inc(mm_done, 1)

                scores(0)
                gate(0, 0)
                transposes(0)
                for c in range(1, TT):
                    scores(c)
                    if c == 2:
                        gate(1, 0)
                    else:
                        gate(c // 2, 1)
                    dve(phase, (("tl", c - 1), banks_of(c - 1) - 1), l, i)
                    products(c - 1)
                    transposes(c)

            def before_start(steps, phase, l, i, name):
                left = steps.per["att"] - steps.index["att"][name] - 1
                assert steps.per["att_first"] - steps.index["att_first"][name] - 1 == left
                return steps.start(phase, l, i) - left

            def products(c):
                blocks = blocks_of(c)
                for n, (g, m) in enumerate(blocks):
                    mm = mm3(lo4[3][:, c * 128:(c + 1) * 128], avh[:, m, g * 128:(g + 1) * 128],
                             avl[:, m, g * 128:(g + 1) * 128], pth[:, n * 128:(n + 1) * 128],
                             ptl[:, n * 128:(n + 1) * 128], n == 0, n == len(blocks) - 1)
                mm.then_inc(mm_done, 1)

            def merge(phase, l, i):
                for p in range(2):
                    for u in range(2):
                        use(phase, 3 * p + u, l, i)
                        for n in range(2):
                            f = 4 * p + 2 * u + n
                            if f == 0:
                                dve("att", (("m", 3), 2), l, AI - 2)
                            if f == 3:
                                act("att", ("sg", 1), l, AI - 2)
                            if f >= 4:
                                act(phase, ("sg", f - 4), l)
                            features(hi4[f % 4], parts_of(3 * p + u, 0, 8, 256), n).then_inc(mm_done, 1)
                        if p == 0 and u == 0:
                            pe.wait_ge(dve_done, DV.start(phase, l))
                            products(3)
                    use(phase, 3 * p + 2, l, i)
                    if p == 0:
                        dve(phase, "yl", l)
                    h, w = parts_of(3 * p + 2, 0, 4, 512)
                    for n in range(4):
                        if p:
                            dve(phase, ("yg", n), l)
                        at = slice(n * 128, n * 128 + 128)
                        for k in range(4):
                            mm = mm3(lo4[n][:, :], h[:, k, at], w[:, k, at], yah[:, k, :], yal[:, k, :], k == 0, k == 3)
                        mm.then_inc(mm_done, 1)

            def project(phase, l, i):
                for n in range(2):
                    for half in range(2):
                        c = 2 * n + half
                        use(phase, c, l, i)
                        if c == 0:
                            act("merge", ("sg", 7), l)
                            dve("merge", ("ml", 3), l)
                        if c == 1:
                            dve("merge", ("ml", 7), l)
                        for t in range(TT):
                            mm = token_rows((hi4, lo4)[n][t], parts_of(c, 0, 4, 512), t, mgh, mgl, 4 * half, KT)
                            if half or t == TT - 1:
                                mm.then_inc(mm_done, 1)

            def ffn(phase, l, i):
                bodies_of = 2 if phase in ("ffn", "ffn_end") else 1
                for b in range(bodies_of):
                    if phase != "ffn_last":
                        for z in range(2):
                            c = 3 * b + z
                            use(phase, c, l, i)
                            if z == 0 and b == 1:
                                dve(phase, ("al", 1, 0), l, i)
                            elif z == 0 and phase == "ffn":
                                dve("ffn_first", ("al", 1, 0), l)
                                dve("ffn", ("al", 1, 1), l, i - 1)
                            elif z == 0 and phase == "ffn_end":
                                dve("ffn", ("al", 1, 1), l, PAIRS // 2 - 2)
                            for k in range(2):
                                steps = ("pre_ffn", l) if phase == "ffn_first" and z == k == 0 else None
                                features(ffn_banks(phase)[2 * z + k], parts_of(c, 0, 8, 256), k, steps).then_inc(mm_done, 1)
                    if phase == "ffn_first":
                        continue
                    if phase == "ffn_last":
                        use(phase, 1, l, i)
                        dve("ffn_end", ("al", 1, 1), l)
                    else:
                        use(phase, 3 * b + 2, l, i)
                    for g in R8:
                        t, cols = g // 2, slice(g % 2 * 512, g % 2 * 512 + 512)
                        if g >= 4:
                            dve(phase, ("d", g - 4, b), l, i)
                        elif b:
                            dve(phase, ("d", g + 4, 0), l, i)
                        else:
                            pe.wait_ge(dve_done, DV.start(phase, l, i) - (3 - g))
                        if phase == "ffn_last":
                            for k in range(2):
                                mm = token_rows(lo4[g % 4], parts_of(k, 0, 1, 1024), t, ffh[:, :, :], ffl[:, :, :], k, 2, cols)
                        else:
                            mm = token_rows(lo4[g % 4], parts_of(3 * b + 2, 0, 2, 1024), t,
                                            ffh[:, 2 * b:2 * b + 2, :], ffl[:, 2 * b:2 * b + 2, :], 0, 2, cols)
                        mm.then_inc(mm_done, 1)

            def body(phase, l, i):
                if phase in ("pre_mix", "pre_ffn"):
                    pre(phase, l, i)
                elif phase == "ret_first":
                    ret_first(phase, l, i)
                elif phase == "ret":
                    ret(phase, l, i)
                elif phase == "ret_last":
                    ret_last(phase, l, i)
                elif phase in ("att_first", "att"):
                    att(phase, l, i)
                elif phase == "merge":
                    merge(phase, l, i)
                elif phase == "w_o":
                    project(phase, l, i)
                elif phase.startswith("ffn"):
                    ffn(phase, l, i)

            pe.sem_inc(mm_done, 1)
            pe.wait_ge(early_landed, 16 * 2)
            with pe.Fori(0, DEPTH) as l:
                bodies(pe, l, body)

        @block.scalar
        def _(sc):
            def round_unit(phase, c, l, i, size=None):
                s = c % SLOTS
                size = size or UNITS[phase][c][0]
                sc.activation(whi[s][:, 0:size], raw[s][:, 0:size], ACT.Copy).then_inc(hi_ready, 1)

            def ready(phase, c, l, i):
                sc.wait_ge(landed[c % SLOTS], UN.landed(phase, c, l, i))
                if c == 1:
                    sc.wait_ge(mm_done, PE.start(phase, l, i))
                else:
                    sc.wait_ge(mm_done, PE.of(phase, UNIT_END[phase][c - 2], l, i))
                round_unit(phase, c, l, i)

            def ahead(phase, l, i):
                size, dmas = AHEAD[phase]
                c = len(UNITS[phase]) - 2
                sc.wait_ge(landed[0], UN.landed(phase, c, l, i) + 16 * dmas)
                sc.wait_ge(mm_done, PE.of(phase, UNIT_END[phase][c], l, i))
                round_unit(phase, 0, l, i, size)

            def step(ins):
                ins.then_inc(act_done, 1)

            def pe(phase, name, l, i=0):
                sc.wait_ge(mm_done, PE.of(phase, name, l, i))

            def dve(phase, name, l, i=0):
                sc.wait_ge(dve_done, DV.of(phase, name, l, i))

            def own(phase, name, l, i=0):
                sc.wait_ge(act_done, AC.of(phase, name, l, i))

            def square(t):
                step(sc.activation(junk[:, t % 2, :], acc_t[:, t, :], ACT.Square, scale=float(D) ** -0.5,
                                   accum_out=ss[:, t:t + 1]))

            def root(phase, l, t):
                dve(phase, ("v", t), l)
                step(sc.activation(sq[:, t:t + 1], vv[:, t:t + 1], ACT.Sqrt))

            def pre(phase, l, i):
                mix = phase == "pre_mix"
                if mix:
                    sc.wait_ge(dve_done, DV.start(phase, l))
                    sc.dma_start(gpost[:, :], g_post_mix[bass.ds(l, 1), :].partition_broadcast(P)).then_inc(gpost_landed, 16)
                for t in range(TT):
                    if mix:
                        sc.wait_ge(x_landed[t], 16)
                    else:
                        dve("post_mix", ("xa", t), l)
                    if t >= 2:
                        own(phase, ("sq", t - 2), l)
                    elif mix:
                        sc.wait_ge(act_done, AC.start(phase, l))
                    else:
                        own("post_mix", ("sq", t + 2), l)
                    square(t)
                    root(phase, l, t)
                    if mix and t < 2:
                        sc.wait_ge(landed[t], UN.landed("ret_first", t, l))
                        sc.wait_ge(mm_done, PE.start(phase, l))
                        round_unit("ret_first", t, l, 0)
                if not mix:
                    sc.dma_start(x_rows(xs), acc_t).then_inc(x_saved, 16)
                    sc.dma_start(gpost[:, :], g_post_ffn[bass.ds(l, 1), :].partition_broadcast(P)).then_inc(gpost_landed, 16)
                    sc.wait_ge(landed[1], UN.landed("ffn_first", 1, l))
                    sc.wait_ge(mm_done, PE.start("post_mix", l))
                    round_unit("ffn_first", 1, l, 0)
                g0 = 0 if mix else 8
                for k in range(KT):
                    pe(phase, ("x", k), l)
                    step(sc.activation(hhi[:, k, :], banks[k][:, :], ACT.Copy, scale=gcur[:, g0 + k:g0 + k + 1]))

            def post(phase, l, i):
                for t in range(TT):
                    if phase == "post_mix":
                        pe("w_o", ("o", 1, t), l)
                        step(sc.activation(acc_t[:, t, 512:1024], lo4[t][:, :], ACT.Copy))
                        own(phase, ("o", t), l)
                    else:
                        dve("ffn_last", ("d", 2 * t + 1, 0), l)
                    if t >= 2:
                        own(phase, ("sq", t - 2), l)
                    else:
                        sc.wait_ge(act_done, AC.start(phase, l))
                    square(t)
                    root(phase, l, t)
                if phase == "post_ffn":
                    dve(phase, ("xa", 3), l)
                    sc.dma_start(x_rows(xs), acc_t).then_inc(x_saved, 16)

            def root_ret(phase, l, i):
                dve(phase, "v", l, i)
                step(sc.activation(sq[:, :], vv[:, :], ACT.Sqrt))

            def gated_hi(phase, l, i):
                for e in range(4):
                    dve(phase, ("zm", e), l, i)
                    step(sc.activation(rvh[:, e, :], scr[:, e, :], ACT.Copy))

            def rotated_hi(phase, x, dst, l, i):
                for n in range(2):
                    dve(phase, (x, 2 + 3 * n), l, i)
                    step(sc.activation(dst[:, n, :], scr[:, 2 * n, :], ACT.Copy))

            def values_hi(phase, l, i):
                for t in range(TT):
                    pe(phase, ("v", t), l, i)
                    step(sc.activation(rvh[:, t, :], hi4[t][:, :], ACT.Copy))

            def scores_hi(phase, l, i):
                at = 0
                for j in range(TT):
                    n = SEQ - j * 128
                    dve(phase, ("pm", j), l, i)
                    step(sc.activation(rph[:, at:at + n], scr[:, j, 0:n], ACT.Copy))
                    at += n
                src = decays[1] if phase == "ret_first" else decays[bass.ds(i + 2, 1)].rearrange("o p n -> p (o n)")
                sc.dma_start(decay[:, :], src).then_inc(decay_landed, 16)

            def silu(phase, e, l, i):
                pe(phase, ("g", e), l, i)
                step(sc.activation(sgr[:, e, :], hi4[e][:, :], ACT.Silu))

            def ret_first(phase, l, i):
                ready(phase, 2, l, i)
                rotated_hi(phase, "q", rqh, l, i)
                ready(phase, 3, l, i)
                rotated_hi(phase, "k", rkh, l, i)
                ready(phase, 4, l, i)
                for e in range(2):
                    silu(phase, e, l, i)
                ready(phase, 5, l, i)
                values_hi(phase, l, i)
                ahead(phase, l, i)
                scores_hi(phase, l, i)
                for e in range(2, 4):
                    silu(phase, e, l, i)

            def ret(phase, l, i):
                ready(phase, 1, l, i)
                root_ret(phase, l, i)
                ready(phase, 2, l, i)
                gated_hi(phase, l, i)
                ready(phase, 3, l, i)
                rotated_hi(phase, "q", rqh, l, i)
                rotated_hi(phase, "k", rkh, l, i)
                for c in (4, 5, 6):
                    ready(phase, c, l, i)
                values_hi(phase, l, i)
                ready(phase, 7, l, i)
                scores_hi(phase, l, i)
                ahead(phase, l, i)
                dve(phase, ("zl", 3), l, i)
                for e in range(4):
                    silu(phase, e, l, i)

            def qk_hi(phase, n, l, i, back):
                pe(phase, ("x", n), l, i)
                back()
                step(sc.activation(scr[0:32, 2 + n % 2, :], xbank[n][0:32, :], ACT.Copy))
                dve(phase, ("xa", n), l, i)
                dst = (aqh if n < 3 else akh)[:, n % 3, :]
                step(sc.activation(dst, scr[:, n % 2, :], ACT.Copy))

            def ret_last(phase, l, i):
                ready(phase, 1, l, i)
                root_ret(phase, l, i)
                ready(phase, 2, l, i)
                gated_hi(phase, l, i)
                for n in range(4):
                    if n == 2:
                        ready(phase, 3, l, i)
                    qk_hi(phase, n, l, i, lambda: dve(phase, ("zl", 3) if n < 2 else ("xs", n - 2), l))
                ahead(phase, l, i)

            def att(phase, l, i):
                first = phase == "att_first"
                at_tile, rest = ({5: 2}, (3, 4)) if first else ({1: 2, 3: 3, 5: 4}, (5, 6))
                ready(phase, 1, l, i)
                for n in range(4 if first else 0, 6):
                    if n in at_tile:
                        ready(phase, at_tile[n], l, i)
                    if n < 2:
                        back = lambda: sc.wait_ge(dve_done, DV.start(phase, l, i))
                    elif first:
                        back = lambda: dve("ret_last", ("xs", n - 2), l)
                    else:
                        back = lambda: dve(phase, ("xs", n - 2), l, i)
                    qk_hi(phase, n, l, i, back)
                    if n == 1:
                        output_hi(phase, bass.ds(i, 1), l, i)
                for c in rest:
                    ready(phase, c, l, i)
                for t in range(TT):
                    pe(phase, ("v", t), l, i)
                    step(sc.activation(avh[:, t, :], lo4[t][:, 0:384], ACT.Copy))
                ready(phase, len(UNITS[phase]) - 1, l, i)

                def exps(c):
                    w = len(blocks_of(c)) * 128
                    dve(phase, ("mx", c), l, i)
                    step(sc.activation(prob[:, c % 2, 0:w], prob[:, c % 2, 0:w], ACT.Exp,
                                       bias=nmax[:, c % 2:c % 2 + 1], accum_out=den[:, c % 2:c % 2 + 1]))

                def key_major(c):
                    w = len(blocks_of(c)) * 128
                    pe(phase, ("t", c), l, i)
                    if c:
                        pe(phase, ("p", c - 1), l, i)
                    for b in range(banks_of(c)):
                        n = min(512, w - 512 * b)
                        step(sc.activation(pth[:, 512 * b:512 * b + n], lo4[b][:, 0:n], ACT.Copy))

                def gate(n):
                    pe(phase, ("g", n), l, i)
                    if n:
                        dve(phase, ("gm", 0), l, i)
                    else:
                        sc.wait_ge(dve_done, DV.start(phase, l, i))
                    step(sc.activation(sga[:, 0, :], hi4[3][:, :], ACT.Sigmoid))

                exps(0)
                key_major(0)
                exps(1)
                gate(0)
                key_major(1)
                ahead(phase, l, i)
                exps(2)
                key_major(2)
                exps(3)
                gate(1)
                key_major(3)

            def output_hi(phase, at, l, i):
                pe(phase, "pp", l, i)
                step(sc.activation(yah[:, at, :].rearrange("p o n -> p (o n)"), lo4[3][:, :], ACT.Copy))

            def merge(phase, l, i):
                def sigmoid(f):
                    pe(phase, ("a", f), l)
                    if f < 4:
                        dve("att", ("xl", 5), l, AI - 2)
                    else:
                        dve(phase, ("ym", f - 4), l)
                    step(sc.activation(scr[:, f % 4, :], hi4[f % 4][:, :], ACT.Sigmoid))

                def merged_hi(f):
                    dve(phase, ("ym", f), l)
                    step(sc.activation(mgh[:, f, :], acc_f[:, f, :], ACT.Copy))

                ready(phase, 1, l, i)
                sc.wait_ge(act_done, AC.start(phase, l))
                sigmoid(0)
                ready(phase, 2, l, i)
                sigmoid(1)
                output_hi(phase, slice(AI - 1, AI), l, i)
                ready(phase, 3, l, i)
                sigmoid(2)
                sigmoid(3)
                for f in range(3):
                    merged_hi(f)
                ready(phase, 4, l, i)
                merged_hi(3)
                sigmoid(4)
                ready(phase, 5, l, i)
                for f in range(5, 8):
                    sigmoid(f)
                ahead(phase, l, i)
                for f in range(4, 8):
                    merged_hi(f)

            def project(phase, l, i):
                sc.wait_ge(x_saved, 16 + l * 32)
                sc.dma_start(rows, x_rows(xs)).then_inc(rows_landed, 16)
                ready(phase, 1, l, i)
                ready(phase, 2, l, i)
                dve("merge", ("ml", 7), l)
                for t in range(TT):
                    pe(phase, ("o", 0, t), l, i)
                    step(sc.activation(acc_t[:, t, 0:512], hi4[t][:, :], ACT.Copy))
                ready(phase, 3, l, i)
                ahead(phase, l, i)

            def ffn(phase, l, i):
                if phase == "ffn_last":
                    sc.wait_ge(x_saved, 32 + l * 32)
                    pe("pre_ffn", ("x", 7), l)
                    sc.dma_start(rows, x_rows(xs)).then_inc(rows_landed, 16)
                    ready(phase, 1, l, i)
                    return
                for b in range(1 if phase == "ffn_first" else 2):
                    if phase != "ffn_first":
                        ready(phase, 3 * b + 1, l, i)
                        ready(phase, 3 * b + 2, l, i)
                    for k in range(2):
                        pe(phase, ("g", k, b), l, i)
                        if b:
                            dve(phase, ("am", k, 0), l, i)
                        else:
                            sc.wait_ge(dve_done, DV.start(phase, l, i))
                        step(sc.activation(scr[:, k, :], ffn_banks(phase)[k][:, :], ACT.Silu))
                    if phase != "ffn_first" and b == 0:
                        ready(phase, 3, l, i)
                    else:
                        ahead(phase, l, i)
                    par = pair_slot(phase, b)
                    for k in range(2):
                        dve(phase, ("am", k, b), l, i)
                        step(sc.activation(ffh[:, 2 * par + k, :], scr[:, 2 + k, :], ACT.Copy))

            def body(phase, l, i):
                if phase in ("pre_mix", "pre_ffn"):
                    pre(phase, l, i)
                elif phase in ("post_mix", "post_ffn"):
                    post(phase, l, i)
                elif phase == "ret_first":
                    ret_first(phase, l, i)
                elif phase == "ret":
                    ret(phase, l, i)
                elif phase == "ret_last":
                    ret_last(phase, l, i)
                elif phase in ("att_first", "att"):
                    att(phase, l, i)
                elif phase == "merge":
                    merge(phase, l, i)
                elif phase == "w_o":
                    project(phase, l, i)
                else:
                    ffn(phase, l, i)

            sc.sem_inc(act_done, 1)
            with sc.Fori(0, DEPTH) as l:
                bodies(sc, l, body)

        @block.vector
        def _(ve):
            def step(ins):
                ins.then_inc(dve_done, 1)

            def pe(phase, name, l, i=0):
                ve.wait_ge(mm_done, PE.of(phase, name, l, i))

            def act(phase, name, l, i=0):
                ve.wait_ge(act_done, AC.of(phase, name, l, i))

            def own(phase, name, l, i=0):
                ve.wait_ge(dve_done, DV.of(phase, name, l, i))

            def reciprocal_root(phase, rooted, name, at, l, i=0):
                v, r, a = vv[:, at], rs[:, at], aa[:, at]
                act(phase, rooted, l, i)
                step(ve.reciprocal(r, sq[:, at]))
                own(phase, name("rc"), l, i)
                step(ve.tensor_tensor(a, r, r, ALU.mult))
                own(phase, name("n0"), l, i)
                step(ve.scalar_tensor_tensor(out=a, in0=a, scalar=-0.5, in1=v, op0=ALU.mult, op1=ALU.mult))
                own(phase, name("n1"), l, i)
                step(ve.scalar_tensor_tensor(out=r, in0=a, scalar=1.5, in1=r, op0=ALU.add, op1=ALU.mult))

            def mean_square(phase, t, l):
                act(phase, ("sq", t), l)
                step(ve.tensor_scalar(vv[:, t:t + 1], ss[:, t:t + 1], EPS, None, ALU.add))

            def tile_root(phase, t, l):
                reciprocal_root(phase, ("rt", t), lambda z: (z, t), slice(t, t + 1), l)

            def pre(phase, l, i):
                mix = phase == "pre_mix"
                if mix:
                    ve.wait_ge(dve_done, DV.start(phase, l))
                    step(ve.tensor_copy(gcur[:, :], gall[:, bass.ds(l * 16, 16)]))
                for t in range(TT):
                    mean_square(phase, t, l)
                    tile_root(phase, t, l)
                    own(phase, ("n2", t), l)
                    step(ve.tensor_scalar(rows[:, t, :], acc_t[:, t, :], rs[:, t:t + 1], None, ALU.mult))
                g0 = 0 if mix else 8
                for k in range(KT):
                    act(phase, ("hh", k), l)
                    step(ve.scalar_tensor_tensor(out=hlo[:, k, :], in0=banks[k][:, :], scalar=gcur[:, g0 + k:g0 + k + 1],
                                                 in1=hhi[:, k, :].bitcast(F32), op0=ALU.mult, op1=ALU.subtract))
                ve.wait_ge(x_saved, (16 if mix else 32) + l * 32)
                own(phase, ("h", 3), l)
                step(ve.memset(acc[:, :], 0.0))

            def post(phase, l, i):
                for t in range(TT + 1):
                    if t < TT:
                        mean_square(phase, t, l)
                    if t == 1:
                        ve.wait_ge(gpost_landed, (16 if phase == "post_mix" else 32) + l * 32)
                        ve.wait_ge(rows_landed, (16 if phase == "post_mix" else 32) + l * 32)
                    if t:
                        p = t - 1
                        own(phase, ("n2", p), l)
                        step(ve.scalar_tensor_tensor(out=acc_t[:, p, :], in0=acc_t[:, p, :], scalar=rs[:, p:p + 1],
                                                     in1=gpost[:, :], op0=ALU.mult, op1=ALU.mult))
                        own(phase, ("pg", p), l)
                        step(ve.tensor_tensor(acc_t[:, p, :], acc_t[:, p, :], rows[:, p, :], ALU.add))
                    if t < TT:
                        tile_root(phase, t, l)

            def normalise(phase, l, i):
                ve.wait_ge(dve_done, DV.start(phase, l, i))
                step(ve.tensor_scalar(vv[:, :], bag[:, :, 1], EPS, None, ALU.add))
                reciprocal_root(phase, "rt", lambda z: z, slice(0, 4), l, i)
                own(phase, "n2", l, i)
                for t in range(TT):
                    step(ve.tensor_scalar(yn[:, t, :], lo4[t][:, :], bag[:, t, 0:1], rs[:, t:t + 1],
                                          ALU.subtract, ALU.mult))

            def gated(phase, l, i):
                ve.wait_ge(act_done, AC.start(phase, l, i))
                for e in range(4):
                    pe(phase, ("t", e), l, i)
                    step(ve.tensor_tensor(scr[:, e, :], lo4[e][:, :], sgr[:, e, :], ALU.mult))
                    act(phase, ("zh", e), l, i)
                    own(phase, ("zm", e), l, i)
                    step(ve.tensor_tensor(rvl[:, e, :], scr[:, e, :], rvh[:, e, :].bitcast(F32), ALU.subtract))

            def rotate(phase, x, before, ba, bb, dh, dl, l, i):
                cos, sin = trig[:, 0, :], trig[:, 1, :]
                if before:
                    own(phase, before, l, i)
                else:
                    ve.wait_ge(dve_done, DV.start(phase, l, i))
                pe(phase, (x, 1), l, i)
                step(ve.tensor_tensor(scr[:, 0, :], ba[:, :], cos, ALU.mult))
                step(ve.tensor_tensor(scr[:, 1, :], bb[:, :], sin, ALU.mult))
                own(phase, (x, 1), l, i)
                step(ve.tensor_tensor(scr[:, 0, :], scr[:, 0, :], scr[:, 1, :], ALU.subtract))
                step(ve.tensor_tensor(scr[:, 2, :], ba[:, :], sin, ALU.mult))
                step(ve.tensor_tensor(scr[:, 3, :], bb[:, :], cos, ALU.mult))
                own(phase, (x, 4), l, i)
                step(ve.tensor_tensor(scr[:, 2, :], scr[:, 2, :], scr[:, 3, :], ALU.add))
                for n in range(2):
                    act(phase, (x + "h", n), l, i)
                    own(phase, (x, 2 + 3 * n), l, i)
                    step(ve.tensor_tensor(dl[:, n, :], scr[:, 2 * n, :], dh[:, n, :].bitcast(F32), ALU.subtract))

            def add_ret_out(phase, l, i):
                for f in range(8):
                    pe(phase, ("w", f), l, i)
                    step(ve.tensor_tensor(acc_f[:, f, :], acc_f[:, f, :], lo4[f % 4][:, :], ALU.add))

            def ret(phase, l, i):
                if phase == "ret":
                    normalise(phase, l, i)
                    gated(phase, l, i)
                else:
                    ve.wait_ge(const_landed, 16 * 4)
                side = hi4 if phase == "ret" else lo4
                rotate(phase, "q", ("zl", 3) if phase == "ret" else None, side[0], side[1], rqh, rql, l, i)
                rotate(phase, "k", ("ql", 1), hi4[2], hi4[3], rkh, rkl, l, i)
                if phase == "ret":
                    add_ret_out(phase, l, i)
                for t in range(TT):
                    act(phase, ("vh", t), l, i)
                    step(ve.tensor_tensor(rvl[:, t, :], hi4[t][:, :], rvh[:, t, :].bitcast(F32), ALU.subtract))
                h = 0 if phase == "ret_first" else i + 1
                ve.wait_ge(decay_landed, l * (16 * RH) + (h * 16 + 16))
                own(phase, ("kl", 1), l, i)
                at = 0
                for j in range(TT):
                    n = SEQ - j * 128
                    pe(phase, ("s", j), l, i)
                    step(ve.tensor_tensor(scr[:, j, 0:n], lo4[j][:, 0:n], decay[:, 0:n], ALU.mult))
                    act(phase, ("ph", j), l, i)
                    own(phase, ("pm", j), l, i)
                    step(ve.tensor_tensor(rpl[:, at:at + n], scr[:, j, 0:n], rph[:, at:at + n].bitcast(F32), ALU.subtract))
                    at += n
                for t in range(TT):
                    pe(phase, ("y", t), l, i)
                    step(ve.bn_stats(bst[:, t, :], lo4[t][:, :]))
                    own(phase, ("st", t), l, i)
                    ve.sem_inc(ve_waited, 1)
                    step(ve.bn_aggr(bag[:, t, :], bst[:, t, :]))

            def qk_tile(phase, n, free, l, i):
                s = n % 2
                act(phase, ("xc", n), l, i)
                free()
                step(ve.tensor_tensor(scr[:, s, :], xbank[n][:, :], acos[:, :], ALU.mult))
                step(ve.stream_shuffle(shuf[0:32, s, :], scr[0:32, 2 + s, :], [(m + 16) % 32 for m in range(32)]))
                own(phase, ("xs", n), l, i)
                step(ve.tensor_tensor(shuf[0:32, s, :], shuf[0:32, s, :], asin[:, :], ALU.mult))
                own(phase, ("xp", n), l, i)
                step(ve.tensor_tensor(scr[0:32, s, :], scr[0:32, s, :], shuf[0:32, s, :], ALU.add))
                act(phase, ("xh", n), l, i)
                own(phase, ("xa", n), l, i)
                dh, dl = (aqh, aql) if n < 3 else (akh, akl)
                step(ve.tensor_tensor(dl[:, n % 3, :], scr[:, s, :], dh[:, n % 3, :].bitcast(F32), ALU.subtract))

            def ret_last(phase, l, i):
                normalise(phase, l, i)
                gated(phase, l, i)
                for n in range(4):
                    qk_tile(phase, n, lambda: own(phase, ("zl", 3) if n < 2 else ("xl", n - 2), l), l, i)
                add_ret_out(phase, l, i)

            def att(phase, l, i):
                first = phase == "att_first"
                head = 0 if first else i + 1
                for n in range(4 if first else 0, 6):
                    if n < 2 or first:
                        free = lambda: ve.wait_ge(dve_done, DV.start(phase, l, i))
                    else:
                        free = lambda: own(phase, ("xl", n - 2), l, i)
                    qk_tile(phase, n, free, l, i)
                    if n == 1:
                        output_lo(phase, bass.ds(i, 1), l, i)
                for t in range(TT):
                    act(phase, ("vh", t), l, i)
                    step(ve.tensor_tensor(avl[:, t, :], lo4[t][:, 0:384], avh[:, t, :].bitcast(F32), ALU.subtract))

                def soft(c):
                    q = c % 2
                    pe(phase, ("s", c), l, i)
                    if c >= 2:
                        pe(phase, ("t", c - 2), l, i)
                    ve.sem_inc(ve_waited, 1)
                    at = 0
                    for g in range(AG):
                        w = (min(c, 1) + 1 if g == 0 else c + 1) * 128
                        off = 256 - w if g == 0 else 256 + 512 * g - w
                        step(ve.tensor_tensor_reduce(prob[:, q, at:at + w], hi4[g][:, 0:w], masks[:, off:off + w],
                                                     ATT_SCALE, -3.0e38, ALU.add, ALU.max, rmax[:, q, g:g + 1]))
                        at += w
                    own(phase, (("m", c), 2), l, i)
                    step(ve.tensor_reduce(nmax[:, q:q + 1], rmax[:, q, :], AX_X, ALU.max, negate=True))
                    act(phase, ("ex", c), l, i)
                    step(ve.reciprocal(rden[:, q:q + 1], den[:, q:q + 1]))
                    own(phase, ("rc", c), l, i)
                    step(ve.tensor_scalar(prob[:, q, 0:at], prob[:, q, 0:at], rden[:, q:q + 1], None, ALU.mult))

                def key_major(c):
                    w = len(blocks_of(c)) * 128
                    for b in range(banks_of(c)):
                        n = min(512, w - 512 * b)
                        act(phase, (("th", c), b), l, i)
                        step(ve.tensor_tensor(ptl[:, 512 * b:512 * b + n], lo4[b][:, 0:n],
                                              pth[:, 512 * b:512 * b + n].bitcast(F32), ALU.subtract))

                def gated_tile(n):
                    act(phase, ("sg", n), l, i)
                    tile = acc_f[:, bass.ds(head * 2 + n, 1), :].rearrange("p o n -> p (o n)")
                    step(ve.tensor_tensor(tile, tile, sga[:, 0, :], ALU.mult))

                soft(0)
                key_major(0)
                soft(1)
                if first:
                    own("ret_last", ("wa", 7), l)
                gated_tile(0)
                key_major(1)
                soft(2)
                key_major(2)
                soft(3)
                gated_tile(1)
                key_major(3)

            def output_lo(phase, at, l, i):
                act(phase, "yh", l, i)
                step(ve.tensor_tensor(yal[:, at, :].rearrange("p o n -> p (o n)"), lo4[3][:, :],
                                      yah[:, at, :].rearrange("p o n -> p (o n)").bitcast(F32), ALU.subtract))

            def merge(phase, l, i):
                output_lo(phase, slice(AI - 1, AI), l, i)
                for f in range(8):
                    act(phase, ("sg", f), l)
                    pe(phase, ("w", f), l)
                    step(ve.tensor_tensor(scr[:, f % 4, :], scr[:, f % 4, :], lo4[f % 4][:, :], ALU.mult))
                    own(phase, ("yg", f), l)
                    step(ve.tensor_tensor(acc_f[:, f, :], acc_f[:, f, :], scr[:, f % 4, :], ALU.add))
                    act(phase, ("mh", f), l)
                    own(phase, ("ym", f), l)
                    step(ve.tensor_tensor(mgl[:, f, :], acc_f[:, f, :], mgh[:, f, :].bitcast(F32), ALU.subtract))

            def ffn(phase, l, i):
                for b in range(2 if phase in ("ffn", "ffn_end") else 1):
                    if phase != "ffn_last":
                        par = pair_slot(phase, b)
                        for k in range(2):
                            act(phase, ("si", k, b), l, i)
                            pe(phase, ("u", k, b), l, i)
                            step(ve.tensor_tensor(scr[:, 2 + k, :], scr[:, k, :], hi4[2 + k][:, :], ALU.mult))
                            act(phase, ("ah", k, b), l, i)
                            own(phase, ("am", k, b), l, i)
                            step(ve.tensor_tensor(ffl[:, 2 * par + k, :], scr[:, 2 + k, :],
                                                  ffh[:, 2 * par + k, :].bitcast(F32), ALU.subtract))
                    if phase != "ffn_first":
                        for g in R8:
                            pe(phase, ("d", g, b), l, i)
                            sums = acc_t[:, g // 2, g % 2 * 512:g % 2 * 512 + 512]
                            step(ve.tensor_tensor(sums, sums, lo4[g % 4][:, :], ALU.add))

            def body(phase, l, i):
                if phase in ("pre_mix", "pre_ffn"):
                    pre(phase, l, i)
                elif phase in ("post_mix", "post_ffn"):
                    post(phase, l, i)
                elif phase in ("ret_first", "ret"):
                    ret(phase, l, i)
                elif phase == "ret_last":
                    ret_last(phase, l, i)
                elif phase in ("att_first", "att"):
                    att(phase, l, i)
                elif phase == "merge":
                    merge(phase, l, i)
                elif phase.startswith("ffn"):
                    ffn(phase, l, i)

            ve.sem_inc(dve_done, 1)
            ve.wait_ge(early_landed, 16 * 2)
            with ve.Fori(0, DEPTH) as l:
                bodies(ve, l, body)


def pair_slot(phase, b):
    return 0 if phase == "ffn_first" else 1 - b


def tables():
    f32 = np.float32
    pos = np.arange(SEQ, dtype=f32)
    half = 128
    inv = (f32(10000.0) ** (-np.arange(half, dtype=f32) / f32(half))).astype(f32)
    ang = (pos[None, :] * inv[:, None]).astype(f32)
    trig = np.stack([np.cos(ang), np.sin(ang)], axis=1).astype(f32)
    half = 16
    inv = (f32(500000.0) ** (-np.arange(half, dtype=f32) / f32(half))).astype(f32)
    ang = (pos[None, :] * inv[:, None]).astype(f32)
    acos = np.ones((P, SEQ), f32)
    acos[0:16] = acos[16:32] = np.cos(ang)
    asin = np.concatenate([-np.sin(ang), np.sin(ang)]).astype(f32)
    q, k = np.arange(P)[:, None], np.arange(P)[None, :]
    parts = [k >= q, k <= q]
    for r in (4, 16):
        same = (q - k) % r == 0
        parts += [same, same, same, same & (k <= q)]
    masks = np.where(np.concatenate(parts, axis=1), 0.0, NEG).astype(f32)
    n, p = np.arange(SEQ)[None, :], np.arange(P)[:, None]
    decays = []
    for h in range(RH):
        lg = np.log(1.0 - 2.0 ** (-5.0 - h))
        decays.append(np.where(n >= p, np.exp(np.maximum(n - p, 0) * lg), 0.0) / 16.0)
    decays.append(decays[0])
    return {"ident": np.eye(P, dtype=f32), "ret_trig": trig, "att_cos": acos, "att_sin": asin,
            "att_masks": masks, "decays": np.stack(decays).astype(f32)}


def kernel(x, w_in, w_ret_out, w_att_out, w_o, w_ffn_gate, w_ffn_up, w_ffn_down,
           g_pre_mix, g_post_mix, g_pre_ffn, g_post_ffn):
    import concourse.bacc as bacc
    from concourse.bass_utils import run_bass_kernel_spmd

    nc = bacc.Bacc("TRN2", target_bir_lowering=False, num_devices=1)
    gains = np.stack([np.asarray(g_pre_mix), np.asarray(g_pre_ffn)], axis=1).reshape(DEPTH, 2, KT, P)
    gains = np.ascontiguousarray(gains.transpose(3, 0, 1, 2).reshape(P, DEPTH * 2 * KT))
    arrays = {"x": np.asarray(x).reshape(SEQ, D), "w_in": w_in, "w_ret": w_ret_out, "w_att": w_att_out, "w_o": w_o,
              "w_gate": w_ffn_gate, "w_up": w_ffn_up, "w_down": w_ffn_down, "gains": gains,
              "g_post_mix": g_post_mix, "g_post_ffn": g_post_ffn}
    t = tables()
    arrays |= {"ident_in": t["ident"], "ret_trig": t["ret_trig"], "att_cos": t["att_cos"], "att_sin": t["att_sin"],
               "att_masks": t["att_masks"], "decays": t["decays"]}
    arrays = {k: np.ascontiguousarray(v) for k, v in arrays.items()}
    args = [nc.dram_tensor(k, v.shape, F32, kind="ExternalInput").ap() for k, v in arrays.items()]
    out = nc.dram_tensor("out", (SEQ, D), F32, kind="ExternalOutput").ap()
    build(nc, *args, out)
    r = run_bass_kernel_spmd(nc, [arrays], core_ids=[0])
    return r.results[0]["out"].reshape(1, SEQ, D)
```

```python
from contextlib import ExitStack

import numpy as np

import concourse.bass as bass
from concourse import mybir

F32 = mybir.dt.float32
F32R = mybir.dt.float32r
ALU = mybir.AluOpType
ACT = mybir.ActivationFunctionType
AX_X = mybir.AxisListType.X

P = 128
D = 1024
SEQ = 512
DEPTH = 2
KT = D // P
TT = SEQ // P
RH = 4
AG = 3
AI = 4
DFF = 2816
PAIRS = DFF // (2 * P)
EPS = 1e-6
NEG = -1e30
ATT_SCALE = 1.0 / float(np.sqrt(128.0))
RQ, RK, RV, RG, AQ, AK, AV, GR, GA = 0, 1024, 2048, 4096, 6144, 7680, 9216, 10752, 11776
D_IN = 12800
SLOTS = 2
SLOT = 2048


class Steps:

    def __init__(self, prologue, plan):
        self.base, self.per = {"start": 1}, {"start": len(prologue)}
        self.index, at = {"start": {name: n for n, name in enumerate(prologue)}}, 1 + len(prologue)
        for phase, times, labels in plan:
            self.base[phase], self.per[phase] = at, len(labels)
            self.index[phase] = {name: n for n, name in enumerate(labels)}
            assert len(self.index[phase]) == len(labels)
            at += times * len(labels)
        self.layer = at - 1 - len(prologue)

    def start(self, phase, l, i=0):
        return l * self.layer + (self.base[phase] + i * self.per[phase])

    def of(self, phase, name, l, i=0):
        return l * self.layer + (i * self.per[phase] + (self.base[phase] + self.index[phase][name] + 1))

    def last(self, phase, name, l, i):
        at = self.base[phase] + self.index[phase][name] + 1 - self.per[phase]
        assert at > 0
        return l * self.layer + (i * self.per[phase] + at)


PHASES = [("pre_mix", 1), ("ret_first", 1), ("ret", RH - 1), ("ret_last", 1), ("att_first", 1),
          ("att", AI - 1), ("merge", 1), ("w_o", 1), ("post_mix", 1), ("pre_ffn", 1), ("ffn_first", 1),
          ("ffn", PAIRS // 2 - 1), ("ffn_end", 1), ("ffn_last", 1), ("post_ffn", 1)]

FULL, HALF = (2048, 2), (1024, 1)
VALUES = [(1152, 3), (1152, 3), (768, 3)]
UNITS = {
    "pre_mix": [],
    "ret_first": [FULL] * 6,
    "ret": [FULL] * 8,
    "ret_last": [FULL] * 4,
    "att_first": [FULL] + VALUES + [HALF] * 2,
    "att": [FULL] * 3 + VALUES + [HALF] * 2,
    "merge": [FULL] * 6,
    "w_o": [FULL] * 4,
    "post_mix": [], "pre_ffn": [],
    "ffn_first": [FULL] * 2,
    "ffn": [FULL] * 6,
    "ffn_end": [FULL] * 6,
    "ffn_last": [HALF] * 2,
    "post_ffn": [],
}
AHEAD = {"ret_first": FULL, "ret": FULL, "ret_last": FULL, "att_first": FULL, "att": FULL, "merge": FULL,
         "w_o": FULL, "ffn_first": FULL, "ffn": FULL, "ffn_end": HALF}


class Units:

    def __init__(self):
        self.base, self.dmas, at, dmas = {}, {}, 0, [0, 0]
        for phase, times in PHASES:
            assert len(UNITS[phase]) % SLOTS == 0
            self.base[phase] = at
            self.dmas[phase] = list(dmas)
            at += times * len(UNITS[phase])
            for s in range(SLOTS):
                dmas[s] += times * sum(n for _, n in UNITS[phase][s::SLOTS])
        self.layer, self.layer_dmas = at, dmas

    def number(self, phase, c, l, i=0):
        return l * self.layer + (i * len(UNITS[phase]) + (self.base[phase] + c))

    def landed(self, phase, c, l, i=0):
        s = c % SLOTS
        per = sum(n for _, n in UNITS[phase][s::SLOTS])
        upto = sum(n for _, n in UNITS[phase][s:c + 1:SLOTS])
        return l * (16 * self.layer_dmas[s]) + (i * (16 * per) + 16 * (self.dmas[phase][s] + upto))


R4, R8 = range(4), range(8)
RSTD = ("v", "rc", "sr", "n0", "n1")
NORM = ("v2", "rc2", "n02", "n12")


def rotated(x):
    return [(x, n) for n in range(6)] + [(x + "l", 0), (x + "l", 1)]


def retention_plan(phase):
    out_pe = [("w", f) for f in R8]
    gated_dve = [(z, e) for e in R4 for z in ("zm", "zl")]
    norm_dve = list(RSTD) + [("yn", t) for t in R4]
    scores_dve = [(z, j) for j in R4 for z in ("pm", "pl")] + [(z, t) for t in R4 for z in ("st", "ag")]
    vals = [("end", "v")] + [("v", t) for t in R4] + [("s", j) for j in R4]
    if phase == "ret_first":
        pe = [("q", 0), ("q", 1), ("k", 0), ("k", 1), ("g", 0), ("g", 1)] + vals + [("g", 2), ("g", 3)]
        act = [("qh", 0), ("qh", 1), ("kh", 0), ("kh", 1), ("sg", 0), ("sg", 1)] + [("vh", t) for t in R4]
        act += [("ph", j) for j in R4] + [("sg", 2), ("sg", 3)]
        dve = rotated("q") + rotated("k") + ["clear"] + [("vl", t) for t in R4] + scores_dve
        return pe + [("y", t) for t in R4], act, dve
    if phase == "ret":
        pe = [("q", 0), ("q", 1)] + [("t", e) for e in R4] + [("k", 0), ("k", 1)] + out_pe + vals
        pe += [("g", e) for e in R4] + [("y", t) for t in R4]
        act = ["rt"] + [("zh", e) for e in R4] + [("qh", 0), ("qh", 1), ("kh", 0), ("kh", 1)]
        act += [("vh", t) for t in R4] + [("ph", j) for j in R4] + [("sg", e) for e in R4]
        dve = norm_dve + gated_dve + rotated("q") + rotated("k") + [("wa", f) for f in R8]
        return pe, act, dve + [("vl", t) for t in R4] + scores_dve
    pe = [("x", 0), ("x", 1)] + [("t", e) for e in R4] + [("x", 2), ("x", 3)] + out_pe
    act = ["rt"] + [("zh", e) for e in R4] + [(z, n) for n in R4 for z in ("xc", "xh")]
    dve = norm_dve + gated_dve
    for n in R4:
        dve += [("wa", f) for f in ADD_BEFORE.get(n, [])] + [(z, n) for z in XSTEPS]
    return pe, act, dve + [("wa", f) for f in range(4, 8)]


ADD_BEFORE = {2: [0, 1], 3: [2, 3]}
XSTEPS = ("xm", "xs", "xp", "xa", "xl")


def attention_plan(phase):
    ends = [("end", 0), ("end", 1)] + [("v", t) for t in R4]
    pe = [("s", 0), ("s", 1), ("t", 0), ("g", 0), ("s", 2), ("t", 1), ("s", 3), ("t", 2), "p", ("g", 1), ("t", 3)]
    hi = lambda c: [(("th", c), g) for g in range(AG)]
    lo = lambda c: [(("tl", c), g) for g in range(AG)]
    act = [("ex", 0)] + hi(0) + [("ex", 1), ("sg", 0)] + hi(1) + [("ex", 2)] + hi(2) + [("ex", 3), ("sg", 1)] + hi(3)
    dve = []
    for c in range(TT):
        dve += [(("m", c), g) for g in range(AG)] + [("mx", c)] + (lo(c - 1) if c else [])
        dve += [("gm", 0)] * (c == 2) + [("rc", c), ("pn", c)]
    dve += [("gm", 1)] + lo(3)
    first = 4 if phase == "att_first" else 0
    xs = range(first, 6)
    x_pe, x_act, x_dve = [], [], []
    for n in xs:
        x_pe += [("x", n)]
        x_act += [("xc", n), ("xh", n)]
        x_dve += [(z, n) for z in XSTEPS]
        if n == 1:
            x_pe, x_act, x_dve = x_pe + ["pp"], x_act + ["yh"], x_dve + ["yl"]
    return (x_pe + ends + pe, x_act + [("vh", t) for t in R4] + act, x_dve + [("vl", t) for t in R4] + dve)


def ffn_plan(phase):
    pe, act, dve = [], [], []
    for b in range(2 if phase in ("ffn", "ffn_end") else 1):
        if phase != "ffn_last":
            pe += [(z, k, b) for z in ("g", "u") for k in range(2)]
            act += [("si", 0, b), ("si", 1, b), ("ah", 0, b), ("ah", 1, b)]
            dve += [(z, k, b) for k in range(2) for z in ("am", "al")]
        if phase != "ffn_first":
            pe += [("d", g, b) for g in R8]
            dve += [("d", g, b) for g in R8] * (phase != "ffn_last")
        else:
            dve += ["clear"]
    return pe, act, dve


AFTER_FIRST_TILE = [("rt", 3), ("s2", 2)]


def plans():
    pre = ([("x", k) for k in R8], [("r2", 2), ("s2", 3), ("r2", 3)] + [("hh", k) for k in R8],
           [("v2", 2), ("h", 1)] + [(z, 2) for z in NORM[1:]] + [("v2", 3), ("h", 2)]
           + [(z, 3) for z in NORM[1:]] + [("h", 3)] + [("hl", k) for k in R8])
    post_act = [("sq", 0), ("rt", 0)] + [("sq", 1), ("rt", 1), ("s2", 0)] + [("sq", 2), ("r2", 0), ("rt", 2)]
    post_act += [("s2", 1), ("sq", 3), ("r2", 1), ("h", 0), ("rt", 3), ("s2", 2)]

    def post_dve(mix):
        steps = [] if mix else [("d", g) for g in R4]
        for t in R4:
            steps += [("v", t)] + [("z", t)] * mix + [("rc", t), ("n0", t), ("n1", t)]
            steps += [("d", 2 * t + 4), ("d", 2 * t + 5)] * (t < 2 and not mix) + [("v2", t - 1)] * (0 < t < 3)
            steps += [("xa", t)] + [(z, t - 1) for z in NORM[1:]] * (0 < t < 3)
        return steps
    merge_pe = [("a", 0), ("a", 1), "pp", ("a", 2), ("a", 3)] + [("w", f) for f in R4]
    merge_pe += [("a", f) for f in range(4, 8)] + [("w", f) for f in range(4, 8)]
    merge_act = [("sg", 0), ("sg", 1), "yh", ("sg", 2), ("sg", 3)] + [("mh", f) for f in R4]
    merge_act += [("sg", f) for f in range(4, 8)] + [("mh", f) for f in range(4, 8)]
    lists = {
        "pre_mix": pre,
        "ret_first": retention_plan("ret_first"), "ret": retention_plan("ret"),
        "ret_last": retention_plan("ret_last"),
        "att_first": attention_plan("att_first"), "att": attention_plan("att"),
        "merge": (merge_pe, merge_act, ["yl"] + [(z, f) for f in R8 for z in ("yg", "ym", "ml")]),
        "w_o": ([("end", 0)] + [("o", 0, t) for t in R4] + [("end", 2)] + [("o", 1, t) for t in R4],
                [("sq", t) for t in R4], [("z", t) for t in R4] + ["e"]),
        "post_mix": ([], post_act, post_dve(True)),
        "pre_ffn": pre,
        "ffn_first": ffn_plan("ffn_first"), "ffn": ffn_plan("ffn"), "ffn_end": ffn_plan("ffn_end"),
        "ffn_last": ffn_plan("ffn_last"),
        "post_ffn": ([], post_act, post_dve(False)),
    }
    start = [[], [(z, 0) for z in ("s2", "r2", "h")] + [("s2", 1), ("r2", 1), ("s2", 2)],
             [(z, t) for t in range(2) for z in NORM]]
    return [(start[e], [(p, n, lists[p][e]) for p, n in PHASES]) for e in range(3)]


def blocks_of(c):
    return ([(0, m) for m in range(max(0, c - 1), c + 1)] + [(1, m) for m in range(c + 1)]
            + [(2, m) for m in range(c + 1)])


PAIR_BASE = [[0, 3, 6], [0, 4, 11]]


def block_at(c, g, m):
    return PAIR_BASE[c // 2][g] + 1 - c % 2 + 2 * (c - m)


def keys_of(c, g):
    return [m for h, m in blocks_of(c) if h == g]


UNIT_END = {
    "ret_first": [("q", 1), ("k", 1), ("g", 1), ("end", "v"), ("v", 3), ("g", 3)],
    "ret": [("q", 1), ("k", 1), ("w", 3), ("w", 7), ("end", "v"), ("v", 3), ("g", 1), ("g", 3)],
    "ret_last": [("x", 1), ("x", 3), ("w", 3), ("w", 7)],
    "att_first": [("x", 5), ("end", 0), ("end", 1), ("v", 3), ("g", 0), ("g", 1)],
    "att": [("x", 1), ("x", 3), ("x", 5), ("end", 0), ("end", 1), ("v", 3), ("g", 0), ("g", 1)],
    "merge": [("a", 1), ("a", 3), ("w", 3), ("a", 5), ("a", 7), ("w", 7)],
    "w_o": [("end", 0), ("o", 0, 3), ("end", 2), ("o", 1, 3)],
    "ffn_first": [("g", 1, 0), ("u", 1, 0)],
    "ffn": [x for b in range(2) for x in (("g", 1, b), ("u", 1, b), ("d", 7, b))],
}
UNIT_END["ffn_end"] = UNIT_END["ffn"]


def build(nc, x, w_in, w_ret, w_att, w_o, w_gate, w_up, w_down, gains, g_post_mix, g_post_ffn,
          ident_in, ret_trig, att_cos, att_sin, att_masks, decays, out):
    plan_pe, plan_act, plan_dve = plans()
    PE, AC, DV, UN = Steps(*plan_pe), Steps(*plan_act), Steps(*plan_dve), Units()

    with ExitStack() as ctx:
        def sb(name, shape, dt=F32):
            return ctx.enter_context(nc.sbuf_tensor(name, shape, dt))

        def sem(name):
            return ctx.enter_context(nc.semaphore(name))

        raw = [sb(f"raw{s}", [P, SLOT]) for s in range(SLOTS)]
        whi = [sb(f"whi{s}", [P, SLOT], F32R) for s in range(SLOTS)]
        wlo = [sb(f"wlo{s}", [P, SLOT], F32R) for s in range(SLOTS)]
        hhi = sb("hhi", [P, KT, SEQ], F32R)
        hlo = sb("hlo", [P, KT, SEQ], F32R)
        acc = sb("acc", [P, TT * D])
        acc_t = acc[:, :].rearrange("p (t n) -> p t n", t=TT)
        acc_f = acc[:, :].rearrange("p (f n) -> p f n", f=8)
        R = sb("split_operands", [P, 17152], F32R)
        F = sb("scratch", [P, 6144])

        def region(buf, at, *shape):
            n = int(np.prod(shape))
            v = buf[:, at:at + n]
            return v.rearrange("p (a b) -> p a b", a=shape[0]) if len(shape) == 2 else v

        rqh, rql, rkh, rkl = (region(R, n * 1024, 2, SEQ) for n in range(4))
        rph, rpl = region(R, 4096, 1280), region(R, 5376, 1280)
        rvh, rvl = region(R, 9216, 4, SEQ), region(R, 11264, 4, SEQ)
        aqh, aql = region(R, 0, 3, SEQ), region(R, 1536, 3, SEQ)
        avh, avl = region(R, 3072, 4, 384), region(R, 4608, 4, 384)
        akh, akl = region(R, 6144, 3, SEQ), region(R, 7680, 3, SEQ)
        pt = [(region(R, 10752, 9, P), region(R, 11904, 9, P)), (region(R, 6144, 18, P), region(R, 8448, 18, P))]
        yah, yal = region(R, 13056, 4, SEQ), region(R, 15104, 4, SEQ)
        mgh, mgl = region(R, 0, 8, SEQ), region(R, 4096, 8, SEQ)
        ffh, ffl = region(R, 0, 4, SEQ), region(R, 2048, 4, SEQ)

        rows = region(F, 0, 4, D)
        junk = hlo[:, 0:2, :].rearrange("p a b -> p (a b)")
        zf = region(F, 4096, 2, D)
        yn = region(F, 0, 4, SEQ)
        sgr = region(F, 2048, 4, SEQ)
        scr = region(F, 4096, 4, SEQ)
        prob = region(F, 0, 2, 1280)
        shuf = region(F, 2560, 2, SEQ)
        sga = region(F, 3584, 1, SEQ)

        ident = sb("ident", [P, P])
        trig = sb("trig", [P, 2, SEQ])
        acos = sb("acos", [P, SEQ])
        asin = sb("asin", [32, SEQ])
        masks = sb("masks", [P, 1280])
        decay = sb("decay", [P, SEQ])
        gall = sb("gall", [P, DEPTH * 16])
        gpost = sb("gpost", [P, D])
        ss, vv, sq, rs, aa = (sb(n, [P, 8]) for n in ("sum_sq", "var", "root", "rstd", "newton"))
        ss0 = sb("sum_sq_first_half", [P, 4])
        bst = sb("bst", [P, 4, 6])
        bag = sb("bag", [P, 4, 2])
        rmax = sb("rmax", [P, 2, 3])
        nmax = sb("nmax", [P, 2])
        den = sb("den", [P, 2])
        rden = sb("rden", [P, 2])

        banks = [ctx.enter_context(nc.psum_tensor(f"bank{b}", [P, 512], F32)) for b in range(8)]
        lo4, hi4 = banks[:4], banks[4:]
        xbank = [hi4[0], hi4[1], hi4[2], hi4[3], hi4[0], hi4[1]]
        ffn_banks = lambda phase: lo4[:2] + hi4[2:] if phase == "ffn_first" else hi4
        xs = nc.dram_tensor("x_between", (SEQ, D), F32, kind="Internal").ap()

        landed = [sem(f"unit_landed{s}") for s in range(SLOTS)]
        hi_ready = sem("unit_hi_ready")
        lo_ready = sem("unit_lo_ready")
        mm_done = sem("mm_done")
        act_done = sem("act_done")
        dve_done = sem("dve_done")
        early_landed = sem("early_landed")
        pool_done = sem("pool_done")
        const_landed = sem("const_landed")
        decay_landed = sem("decay_landed")
        gpost_landed = sem("gpost_landed")
        ve_waited = sem("ve_waited")
        x_landed = [sem(f"x_landed{t}") for t in range(TT)]
        rows_landed = sem("rows_landed")
        x_saved = sem("x_saved")
        out_saved = sem("out_saved")

        x_rows = lambda a: a.rearrange("(t p) n -> p t n", p=P)
        win = w_in.rearrange("l (k p) n -> p (l k) n", p=P)
        wret = w_ret.rearrange("l (k p) n -> p (l k) n", p=P)
        watt = w_att.rearrange("l (k p) n -> p (l k) n", p=P)
        wout = w_o.rearrange("l (k p) n -> p (l k) n", p=P)
        wgate = w_gate.rearrange("l (k p) n -> p (l k) n", p=P)
        wup = w_up.rearrange("l (k p) n -> p (l k) n", p=P)
        wdown = w_down.rearrange("l (k p) n -> p (l k) n", p=P)

        block = ctx.enter_context(nc.Block())

        def bodies(eng, l, body):
            for phase, times in PHASES:
                if times == 1:
                    body(phase, l, 0)
                else:
                    with eng.Fori(0, times) as i:
                        body(phase, l, i)

        @block.sync
        def _(sp):
            for dst, src in ((gall[:, :], gains), (ident[:, :], ident_in)):
                sp.dma_start(dst, src).then_inc(early_landed, 16)
            for t in range(TT):
                sp.dma_start(acc_t[:, t, :], x[t * P:(t + 1) * P, :]).then_inc(x_landed[t], 16)

            def unit(phase, c, l, i, parts):
                assert len(parts) == UNITS[phase][c][1]
                sp.wait_ge(lo_ready, UN.number(phase, c, l, i) + 1)
                for at, k, n, src in parts:
                    dst = raw[c % SLOTS][:, at:at + k * n].rearrange("p (k n) -> p k n", k=k)
                    sp.dma_start(dst, src).then_inc(landed[c % SLOTS], 16)

            def cols(w, l, col, n=256):
                if n == 128:
                    return [(0, 8, n, w[:, bass.ds(l * 8, 8), bass.ds(col, n)])]
                return [(h * 4 * n, 4, n, w[:, bass.ds(l * 8 + h * 4, 4), bass.ds(col, n)]) for h in range(2)]

            def rows4(w, k0, col):
                return [(h * 1024, 2, 512, w[:, bass.ds(k0 + 2 * h, 2), bass.ds(col, 512)]) for h in range(2)]

            def two_tiles(l, i, u):
                tiles = [AQ + g * 512 for g in range(AG)] + [AK + g * 512 for g in range(AG)]
                return [(n * 1024, 8, 128, win[:, bass.ds(l * 8, 8), bass.ds(i * 128 + tiles[2 * u + n], 128)])
                        for n in range(2)]

            def first_units(l):
                for c, at in enumerate((RQ, RK)):
                    unit("ret_first", c, l, 0, cols(win, l, at))

            def body(phase, l, i):
                put = lambda c, parts: unit(phase, c, l, i, parts)
                if phase in ("ret_first", "ret"):
                    h = 0 if phase == "ret_first" else i + 1
                    q, k = cols(win, l, h * 256 + RQ), cols(win, l, h * 256 + RK)
                    v = [rows4(win, l * 8 + 4 * n, h * 512 + RV) for n in range(2)]
                    gate = [cols(win, l, h * 512 + (RG + 256 * n)) for n in range(2)]
                    if phase == "ret_first":
                        order = [q, k, gate[0], v[0], v[1], gate[1]]
                    else:
                        order = [q, k] + [rows4(wret, l * 16 + (h * 4 - 4), 512 * n) for n in range(2)] + v + gate
                    for c, parts in enumerate(order):
                        if phase == "ret" or c >= 2:
                            put(c, parts)
                elif phase == "ret_last":
                    for u in range(2):
                        put(u, two_tiles(l, 0, u))
                    for n in range(2):
                        put(2 + n, rows4(wret, l * 16 + (RH * 4 - 4), 512 * n))
                elif phase in ("att_first", "att"):
                    a = 0 if phase == "att_first" else i + 1
                    c = 0
                    for u in range(2 if phase == "att_first" else 0, 3):
                        put(c, two_tiles(l, a, u))
                        c += 1
                    for k0, k in ((0, 3), (3, 3), (6, 2)):
                        put(c, [(g * k * 128, k, 128, win[:, bass.ds(l * 8 + k0, k), bass.ds(a * 128 + (AV + g * 512), 128)])
                                for g in range(AG)])
                        c += 1
                    for n in range(2):
                        put(c + n, cols(win, l, a * 256 + (GR + 128 * n), 128))
                elif phase == "merge":
                    for n in range(2):
                        put(3 * n, cols(win, l, GA + 512 * n))
                        put(3 * n + 1, cols(win, l, GA + 512 * n + 256))
                        put(3 * n + 2, rows4(watt, l * 4, 512 * n))
                elif phase == "w_o":
                    for n in range(2):
                        for k in range(2):
                            put(2 * n + k, rows4(wout, l * 8 + 4 * k, 512 * n))
                elif phase.startswith("ffn"):
                    pairs = {"ffn_first": [0], "ffn": [i * 2 + 1, i * 2 + 2], "ffn_end": [PAIRS - 2, PAIRS - 1],
                             "ffn_last": []}[phase]
                    c = 0
                    for j in pairs:
                        put(c, cols(wgate, l, j * 256))
                        put(c + 1, cols(wup, l, j * 256))
                        c += 2
                        if phase != "ffn_first":
                            k0 = l * (DFF // P) + (j * 2 - 2)
                            put(c, [(k * 1024, 1, 1024, wdown[:, bass.ds(k0 + k, 1), :]) for k in range(2)])
                            c += 1
                    if phase == "ffn_last":
                        for k in range(2):
                            put(k, [(0, 1, 1024, wdown[:, bass.ds(l * (DFF // P) + (2 * PAIRS - 2 + k), 1), :])])

            first_units(0)
            for dst, src in ((trig[:, :, :], ret_trig), (acos[:, :], att_cos),
                             (asin[:, :], att_sin), (masks[:, :], att_masks)):
                sp.dma_start(dst, src).then_inc(const_landed, 16)
            sp.dma_start(decay[:, :], decays[0]).then_inc(decay_landed, 16)
            with sp.Fori(0, DEPTH - 1) as l:
                bodies(sp, l, body)
                first_units(l + 1)
            bodies(sp, DEPTH - 1, body)
            for t in range(TT):
                sp.wait_ge(dve_done, DV.of("post_ffn", ("xa", t), DEPTH - 1))
                sp.dma_start(out[t * P:(t + 1) * P, :], acc_t[:, t, :]).then_inc(out_saved, 16)
            sp.wait_ge(out_saved, 16 * TT)
            sp.wait_ge(x_saved, 16 * 2 * DEPTH)
            sp.wait_ge(rows_landed, 16 * 2 * DEPTH)
            sp.wait_ge(gpost_landed, 16 * 2 * DEPTH)
            sp.wait_ge(decay_landed, 16 * (1 + RH * DEPTH))

        @block.gpsimd
        def _(pool):
            pool.sem_inc(lo_ready, 2)

            def times_gain(l):
                pool.wait_ge(gpost_landed, 32 + l * 32)
                for t in range(TT):
                    pool.wait_ge(dve_done, DV.of("post_ffn", ("d", 2 * t + 1), l))
                    if t >= 2:
                        pool.wait_ge(dve_done, DV.of("post_ffn", ("xa", t - 2), l))
                    pool.tensor_tensor(zf[:, t % 2, :], acc_t[:, t, :], gpost[:, :], ALU.mult).then_inc(pool_done, 1)

            def body(phase, l, i):
                if phase == "post_ffn":
                    times_gain(l)
                for c, (size, _) in enumerate(UNITS[phase]):
                    s = c % SLOTS
                    pool.wait_ge(hi_ready, UN.number(phase, c, l, i) + 1)
                    pool.tensor_tensor(wlo[s][:, 0:size], raw[s][:, 0:size], whi[s][:, 0:size].bitcast(F32),
                                       ALU.subtract).then_inc(lo_ready, 1)

            with pool.Fori(0, DEPTH) as l:
                bodies(pool, l, body)

        @block.tensor
        def _(pe):
            def mm3(o, lh, ll, rh, rl, start, stop):
                pe.matmul(o, lh, rh, start=start, stop=False)
                pe.matmul(o, lh, rl, start=False, stop=False)
                return pe.matmul(o, ll, rh, start=False, stop=stop)

            def use(phase, c, l, i):
                pe.wait_ge(lo_ready, UN.number(phase, c, l, i) + 3)

            def dve(phase, name, l, i=0):
                pe.wait_ge(dve_done, DV.of(phase, name, l, i))

            def act(phase, name, l, i=0):
                pe.wait_ge(act_done, AC.of(phase, name, l, i))

            def parts_of(c, at, k, n):
                return [w[c % SLOTS][:, at:at + k * n].rearrange("p (k n) -> p k n", k=k) for w in (whi, wlo)]

            def features(o, weights, tile, h_steps=None, ks=range(KT)):
                h, w = weights
                at = slice(tile * 128, tile * 128 + 128)
                for k in ks:
                    if h_steps:
                        dve(h_steps[0], ("hl", k), h_steps[1])
                    mm = mm3(o[:, :], h[:, k, at], w[:, k, at], hhi[:, k, :], hlo[:, k, :], k == 0, k == KT - 1)
                return mm

            def token_rows(o, weights, t, lh, ll, k0, ktotal, cols=slice(0, 512)):
                h, w = weights
                at = slice(t * 128, t * 128 + 128)
                for k in range(h.shape[1]):
                    kk = k0 + k
                    mm = mm3(o[:, :], lh[:, kk, at], ll[:, kk, at], h[:, k, cols], w[:, k, cols],
                             kk == 0, kk == ktotal - 1)
                return mm

            def pre(phase, l, i):
                for t in range(TT):
                    if t:
                        dve(phase, ("h", t), l)
                    elif phase == "pre_ffn":
                        act("post_mix", ("h", 0), l)
                        dve("post_mix", ("z", 3), l)
                    else:
                        pe.wait_ge(act_done, AC.start(phase, l) - len(AFTER_FIRST_TILE))
                    for k in range(KT):
                        mm = pe.transpose(banks[k][:, t * 128:(t + 1) * 128], rows[:, t, k * 128:(k + 1) * 128],
                                          ident[:, :])
                        if t == TT - 1:
                            mm.then_inc(mm_done, 1)

            def back_transposes(phase, l, i):
                dve(phase, ("yn", 3), l, i)
                for e in range(4):
                    for t in range(TT):
                        mm = pe.transpose(lo4[e][:, t * 128:(t + 1) * 128], yn[:, t, e * 128:(e + 1) * 128],
                                          ident[:, :])
                    mm.then_inc(mm_done, 1)

            def ret_out(phase, c0, l, i):
                dve(phase, ("zl", 3), l, i)
                for half in range(2):
                    use(phase, c0 + half, l, i)
                    h, w = parts_of(c0 + half, 0, 4, 512)
                    for f in range(4):
                        if half:
                            dve(phase, ("wa", f), l, i)
                        at = slice(f * 128, f * 128 + 128)
                        for k in range(4):
                            mm = mm3(lo4[f][:, :], h[:, k, at], w[:, k, at], rvh[:, k, :], rvl[:, k, :],
                                     k == 0, k == 3)
                        mm.then_inc(mm_done, 1)

            def ret_values(phase, c0, l, i):
                dve(phase, ("kl", 1), l, i)
                for half in range(2):
                    use(phase, c0 + half, l, i)
                    for t in range(TT):
                        mm = token_rows(hi4[t], parts_of(c0 + half, 0, 4, 512), t, hhi, hlo, 4 * half, KT)
                        if half or t == TT - 1:
                            mm.then_inc(mm_done, 1)

            def ret_scores():
                for j in range(TT):
                    n = SEQ - j * 128
                    for d in range(2):
                        mm = mm3(lo4[j][:, 0:n], rkh[:, d, j * 128:(j + 1) * 128], rkl[:, d, j * 128:(j + 1) * 128],
                                 rqh[:, d, j * 128:SEQ], rql[:, d, j * 128:SEQ], d == 0, d == 1)
                    mm.then_inc(mm_done, 1)

            def ret_output(phase, l, i):
                dve(phase, ("pl", 3), l, i)
                for t in range(TT):
                    for j in range(t + 1):
                        at = sum(SEQ - 128 * a for a in range(j)) + (t - j) * 128
                        mm = mm3(lo4[t][:, :], rph[:, at:at + 128], rpl[:, at:at + 128], rvh[:, j, :], rvl[:, j, :],
                                 j == 0, j == t)
                    mm.then_inc(mm_done, 1)

            def ret_first(phase, l, i):
                use(phase, 0, l, i)
                features(lo4[0], parts_of(0, 0, 8, 256), 0, ("pre_mix", l)).then_inc(mm_done, 1)
                features(lo4[1], parts_of(0, 0, 8, 256), 1).then_inc(mm_done, 1)
                use(phase, 1, l, i)
                for n in range(2):
                    features(hi4[2 + n], parts_of(1, 0, 8, 256), n).then_inc(mm_done, 1)
                use(phase, 2, l, i)
                for n in range(2):
                    features(lo4[2 + n], parts_of(2, 0, 8, 256), n).then_inc(mm_done, 1)
                ret_values(phase, 3, l, i)
                act(phase, ("sg", 1), l)
                ret_scores()
                use(phase, 5, l, i)
                dve(phase, ("vl", 3), l)
                for n in range(2):
                    features(hi4[2 + n], parts_of(5, 0, 8, 256), n).then_inc(mm_done, 1)
                ret_output(phase, l, i)

            def ret(phase, l, i):
                use(phase, 0, l, i)
                pe.wait_ge(act_done, AC.start(phase, l, i))
                for n in range(2):
                    features(hi4[n], parts_of(0, 0, 8, 256), n).then_inc(mm_done, 1)
                back_transposes(phase, l, i)
                use(phase, 1, l, i)
                for n in range(2):
                    features(hi4[2 + n], parts_of(1, 0, 8, 256), n).then_inc(mm_done, 1)
                ret_out(phase, 2, l, i)
                ret_values(phase, 4, l, i)
                dve(phase, ("wa", 7), l, i)
                ret_scores()
                for half in range(2):
                    use(phase, 6 + half, l, i)
                    for n in range(2):
                        e = 2 * half + n
                        dve(phase, ("vl", e), l, i)
                        features(hi4[e], parts_of(6 + half, 0, 8, 256), n).then_inc(mm_done, 1)
                ret_output(phase, l, i)

            def qk_tile(c, n):
                return features(xbank[n], parts_of(c, (n % 2) * 1024, 8, 128), 0).then_inc(mm_done, 1)

            def ret_last(phase, l, i):
                use(phase, 0, l, i)
                pe.wait_ge(act_done, AC.start(phase, l))
                for n in range(2):
                    qk_tile(0, n)
                back_transposes(phase, l, i)
                use(phase, 1, l, i)
                for n in range(2, 4):
                    qk_tile(1, n)
                ret_out(phase, 2, l, i)

            def att(phase, l, i):
                first = phase == "att_first"
                for c, u in enumerate(range(2 if first else 0, 3)):
                    use(phase, c, l, i)
                    for n in (2 * u, 2 * u + 1):
                        if n == 0:
                            pe.wait_ge(dve_done, before_start(DV, phase, l, i, (("m", 3), 2)))
                        if n == 3:
                            pe.wait_ge(act_done, before_start(AC, phase, l, i, ("sg", 1)))
                        if n >= 4:
                            dve("ret_last" if first else phase, ("xl", n - 4), l, i)
                        qk_tile(c, n)
                    if u == 0:
                        pe.wait_ge(dve_done, DV.start(phase, l, i))
                        products(1)
                v0 = 1 if first else 3
                if first:
                    dve("ret_last", ("wa", 7), l)
                else:
                    dve(phase, "yl", l, i)
                for u, (k0, k) in enumerate(((0, 3), (3, 3), (6, 2))):
                    use(phase, v0 + u, l, i)
                    s = (v0 + u) % SLOTS
                    h = whi[s][:, 0:k * 384].rearrange("p (g k n) -> p k g n", g=3, k=k)
                    w = wlo[s][:, 0:k * 384].rearrange("p (g k n) -> p k g n", g=3, k=k)
                    for t in range(TT):
                        at = slice(t * 128, t * 128 + 128)
                        for kk in range(k):
                            mm = mm3(lo4[t][:, 0:384].rearrange("p (g n) -> p g n", g=3),
                                     hhi[:, k0 + kk, at], hlo[:, k0 + kk, at], h[:, kk], w[:, kk],
                                     k0 + kk == 0, k0 + kk == KT - 1)
                        if u == 2 or t == TT - 1:
                            mm.then_inc(mm_done, 1)

                def scores(c):
                    dve(phase, ("xl", 5) if c == 0 else (("m", c - 1), 2), l, i)
                    at = slice(c * 128, c * 128 + 128)
                    for g in range(AG):
                        m0 = max(0, c - 1) if g == 0 else 0
                        keys = slice(m0 * 128, c * 128 + 128)
                        mm = mm3(hi4[g][:, 0:(c + 1 - m0) * 128], aqh[:, g, at], aql[:, g, at],
                                 akh[:, g, keys], akl[:, g, keys], True, True)
                    mm.then_inc(mm_done, 1)

                def gate(n, ks):
                    unit = v0 + 3 + n
                    if ks[0] == 0:
                        use(phase, unit, l, i)
                        if n:
                            act(phase, ("sg", 0), l, i)
                    mm = features(hi4[3], parts_of(unit, 0, 8, 128), 0, ks=ks)
                    if ks[-1] == KT - 1:
                        mm.then_inc(mm_done, 1)

                def transposes(c):
                    dve(phase, ("pn", c), l, i)
                    if c == 0:
                        dve(phase, ("vl", 3), l, i)
                    else:
                        dve(phase, (("tl", c - 1), AG - 1), l, i)
                    for n, (g, m) in enumerate(blocks_of(c)):
                        mm = pe.transpose(lo4[g][:, (c - m) * 128:(c - m) * 128 + 128],
                                          prob[:, c % 2, n * 128:n * 128 + 128], ident[:, :])
                    mm.then_inc(mm_done, 1)

                scores(0)
                gate(0, range(4))
                scores(1)
                transposes(0)
                gate(0, range(4, 8))
                scores(2)
                transposes(1)
                gate(1, range(4))
                scores(3)
                transposes(2)
                dve(phase, (("tl", 1), AG - 1), l, i)
                products(0)
                gate(1, range(4, 8))
                transposes(3)

            def before_start(steps, phase, l, i, name):
                left = steps.per["att"] - steps.index["att"][name] - 1
                assert steps.per["att_first"] - steps.index["att_first"][name] - 1 == left
                return steps.start(phase, l, i) - left

            def products(pair):
                even, odd = 2 * pair, 2 * pair + 1
                both, one = [], []
                for g in range(AG):
                    for m in sorted({*keys_of(even, g), *keys_of(odd, g)}):
                        if m in keys_of(even, g) and m in keys_of(odd, g):
                            both.append((g, m, even, 2))
                        else:
                            one.append((g, m, even if m in keys_of(even, g) else odd, 1))
                steps = both[:-1] + one + both[-1:]
                for n, (g, m, c, tiles) in enumerate(steps):
                    at = block_at(c, g, m)
                    mm = mm3(lo4[3][:, c * 128:(c + tiles) * 128], avh[:, m, g * 128:(g + 1) * 128],
                             avl[:, m, g * 128:(g + 1) * 128], pt[pair][0][:, at:at + tiles, :],
                             pt[pair][1][:, at:at + tiles, :], n == 0, n == len(steps) - 1)
                mm.then_inc(mm_done, 1)

            def merge(phase, l, i):
                for p in range(2):
                    for u in range(2):
                        use(phase, 3 * p + u, l, i)
                        for n in range(2):
                            f = 4 * p + 2 * u + n
                            if f == 0:
                                dve("att", (("m", 3), 2), l, AI - 2)
                            if f == 3:
                                act("att", ("sg", 1), l, AI - 2)
                            if f >= 4:
                                act(phase, ("sg", f - 4), l)
                            features(hi4[f % 4], parts_of(3 * p + u, 0, 8, 256), n).then_inc(mm_done, 1)
                        if p == 0 and u == 0:
                            pe.wait_ge(dve_done, DV.start(phase, l))
                            products(1)
                    use(phase, 3 * p + 2, l, i)
                    if p == 0:
                        dve(phase, "yl", l)
                    h, w = parts_of(3 * p + 2, 0, 4, 512)
                    for n in range(4):
                        if p:
                            dve(phase, ("yg", n), l)
                        at = slice(n * 128, n * 128 + 128)
                        for k in range(4):
                            mm = mm3(lo4[n][:, :], h[:, k, at], w[:, k, at], yah[:, k, :], yal[:, k, :], k == 0, k == 3)
                        mm.then_inc(mm_done, 1)

            def project(phase, l, i):
                for n in range(2):
                    for half in range(2):
                        c = 2 * n + half
                        use(phase, c, l, i)
                        if c == 0:
                            act("merge", ("sg", 7), l)
                            dve("merge", ("ml", 3), l)
                        if c == 1:
                            dve("merge", ("ml", 7), l)
                        for t in range(TT):
                            mm = token_rows((hi4, lo4)[n][t], parts_of(c, 0, 4, 512), t, mgh, mgl, 4 * half, KT)
                            if half or t == TT - 1:
                                mm.then_inc(mm_done, 1)

            def ffn(phase, l, i):
                bodies_of = 2 if phase in ("ffn", "ffn_end") else 1
                for b in range(bodies_of):
                    if phase != "ffn_last":
                        for z in range(2):
                            c = 3 * b + z
                            use(phase, c, l, i)
                            if b == 1:
                                act(phase, ("si", 1, 0), l, i) if z == 0 else dve(phase, ("al", 1, 0), l, i)
                            elif phase == "ffn_end":
                                last = PAIRS // 2 - 2
                                act("ffn", ("si", 1, 1), l, last) if z == 0 else dve("ffn", ("al", 1, 1), l, last)
                            elif phase == "ffn":
                                if z == 0:
                                    act("ffn_first", ("si", 1, 0), l)
                                    pe.wait_ge(act_done, AC.last("ffn", ("si", 1, 1), l, i))
                                else:
                                    dve("ffn_first", ("al", 1, 0), l)
                                    pe.wait_ge(dve_done, DV.last("ffn", ("al", 1, 1), l, i))
                            for k in range(2):
                                steps = ("pre_ffn", l) if phase == "ffn_first" and z == k == 0 else None
                                features(ffn_banks(phase)[2 * z + k], parts_of(c, 0, 8, 256), k, steps).then_inc(mm_done, 1)
                    if phase == "ffn_first":
                        continue
                    if phase == "ffn_last":
                        down_last(phase, l, i)
                        continue
                    use(phase, 3 * b + 2, l, i)
                    for g in R8:
                        t, cols = g // 2, slice(g % 2 * 512, g % 2 * 512 + 512)
                        if g >= 4:
                            dve(phase, ("d", g - 4, b), l, i)
                        elif b:
                            dve(phase, ("d", g + 4, 0), l, i)
                        else:
                            pe.wait_ge(dve_done, DV.start(phase, l, i) - (3 - g))
                        token_rows(lo4[g % 4], parts_of(3 * b + 2, 0, 2, 1024), t, ffh[:, 2 * b:2 * b + 2, :],
                                   ffl[:, 2 * b:2 * b + 2, :], 0, 2, cols).then_inc(mm_done, 1)

            def down_last(phase, l, i):
                dve("ffn_end", ("al", 1, 1), l)
                for half in range(2):
                    for k in range(2):
                        use(phase, k, l, i)
                        for g in range(4 * half, 4 * half + 4):
                            if half == 0 and k == 0:
                                pe.wait_ge(dve_done, DV.start(phase, l, i) - (3 - g))
                            if half and k == 0:
                                dve("post_ffn", ("d", g - 4), l)
                            mm = token_rows(lo4[g % 4], parts_of(k, 0, 1, 1024), g // 2, ffh[:, :, :], ffl[:, :, :],
                                            k, 2, slice(g % 2 * 512, g % 2 * 512 + 512))
                            if k:
                                mm.then_inc(mm_done, 1)

            def body(phase, l, i):
                if phase in ("pre_mix", "pre_ffn"):
                    pre(phase, l, i)
                elif phase == "ret_first":
                    ret_first(phase, l, i)
                elif phase == "ret":
                    ret(phase, l, i)
                elif phase == "ret_last":
                    ret_last(phase, l, i)
                elif phase in ("att_first", "att"):
                    att(phase, l, i)
                elif phase == "merge":
                    merge(phase, l, i)
                elif phase == "w_o":
                    project(phase, l, i)
                elif phase.startswith("ffn"):
                    ffn(phase, l, i)

            pe.sem_inc(mm_done, 1)
            pe.wait_ge(early_landed, 16 * 2)
            with pe.Fori(0, DEPTH) as l:
                bodies(pe, l, body)

        @block.scalar
        def _(sc):
            def round_unit(phase, c, l, i, size=None):
                s = c % SLOTS
                size = size or UNITS[phase][c][0]
                sc.activation(whi[s][:, 0:size], raw[s][:, 0:size], ACT.Copy).then_inc(hi_ready, 1)

            def ready(phase, c, l, i):
                sc.wait_ge(landed[c % SLOTS], UN.landed(phase, c, l, i))
                if c == 1:
                    sc.wait_ge(mm_done, PE.start(phase, l, i))
                else:
                    sc.wait_ge(mm_done, PE.of(phase, UNIT_END[phase][c - 2], l, i))
                round_unit(phase, c, l, i)

            def ahead(phase, l, i):
                size, dmas = AHEAD[phase]
                c = len(UNITS[phase]) - 2
                sc.wait_ge(landed[0], UN.landed(phase, c, l, i) + 16 * dmas)
                sc.wait_ge(mm_done, PE.of(phase, UNIT_END[phase][c], l, i))
                round_unit(phase, 0, l, i, size)

            def step(ins):
                ins.then_inc(act_done, 1)

            def pe(phase, name, l, i=0):
                sc.wait_ge(mm_done, PE.of(phase, name, l, i))

            def dve(phase, name, l, i=0):
                sc.wait_ge(dve_done, DV.of(phase, name, l, i))

            def own(phase, name, l, i=0):
                sc.wait_ge(act_done, AC.of(phase, name, l, i))

            def square(to, of, sums):
                step(sc.activation(to, of, ACT.Square, scale=float(D) ** -0.5, accum_out=sums))

            def root(phase, name, at, l):
                dve(phase, name, l)
                step(sc.activation(sq[:, at:at + 1], vv[:, at:at + 1], ACT.Sqrt, scale=-2.0))

            def mean_square(t):
                square(junk, acc_t[:, t, :], ss[:, 4 + t:5 + t])

            def mean_root(phase, t, l):
                root(phase, ("v2", t), 4 + t, l)

            def normalised(phase, t, l):
                dve(phase, ("n12", t), l)
                step(sc.activation(rows[:, t, :], acc_t[:, t, :], ACT.Copy, scale=rs[:, 4 + t:5 + t]))

            def start():
                for t in range(3):
                    sc.wait_ge(x_landed[t], 16)
                    if t:
                        own("start", ("s2", t - 1), 0)
                    mean_square(t)
                    if t < 2:
                        mean_root("start", t, 0)
                    if t == 0:
                        normalised("start", t, 0)

            def load_gain(g_post, l):
                src = g_post[bass.ds(l, 1), :].partition_broadcast(P)
                sc.dma_start(gpost[:, :], src).then_inc(gpost_landed, 16)

            def pre(phase, l, i):
                mix = phase == "pre_mix"
                if mix:
                    sc.wait_ge(landed[0], UN.landed("ret_first", 0, l))
                    sc.wait_ge(mm_done, PE.start(phase, l))
                    round_unit("ret_first", 0, l, 0)
                    sc.wait_ge(x_landed[3], 16)
                mean_root(phase, 2, l)
                sc.wait_ge(dve_done, DV.start(phase, l))
                sc.wait_ge(act_done, AC.start(phase, l))
                mean_square(3)
                mean_root(phase, 3, l)
                sc.dma_start(x_rows(xs), acc_t).then_inc(x_saved, 16)
                load_gain(g_post_mix if mix else g_post_ffn, l)
                for k in range(KT):
                    pe(phase, ("x", k), l)
                    at = gall[:, bass.ds(l * 16 + (k if mix else 8 + k), 1)]
                    step(sc.activation(hhi[:, k, :], banks[k][:, :], ACT.Copy, scale=at))
                first, before = ("ret_first", "pre_mix") if mix else ("ffn_first", "post_mix")
                sc.wait_ge(landed[1], UN.landed(first, 1, l))
                sc.wait_ge(mm_done, PE.start(before, l))
                round_unit(first, 1, l, 0)

            def post(phase, l, i):
                mix = phase == "post_mix"

                def branch_square(t, before):
                    sc.wait_ge(act_done, AC.start(phase, l)) if before is None else own(phase, before, l)
                    if mix:
                        pe("w_o", ("o", 1, t), l)
                        square(junk[:, 0:512], lo4[t][:, :], ss[:, t:t + 1])
                    else:
                        dve(phase, ("d", 2 * t + 1), l)
                        square(junk, acc_t[:, t, :], ss[:, t:t + 1])

                def x_square(t, before):
                    dve(phase, ("xa", t), l)
                    own(phase, before, l)
                    mean_square(t)

                branch_square(0, None)
                root(phase, ("v", 0), 0, l)
                branch_square(1, ("sq", 0))
                root(phase, ("v", 1), 1, l)
                x_square(0, ("sq", 1))
                branch_square(2, ("s2", 0))
                mean_root(phase, 0, l)
                root(phase, ("v", 2), 2, l)
                x_square(1, ("sq", 2))
                branch_square(3, ("s2", 1))
                mean_root(phase, 1, l)
                normalised(phase, 0, l)
                root(phase, ("v", 3), 3, l)
                x_square(2, ("sq", 3))

            def root_ret(phase, l, i):
                dve(phase, "v", l, i)
                step(sc.activation(sq[:, 0:4], vv[:, 0:4], ACT.Sqrt, scale=-2.0))

            def gated_hi(phase, l, i):
                for e in range(4):
                    dve(phase, ("zm", e), l, i)
                    step(sc.activation(rvh[:, e, :], scr[:, e, :], ACT.Copy))

            def rotated_hi(phase, x, dst, l, i):
                for n in range(2):
                    dve(phase, (x, 2 + 3 * n), l, i)
                    step(sc.activation(dst[:, n, :], scr[:, 2 * n, :], ACT.Copy))

            def values_hi(phase, l, i):
                for t in range(TT):
                    pe(phase, ("v", t), l, i)
                    step(sc.activation(rvh[:, t, :], hi4[t][:, :], ACT.Copy))

            def scores_hi(phase, l, i):
                at = 0
                for j in range(TT):
                    n = SEQ - j * 128
                    dve(phase, ("pm", j), l, i)
                    step(sc.activation(rph[:, at:at + n], scr[:, j, 0:n], ACT.Copy))
                    at += n
                src = decays[1] if phase == "ret_first" else decays[bass.ds(i + 2, 1)].rearrange("o p n -> p (o n)")
                sc.dma_start(decay[:, :], src).then_inc(decay_landed, 16)

            def silu(phase, e, l, i, bank=None):
                pe(phase, ("g", e), l, i)
                step(sc.activation(sgr[:, e, :], (bank or hi4[e])[:, :], ACT.Silu))

            def ret_first(phase, l, i):
                ready(phase, 2, l, i)
                rotated_hi(phase, "q", rqh, l, i)
                ready(phase, 3, l, i)
                rotated_hi(phase, "k", rkh, l, i)
                for e in range(2):
                    silu(phase, e, l, i, lo4[2 + e])
                ready(phase, 4, l, i)
                ready(phase, 5, l, i)
                values_hi(phase, l, i)
                ahead(phase, l, i)
                scores_hi(phase, l, i)
                for e in range(2, 4):
                    silu(phase, e, l, i)

            def ret(phase, l, i):
                ready(phase, 1, l, i)
                root_ret(phase, l, i)
                ready(phase, 2, l, i)
                gated_hi(phase, l, i)
                ready(phase, 3, l, i)
                rotated_hi(phase, "q", rqh, l, i)
                rotated_hi(phase, "k", rkh, l, i)
                for c in (4, 5, 6):
                    ready(phase, c, l, i)
                values_hi(phase, l, i)
                ready(phase, 7, l, i)
                scores_hi(phase, l, i)
                ahead(phase, l, i)
                dve(phase, ("zl", 3), l, i)
                for e in range(4):
                    silu(phase, e, l, i)

            def qk_hi(phase, n, l, i, back):
                pe(phase, ("x", n), l, i)
                back()
                step(sc.activation(scr[0:32, 2 + n % 2, :], xbank[n][0:32, :], ACT.Copy))
                dve(phase, ("xa", n), l, i)
                dst = (aqh if n < 3 else akh)[:, n % 3, :]
                step(sc.activation(dst, scr[:, n % 2, :], ACT.Copy))

            def ret_last(phase, l, i):
                ready(phase, 1, l, i)
                root_ret(phase, l, i)
                ready(phase, 2, l, i)
                gated_hi(phase, l, i)
                for n in range(4):
                    if n == 1:
                        ready(phase, 3, l, i)
                    qk_hi(phase, n, l, i, lambda: dve(phase, ("zl", 3) if n < 2 else ("xs", n - 2), l))
                    if n == 2:
                        ahead(phase, l, i)

            def att(phase, l, i):
                first = phase == "att_first"
                at_tile, rest = ({5: 2}, (3, 4)) if first else ({1: 2, 3: 3, 5: 4}, (5, 6))
                ready(phase, 1, l, i)
                for n in range(4 if first else 0, 6):
                    if n in at_tile:
                        ready(phase, at_tile[n], l, i)
                    if n < 2:
                        back = lambda: sc.wait_ge(dve_done, DV.start(phase, l, i))
                    elif first:
                        back = lambda: dve("ret_last", ("xs", n - 2), l)
                    else:
                        back = lambda: dve(phase, ("xs", n - 2), l, i)
                    qk_hi(phase, n, l, i, back)
                    if n == 1:
                        output_hi(phase, bass.ds(i, 1), l, i)
                for c in rest:
                    ready(phase, c, l, i)
                for t in range(TT):
                    pe(phase, ("v", t), l, i)
                    step(sc.activation(avh[:, t, :], lo4[t][:, 0:384], ACT.Copy))
                ready(phase, len(UNITS[phase]) - 1, l, i)

                def exps(c):
                    w = len(blocks_of(c)) * 128
                    dve(phase, ("mx", c), l, i)
                    step(sc.activation(prob[:, c % 2, 0:w], prob[:, c % 2, 0:w], ACT.Exp,
                                       bias=nmax[:, c % 2:c % 2 + 1], accum_out=den[:, c % 2:c % 2 + 1]))

                def key_major(c):
                    pe(phase, ("t", c), l, i)
                    for g in range(AG):
                        n, at = len(keys_of(c, g)), block_at(c, g, c)
                        step(sc.activation(pt[c // 2][0][:, at:at + 2 * n - 1:2, :],
                                           lo4[g][:, 0:n * 128].rearrange("p (b n) -> p b n", b=n), ACT.Copy))

                def gate(n):
                    pe(phase, ("g", n), l, i)
                    if n:
                        dve(phase, ("gm", 0), l, i)
                    else:
                        sc.wait_ge(dve_done, DV.start(phase, l, i))
                    step(sc.activation(sga[:, 0, :], hi4[3][:, :], ACT.Sigmoid))

                exps(0)
                key_major(0)
                exps(1)
                gate(0)
                key_major(1)
                exps(2)
                ahead(phase, l, i)
                key_major(2)
                exps(3)
                gate(1)
                key_major(3)

            def output_hi(phase, at, l, i):
                pe(phase, "pp", l, i)
                step(sc.activation(yah[:, at, :].rearrange("p o n -> p (o n)"), lo4[3][:, :], ACT.Copy))

            def merge(phase, l, i):
                def sigmoid(f):
                    pe(phase, ("a", f), l)
                    if f < 4:
                        dve("att", ("xl", 5), l, AI - 2)
                    else:
                        dve(phase, ("ym", f - 4), l)
                    step(sc.activation(scr[:, f % 4, :], hi4[f % 4][:, :], ACT.Sigmoid))

                def merged_hi(f):
                    dve(phase, ("ym", f), l)
                    step(sc.activation(mgh[:, f, :], acc_f[:, f, :], ACT.Copy))

                ready(phase, 1, l, i)
                sc.wait_ge(act_done, AC.start(phase, l))
                sigmoid(0)
                ready(phase, 2, l, i)
                sigmoid(1)
                output_hi(phase, slice(AI - 1, AI), l, i)
                ready(phase, 3, l, i)
                sigmoid(2)
                sigmoid(3)
                for f in range(3):
                    merged_hi(f)
                ready(phase, 4, l, i)
                merged_hi(3)
                sigmoid(4)
                ready(phase, 5, l, i)
                for f in range(5, 8):
                    sigmoid(f)
                ahead(phase, l, i)
                for f in range(4, 8):
                    merged_hi(f)

            def project(phase, l, i):
                sc.wait_ge(x_saved, 16 + l * 32)
                sc.dma_start(rows, x_rows(xs)).then_inc(rows_landed, 16)
                ready(phase, 1, l, i)
                ready(phase, 2, l, i)
                dve("merge", ("ml", 7), l)
                for t in range(TT):
                    pe(phase, ("o", 0, t), l, i)
                    if t:
                        own(phase, ("sq", t - 1), l)
                    square(junk[:, 0:512], hi4[t][:, :], ss0[:, t:t + 1])
                ready(phase, 3, l, i)
                ahead(phase, l, i)

            def ffn(phase, l, i):
                if phase == "ffn_last":
                    sc.wait_ge(x_saved, 32 + l * 32)
                    pe("pre_ffn", ("x", 7), l)
                    sc.dma_start(rows, x_rows(xs)).then_inc(rows_landed, 16)
                    ready(phase, 1, l, i)
                    return
                for b in range(1 if phase == "ffn_first" else 2):
                    if phase != "ffn_first":
                        ready(phase, 3 * b + 1, l, i)
                        ready(phase, 3 * b + 2, l, i)
                    for k in range(2):
                        pe(phase, ("g", k, b), l, i)
                        if b:
                            dve(phase, ("am", k, 0), l, i)
                        else:
                            sc.wait_ge(dve_done, DV.start(phase, l, i))
                        step(sc.activation(scr[:, k, :], ffn_banks(phase)[k][:, :], ACT.Silu))
                    par = pair_slot(phase, b)
                    if phase == "ffn_first":
                        ahead(phase, l, i)
                    for k in range(2):
                        if k and phase != "ffn_first":
                            ready(phase, 3, l, i) if b == 0 else ahead(phase, l, i)
                        dve(phase, ("am", k, b), l, i)
                        step(sc.activation(ffh[:, 2 * par + k, :], scr[:, 2 + k, :], ACT.Copy))

            def body(phase, l, i):
                if phase in ("pre_mix", "pre_ffn"):
                    pre(phase, l, i)
                elif phase in ("post_mix", "post_ffn"):
                    post(phase, l, i)
                elif phase == "ret_first":
                    ret_first(phase, l, i)
                elif phase == "ret":
                    ret(phase, l, i)
                elif phase == "ret_last":
                    ret_last(phase, l, i)
                elif phase in ("att_first", "att"):
                    att(phase, l, i)
                elif phase == "merge":
                    merge(phase, l, i)
                elif phase == "w_o":
                    project(phase, l, i)
                else:
                    ffn(phase, l, i)

            sc.sem_inc(act_done, 1)
            sc.wait_ge(early_landed, 16 * 2)
            start()
            with sc.Fori(0, DEPTH) as l:
                bodies(sc, l, body)

        @block.vector
        def _(ve):
            def step(ins):
                ins.then_inc(dve_done, 1)

            def pe(phase, name, l, i=0):
                ve.wait_ge(mm_done, PE.of(phase, name, l, i))

            def act(phase, name, l, i=0):
                ve.wait_ge(act_done, AC.of(phase, name, l, i))

            def own(phase, name, l, i=0):
                ve.wait_ge(dve_done, DV.of(phase, name, l, i))

            def reciprocal_root(phase, root, name, at, l, i=0):
                v, r, a = vv[:, at], rs[:, at], aa[:, at]
                act(phase, root, l, i)
                step(ve.reciprocal(r, sq[:, at]))
                own(phase, name("rc"), l, i)
                if at.stop - at.start == 1:
                    step(ve.scalar_tensor_tensor(out=a, in0=r, scalar=r, in1=v, op0=ALU.mult, op1=ALU.mult))
                else:
                    step(ve.tensor_tensor(a, r, r, ALU.mult))
                    own(phase, "sr", l, i)
                    step(ve.tensor_tensor(a, a, v, ALU.mult))
                own(phase, name("n0"), l, i)
                step(ve.scalar_tensor_tensor(out=r, in0=a, scalar=1.5, in1=r, op0=ALU.add, op1=ALU.mult))

            def norm_sum(phase, t, l):
                act(phase, ("s2", t), l)
                half_mean(t)

            def half_mean(t):
                step(ve.tensor_scalar(vv[:, 4 + t:5 + t], ss[:, 4 + t:5 + t], -0.5, -0.5 * EPS, ALU.mult, ALU.add))

            def norm_root(phase, t, l):
                reciprocal_root(phase, ("r2", t), lambda z: (z + "2", t), slice(4 + t, 5 + t), l)

            def start():
                for t in range(2):
                    norm_sum("start", t, 0)
                    norm_root("start", t, 0)

            def normalised(phase, t):
                step(ve.tensor_scalar(rows[:, t, :], acc_t[:, t, :], rs[:, 4 + t:5 + t], None, ALU.mult))

            def pre(phase, l, i):
                ve.wait_ge(act_done, AC.start(phase, l))
                ve.wait_ge(dve_done, DV.start(phase, l))
                half_mean(2)
                normalised(phase, 1)
                norm_root(phase, 2, l)
                norm_sum(phase, 3, l)
                own(phase, ("n12", 2), l)
                normalised(phase, 2)
                norm_root(phase, 3, l)
                own(phase, ("n12", 3), l)
                normalised(phase, 3)
                for k in range(KT):
                    act(phase, ("hh", k), l)
                    at = gall[:, bass.ds(l * 16 + (k if phase == "pre_mix" else 8 + k), 1)]
                    step(ve.scalar_tensor_tensor(out=hlo[:, k, :], in0=banks[k][:, :], scalar=at,
                                                 in1=hhi[:, k, :].bitcast(F32), op0=ALU.mult, op1=ALU.subtract))

            def clear(phase, l):
                ve.wait_ge(x_saved, (16 if phase == "ret_first" else 32) + l * 32)
                step(ve.memset(acc[:, :], 0.0))

            def project(phase, l, i):
                ve.wait_ge(gpost_landed, 16 + l * 32)
                ve.wait_ge(dve_done, DV.start(phase, l))
                for t in range(TT):
                    act(phase, ("sq", t), l)
                    step(ve.tensor_tensor(acc_t[:, t, 0:512], hi4[t][:, :], gpost[:, 0:512], ALU.mult))
                step(ve.tensor_scalar(ss0[:, :], ss0[:, :], EPS, None, ALU.add))

            def post(phase, l, i):
                mix = phase == "post_mix"
                ve.wait_ge(rows_landed, (16 if mix else 32) + l * 32)
                ve.wait_ge(dve_done, DV.start(phase, l))

                def add_down(t):
                    for g in (2 * t, 2 * t + 1):
                        pe("ffn_last", ("d", g, 0), l)
                        sums = acc_t[:, g // 2, g % 2 * 512:g % 2 * 512 + 512]
                        step(ve.tensor_tensor(sums, sums, lo4[g % 4][:, :], ALU.add))

                if not mix:
                    add_down(0)
                    add_down(1)
                for t in range(TT):
                    act(phase, ("sq", t), l)
                    at = slice(t, t + 1)
                    if mix:
                        step(ve.tensor_scalar(vv[:, at], ss[:, at], ss0[:, at], -0.5, ALU.add, ALU.mult))
                        step(ve.tensor_tensor(acc_t[:, t, 512:1024], lo4[t][:, :], gpost[:, 512:1024], ALU.mult))
                    else:
                        step(ve.tensor_scalar(vv[:, at], ss[:, at], -0.5, -0.5 * EPS, ALU.mult, ALU.add))
                    reciprocal_root(phase, ("rt", t), lambda z: (z, t), at, l)
                    if t < TT - 2 and not mix:
                        add_down(t + 2)
                    if 0 < t < TT - 1:
                        norm_sum(phase, t - 1, l)
                    own(phase, ("n1", t), l)
                    if not mix:
                        ve.wait_ge(pool_done, l * TT + (t + 1))
                    step(ve.scalar_tensor_tensor(out=acc_t[:, t, :], in0=acc_t[:, t, :] if mix else zf[:, t % 2, :],
                                                 scalar=rs[:, at], in1=rows[:, t, :], op0=ALU.mult, op1=ALU.add))
                    if 0 < t < TT - 1:
                        norm_root(phase, t - 1, l)

            def normalise(phase, l, i):
                ve.wait_ge(dve_done, DV.start(phase, l, i))
                step(ve.tensor_scalar(vv[:, 0:4], bag[:, :, 1], -0.5, -0.5 * EPS, ALU.mult, ALU.add))
                reciprocal_root(phase, "rt", lambda z: z, slice(0, 4), l, i)
                own(phase, "n1", l, i)
                for t in range(TT):
                    step(ve.tensor_scalar(yn[:, t, :], lo4[t][:, :], bag[:, t, 0:1], rs[:, t:t + 1],
                                          ALU.subtract, ALU.mult))

            def gated(phase, l, i):
                ve.wait_ge(act_done, AC.start(phase, l, i))
                for e in range(4):
                    pe(phase, ("t", e), l, i)
                    step(ve.tensor_tensor(scr[:, e, :], lo4[e][:, :], sgr[:, e, :], ALU.mult))
                    act(phase, ("zh", e), l, i)
                    own(phase, ("zm", e), l, i)
                    step(ve.tensor_tensor(rvl[:, e, :], scr[:, e, :], rvh[:, e, :].bitcast(F32), ALU.subtract))

            def rotate(phase, x, before, ba, bb, dh, dl, l, i):
                cos, sin = trig[:, 0, :], trig[:, 1, :]
                if before:
                    own(phase, before, l, i)
                else:
                    ve.wait_ge(dve_done, DV.start(phase, l, i))
                pe(phase, (x, 1), l, i)
                step(ve.tensor_tensor(scr[:, 0, :], ba[:, :], cos, ALU.mult))
                step(ve.tensor_tensor(scr[:, 1, :], bb[:, :], sin, ALU.mult))
                own(phase, (x, 1), l, i)
                step(ve.tensor_tensor(scr[:, 0, :], scr[:, 0, :], scr[:, 1, :], ALU.subtract))
                step(ve.tensor_tensor(scr[:, 2, :], ba[:, :], sin, ALU.mult))
                step(ve.tensor_tensor(scr[:, 3, :], bb[:, :], cos, ALU.mult))
                own(phase, (x, 4), l, i)
                step(ve.tensor_tensor(scr[:, 2, :], scr[:, 2, :], scr[:, 3, :], ALU.add))
                for n in range(2):
                    act(phase, (x + "h", n), l, i)
                    own(phase, (x, 2 + 3 * n), l, i)
                    step(ve.tensor_tensor(dl[:, n, :], scr[:, 2 * n, :], dh[:, n, :].bitcast(F32), ALU.subtract))

            def add_ret_out(phase, fs, l, i):
                for f in fs:
                    pe(phase, ("w", f), l, i)
                    step(ve.tensor_tensor(acc_f[:, f, :], acc_f[:, f, :], lo4[f % 4][:, :], ALU.add))

            def ret(phase, l, i):
                if phase == "ret":
                    normalise(phase, l, i)
                    gated(phase, l, i)
                else:
                    ve.wait_ge(const_landed, 16 * 4)
                side = hi4 if phase == "ret" else lo4
                rotate(phase, "q", ("zl", 3) if phase == "ret" else None, side[0], side[1], rqh, rql, l, i)
                rotate(phase, "k", ("ql", 1), hi4[2], hi4[3], rkh, rkl, l, i)
                if phase == "ret":
                    add_ret_out(phase, R8, l, i)
                else:
                    clear(phase, l)
                for t in range(TT):
                    act(phase, ("vh", t), l, i)
                    step(ve.tensor_tensor(rvl[:, t, :], hi4[t][:, :], rvh[:, t, :].bitcast(F32), ALU.subtract))
                h = 0 if phase == "ret_first" else i + 1
                ve.wait_ge(decay_landed, l * (16 * RH) + (h * 16 + 16))
                own(phase, ("kl", 1), l, i)
                at = 0
                for j in range(TT):
                    n = SEQ - j * 128
                    pe(phase, ("s", j), l, i)
                    step(ve.tensor_tensor(scr[:, j, 0:n], lo4[j][:, 0:n], decay[:, 0:n], ALU.mult))
                    act(phase, ("ph", j), l, i)
                    own(phase, ("pm", j), l, i)
                    step(ve.tensor_tensor(rpl[:, at:at + n], scr[:, j, 0:n], rph[:, at:at + n].bitcast(F32), ALU.subtract))
                    at += n
                for t in range(TT):
                    pe(phase, ("y", t), l, i)
                    step(ve.bn_stats(bst[:, t, :], lo4[t][:, :]))
                    own(phase, ("st", t), l, i)
                    ve.sem_inc(ve_waited, 1)
                    step(ve.bn_aggr(bag[:, t, :], bst[:, t, :]))

            def qk_tile(phase, n, free, l, i):
                s = n % 2
                act(phase, ("xc", n), l, i)
                free()
                step(ve.tensor_tensor(scr[:, s, :], xbank[n][:, :], acos[:, :], ALU.mult))
                step(ve.stream_shuffle(shuf[0:32, s, :], scr[0:32, 2 + s, :], [(m + 16) % 32 for m in range(32)]))
                own(phase, ("xs", n), l, i)
                step(ve.tensor_tensor(shuf[0:32, s, :], shuf[0:32, s, :], asin[:, :], ALU.mult))
                own(phase, ("xp", n), l, i)
                step(ve.tensor_tensor(scr[0:32, s, :], scr[0:32, s, :], shuf[0:32, s, :], ALU.add))
                act(phase, ("xh", n), l, i)
                own(phase, ("xa", n), l, i)
                dh, dl = (aqh, aql) if n < 3 else (akh, akl)
                step(ve.tensor_tensor(dl[:, n % 3, :], scr[:, s, :], dh[:, n % 3, :].bitcast(F32), ALU.subtract))

            def ret_last(phase, l, i):
                normalise(phase, l, i)
                gated(phase, l, i)
                for n in range(4):
                    add_ret_out(phase, ADD_BEFORE.get(n, []), l, i)
                    qk_tile(phase, n, lambda: own(phase, ("zl", 3) if n < 2 else ("xl", n - 2), l), l, i)
                add_ret_out(phase, range(4, 8), l, i)

            def att(phase, l, i):
                first = phase == "att_first"
                head = 0 if first else i + 1
                for n in range(4 if first else 0, 6):
                    if n < 2 or first:
                        free = lambda: ve.wait_ge(dve_done, DV.start(phase, l, i))
                    else:
                        free = lambda: own(phase, ("xl", n - 2), l, i)
                    qk_tile(phase, n, free, l, i)
                    if n == 1:
                        output_lo(phase, bass.ds(i, 1), l, i)
                for t in range(TT):
                    act(phase, ("vh", t), l, i)
                    step(ve.tensor_tensor(avl[:, t, :], lo4[t][:, 0:384], avh[:, t, :].bitcast(F32), ALU.subtract))

                def soft(c):
                    q = c % 2
                    pe(phase, ("s", c), l, i)
                    if c >= 2:
                        pe(phase, ("t", c - 2), l, i)
                    ve.sem_inc(ve_waited, 1)
                    at = 0
                    for g in range(AG):
                        w = len(keys_of(c, g)) * 128
                        off = 256 - w if g == 0 else 256 + 512 * g - w
                        step(ve.tensor_tensor_reduce(prob[:, q, at:at + w], hi4[g][:, 0:w], masks[:, off:off + w],
                                                     ATT_SCALE, -3.0e38, ALU.add, ALU.max, rmax[:, q, g:g + 1]))
                        at += w
                    own(phase, (("m", c), 2), l, i)
                    step(ve.tensor_reduce(nmax[:, q:q + 1], rmax[:, q, :], AX_X, ALU.max, negate=True))

                def divide(c):
                    q, w = c % 2, len(blocks_of(c)) * 128
                    act(phase, ("ex", c), l, i)
                    step(ve.reciprocal(rden[:, q:q + 1], den[:, q:q + 1]))
                    own(phase, ("rc", c), l, i)
                    step(ve.tensor_scalar(prob[:, q, 0:w], prob[:, q, 0:w], rden[:, q:q + 1], None, ALU.mult))

                def key_major(c):
                    for g in range(AG):
                        n, at = len(keys_of(c, g)), block_at(c, g, c)
                        blocks = slice(at, at + 2 * n - 1, 2)
                        act(phase, (("th", c), g), l, i)
                        step(ve.tensor_tensor(pt[c // 2][1][:, blocks, :], lo4[g][:, 0:n * 128].rearrange("p (b n) -> p b n", b=n),
                                              pt[c // 2][0][:, blocks, :].bitcast(F32), ALU.subtract))

                def gated_tile(n):
                    act(phase, ("sg", n), l, i)
                    tile = acc_f[:, bass.ds(head * 2 + n, 1), :].rearrange("p o n -> p (o n)")
                    step(ve.tensor_tensor(tile, tile, sga[:, 0, :], ALU.mult))

                for c in range(TT):
                    soft(c)
                    if c:
                        key_major(c - 1)
                    if c == 2:
                        if first:
                            own("ret_last", ("wa", 7), l)
                        gated_tile(0)
                    divide(c)
                gated_tile(1)
                key_major(3)

            def output_lo(phase, at, l, i):
                act(phase, "yh", l, i)
                step(ve.tensor_tensor(yal[:, at, :].rearrange("p o n -> p (o n)"), lo4[3][:, :],
                                      yah[:, at, :].rearrange("p o n -> p (o n)").bitcast(F32), ALU.subtract))

            def merge(phase, l, i):
                output_lo(phase, slice(AI - 1, AI), l, i)
                for f in range(8):
                    act(phase, ("sg", f), l)
                    pe(phase, ("w", f), l)
                    step(ve.tensor_tensor(scr[:, f % 4, :], scr[:, f % 4, :], lo4[f % 4][:, :], ALU.mult))
                    own(phase, ("yg", f), l)
                    step(ve.tensor_tensor(acc_f[:, f, :], acc_f[:, f, :], scr[:, f % 4, :], ALU.add))
                    act(phase, ("mh", f), l)
                    own(phase, ("ym", f), l)
                    step(ve.tensor_tensor(mgl[:, f, :], acc_f[:, f, :], mgh[:, f, :].bitcast(F32), ALU.subtract))

            def ffn(phase, l, i):
                for b in range(2 if phase in ("ffn", "ffn_end") else 1):
                    if phase != "ffn_last":
                        par = pair_slot(phase, b)
                        for k in range(2):
                            act(phase, ("si", k, b), l, i)
                            pe(phase, ("u", k, b), l, i)
                            step(ve.tensor_tensor(scr[:, 2 + k, :], scr[:, k, :], hi4[2 + k][:, :], ALU.mult))
                            act(phase, ("ah", k, b), l, i)
                            own(phase, ("am", k, b), l, i)
                            step(ve.tensor_tensor(ffl[:, 2 * par + k, :], scr[:, 2 + k, :],
                                                  ffh[:, 2 * par + k, :].bitcast(F32), ALU.subtract))
                    if phase in ("ffn", "ffn_end"):
                        for g in R8:
                            pe(phase, ("d", g, b), l, i)
                            sums = acc_t[:, g // 2, g % 2 * 512:g % 2 * 512 + 512]
                            step(ve.tensor_tensor(sums, sums, lo4[g % 4][:, :], ALU.add))
                    elif phase == "ffn_first":
                        clear(phase, l)

            def body(phase, l, i):
                if phase in ("pre_mix", "pre_ffn"):
                    pre(phase, l, i)
                elif phase in ("post_mix", "post_ffn"):
                    post(phase, l, i)
                elif phase in ("ret_first", "ret"):
                    ret(phase, l, i)
                elif phase == "ret_last":
                    ret_last(phase, l, i)
                elif phase in ("att_first", "att"):
                    att(phase, l, i)
                elif phase == "merge":
                    merge(phase, l, i)
                elif phase == "w_o":
                    project(phase, l, i)
                elif phase.startswith("ffn"):
                    ffn(phase, l, i)

            ve.sem_inc(dve_done, 1)
            ve.wait_ge(early_landed, 16 * 2)
            start()
            with ve.Fori(0, DEPTH) as l:
                bodies(ve, l, body)


def pair_slot(phase, b):
    return 0 if phase == "ffn_first" else 1 - b


def tables():
    f32 = np.float32
    pos = np.arange(SEQ, dtype=f32)
    half = 128
    inv = (f32(10000.0) ** (-np.arange(half, dtype=f32) / f32(half))).astype(f32)
    ang = (pos[None, :] * inv[:, None]).astype(f32)
    trig = np.stack([np.cos(ang), np.sin(ang)], axis=1).astype(f32)
    half = 16
    inv = (f32(500000.0) ** (-np.arange(half, dtype=f32) / f32(half))).astype(f32)
    ang = (pos[None, :] * inv[:, None]).astype(f32)
    acos = np.ones((P, SEQ), f32)
    acos[0:16] = acos[16:32] = np.cos(ang)
    asin = np.concatenate([-np.sin(ang), np.sin(ang)]).astype(f32)
    q, k = np.arange(P)[:, None], np.arange(P)[None, :]
    parts = [k >= q, k <= q]
    for r in (4, 16):
        same = (q - k) % r == 0
        parts += [same, same, same, same & (k <= q)]
    masks = np.where(np.concatenate(parts, axis=1), 0.0, NEG).astype(f32)
    n, p = np.arange(SEQ)[None, :], np.arange(P)[:, None]
    decays = []
    for h in range(RH):
        lg = np.log(1.0 - 2.0 ** (-5.0 - h))
        decays.append(np.where(n >= p, np.exp(np.maximum(n - p, 0) * lg), 0.0) / 16.0)
    decays.append(decays[0])
    return {"ident": np.eye(P, dtype=f32), "ret_trig": trig, "att_cos": acos, "att_sin": asin,
            "att_masks": masks, "decays": np.stack(decays).astype(f32)}


def kernel(x, w_in, w_ret_out, w_att_out, w_o, w_ffn_gate, w_ffn_up, w_ffn_down,
           g_pre_mix, g_post_mix, g_pre_ffn, g_post_ffn):
    import concourse.bacc as bacc
    from concourse.bass_utils import run_bass_kernel_spmd

    nc = bacc.Bacc("TRN2", target_bir_lowering=False, num_devices=1)
    gains = np.stack([np.asarray(g_pre_mix), np.asarray(g_pre_ffn)], axis=1).reshape(DEPTH, 2, KT, P)
    gains = np.ascontiguousarray(gains.transpose(3, 0, 1, 2).reshape(P, DEPTH * 2 * KT))
    arrays = {"x": np.asarray(x).reshape(SEQ, D), "w_in": w_in, "w_ret": w_ret_out, "w_att": w_att_out, "w_o": w_o,
              "w_gate": w_ffn_gate, "w_up": w_ffn_up, "w_down": w_ffn_down, "gains": gains,
              "g_post_mix": g_post_mix, "g_post_ffn": g_post_ffn}
    t = tables()
    arrays |= {"ident_in": t["ident"], "ret_trig": t["ret_trig"], "att_cos": t["att_cos"], "att_sin": t["att_sin"],
               "att_masks": t["att_masks"], "decays": t["decays"]}
    arrays = {k: np.ascontiguousarray(v) for k, v in arrays.items()}
    args = [nc.dram_tensor(k, v.shape, F32, kind="ExternalInput").ap() for k, v in arrays.items()]
    out = nc.dram_tensor("out", (SEQ, D), F32, kind="ExternalOutput").ap()
    build(nc, *args, out)
    r = run_bass_kernel_spmd(nc, [arrays], core_ids=[0])
    return r.results[0]["out"].reshape(1, SEQ, D)
```
